# Optimizing a Trainium2 kernel written in Bass

```python
import math
import jax, jax.numpy as jnp
from jax import lax
import numpy as np

D_MODEL = 1024
BATCH = 1
SEQ = 2048
DEPTH = 2

N_MIXERS = 2
N_A_LAYERS = (DEPTH + 1) // 2
N_B_LAYERS = DEPTH // 2
BLOCK_Q = 128
RMS_EPS = 1e-6

N_BUCKETS = 32
MAX_DISTANCE = 128
N_BIAS_COLS = 16

A_HEADS = 16
A_HEAD_DIM = D_MODEL // A_HEADS
A_WIDTH = A_HEADS * A_HEAD_DIM
A_Q_RANK = D_MODEL // 4
A_KV_RANK = D_MODEL // 8
IDX_HEADS = 8
IDX_DIM = 64
TOPK_MAX = 256
A_IN = A_Q_RANK + A_KV_RANK + IDX_DIM + IDX_HEADS + A_WIDTH

B_HEADS = 8
B_HEAD_DIM = D_MODEL // (2 * B_HEADS)
B_WIDTH = B_HEADS * 2 * B_HEAD_DIM
B_IN = 4 * B_WIDTH

kernel_name = "hybrid_dsa_diffattn_adaln_block"

def rms_norm(x, g):
    xf = x.astype(jnp.float32)
    y = xf * lax.rsqrt(jnp.mean(xf * xf, axis=-1, keepdims=True) + RMS_EPS)
    return (y * g.astype(jnp.float32)).astype(x.dtype)

def t5_bucket(rel):
    n = jnp.maximum(rel, 0)
    max_exact = N_BUCKETS // 2
    nf = jnp.maximum(n, 1).astype(jnp.float32)
    large = max_exact + (jnp.log(nf / max_exact) / math.log(MAX_DISTANCE / max_exact)
                         * (N_BUCKETS - max_exact)).astype(jnp.int32)
    large = jnp.minimum(large, N_BUCKETS - 1)
    return jnp.where(n < max_exact, n, large)

def to_blocks(a, nb):
    return jnp.moveaxis(a.reshape(a.shape[0], nb, BLOCK_Q, *a.shape[2:]), 1, 0)

def from_blocks(a):
    a = jnp.moveaxis(a, 0, 1)
    return a.reshape(a.shape[0], a.shape[1] * a.shape[2], *a.shape[3:])

def dsa_mixer(h, rel_bias, w_in, q_norm_g, kv_norm_g, kidx_norm_g, w_uq, w_qidx, w_uk, w_uv, w_out):
    bsz, L, _ = h.shape
    proj = h @ w_in
    o1 = A_Q_RANK
    o2 = o1 + A_KV_RANK
    o3 = o2 + IDX_DIM
    o4 = o3 + IDX_HEADS
    c_q = rms_norm(proj[..., :o1], q_norm_g)
    c_kv = rms_norm(proj[..., o1:o2], kv_norm_g)
    k_idx = rms_norm(proj[..., o2:o3], kidx_norm_g)
    w_idx = proj[..., o3:o4] * (IDX_HEADS ** -0.5 * IDX_DIM ** -0.5)
    gate = proj[..., o4:]

    q = (c_q @ w_uq).reshape(bsz, L, A_HEADS, A_HEAD_DIM)
    q_abs = jnp.einsum('blhd,hrd->blhr', q, w_uk) * (A_HEAD_DIM ** -0.5)
    q_idx = (c_q @ w_qidx).reshape(bsz, L, IDX_HEADS, IDX_DIM)

    k_top = min(TOPK_MAX, L // 4)
    nb = L // BLOCK_Q
    key_pos = jnp.arange(L)

    def block(args):
        qa, qi, wi, start = args
        t = start + jnp.arange(BLOCK_Q)
        causal = key_pos[None, :] <= t[:, None]
        s_idx = jnp.einsum('bqhd,bld->bqhl', qi, k_idx)
        score = jnp.einsum('bqh,bqhl->bql', wi.astype(jnp.float32),
                           jax.nn.relu(s_idx).astype(jnp.float32))
        score = jnp.where(causal[None], score, -jnp.inf)
        _, sel = lax.top_k(score, k_top)
        valid = sel <= t[None, :, None]
        kv_sel = jax.vmap(lambda ck, ix: ck[ix])(c_kv, sel)
        logits = jnp.einsum('bqhr,bqkr->bhqk', qa, kv_sel).astype(jnp.float32)
        bias = rel_bias[t5_bucket(t[None, :, None] - sel)].astype(jnp.float32)
        logits = logits + jnp.moveaxis(bias, -1, 1)
        logits = jnp.where(valid[:, None], logits, -jnp.inf)
        p = jax.nn.softmax(logits, axis=-1).astype(kv_sel.dtype)
        return jnp.einsum('bhqk,bqkr->bqhr', p, kv_sel)

    starts = jnp.arange(nb, dtype=jnp.int32) * BLOCK_Q
    o_lat = from_blocks(lax.map(block, (to_blocks(q_abs, nb), to_blocks(q_idx, nb),
                                        to_blocks(w_idx, nb), starts)))
    o = jnp.einsum('blhr,hrd->blhd', o_lat, w_uv).reshape(bsz, L, A_WIDTH)
    return (o * jax.nn.silu(gate)) @ w_out

def diff_mixer(h, rel_bias, w_in, lam_q1, lam_k1, lam_q2, lam_k2, subln_g, w_out, lambda_init):
    bsz, L, _ = h.shape
    proj = h @ w_in
    q = proj[..., :B_WIDTH].reshape(bsz, L, 2 * B_HEADS, B_HEAD_DIM) * (B_HEAD_DIM ** -0.5)
    k = proj[..., B_WIDTH:2 * B_WIDTH].reshape(bsz, L, 2 * B_HEADS, B_HEAD_DIM)
    v = proj[..., 2 * B_WIDTH:3 * B_WIDTH].reshape(bsz, L, B_HEADS, 2 * B_HEAD_DIM)
    gate = proj[..., 3 * B_WIDTH:]
    lam = (jnp.exp(jnp.sum(lam_q1.astype(jnp.float32) * lam_k1.astype(jnp.float32)))
           - jnp.exp(jnp.sum(lam_q2.astype(jnp.float32) * lam_k2.astype(jnp.float32)))
           + lambda_init)

    nb = L // BLOCK_Q
    key_pos = jnp.arange(L)

    def block(args):
        qb, start = args
        t = start + jnp.arange(BLOCK_Q)
        rel = t[:, None] - key_pos[None, :]
        bias = rel_bias[t5_bucket(rel)].astype(jnp.float32)
        logits = jnp.einsum('bqmd,blmd->bmql', qb, k).astype(jnp.float32)
        logits = logits + jnp.moveaxis(bias, -1, 0)[None]
        logits = jnp.where((rel >= 0)[None, None], logits, -jnp.inf)
        p = jax.nn.softmax(logits, axis=-1).reshape(bsz, B_HEADS, 2, BLOCK_Q, L)
        a = p[:, :, 0] - lam * p[:, :, 1]
        return jnp.einsum('bhql,blhe->bqhe', a.astype(v.dtype), v)

    starts = jnp.arange(nb, dtype=jnp.int32) * BLOCK_Q
    o = from_blocks(lax.map(block, (to_blocks(q, nb), starts)))
    o = rms_norm(o, subln_g) * (1.0 - lambda_init)
    o = o.reshape(bsz, L, B_WIDTH)
    return (o * jax.nn.silu(gate)) @ w_out

def setup_inputs(seed: int = 0) -> dict:
    key = jax.random.key(seed)
    ks = iter(jax.random.split(key, 32))

    def nrm(shape, fan_in, scale=1.0):
        return jax.random.normal(next(ks), shape, jnp.float32) * (scale * fan_in ** -0.5)

    def gain(shape):
        return 1.0 + 0.05 * jax.random.normal(next(ks), shape, jnp.float32)

    na, nbl = N_A_LAYERS, N_B_LAYERS
    return {
        "x": jax.random.normal(next(ks), (BATCH, SEQ, D_MODEL), jnp.float32),
        "c": jax.random.normal(next(ks), (BATCH, D_MODEL), jnp.float32),
        "rel_bias": 0.5 * jax.random.normal(next(ks), (N_BUCKETS, N_BIAS_COLS), jnp.float32),
        "mod_w": nrm((DEPTH, D_MODEL, 3 * D_MODEL), D_MODEL, 0.5),
        "mod_b": 0.02 * jax.random.normal(next(ks), (DEPTH, 3 * D_MODEL), jnp.float32),
        "pre_g": gain((DEPTH, D_MODEL)),
        "post_g": gain((DEPTH, D_MODEL)),
        "a_w_in": nrm((na, D_MODEL, A_IN), D_MODEL),
        "a_q_norm": gain((na, A_Q_RANK)),
        "a_kv_norm": gain((na, A_KV_RANK)),
        "a_kidx_norm": gain((na, IDX_DIM)),
        "a_w_uq": nrm((na, A_Q_RANK, A_WIDTH), A_Q_RANK),
        "a_w_qidx": nrm((na, A_Q_RANK, IDX_HEADS * IDX_DIM), A_Q_RANK),
        "a_w_uk": nrm((na, A_HEADS, A_KV_RANK, A_HEAD_DIM), A_KV_RANK),
        "a_w_uv": nrm((na, A_HEADS, A_KV_RANK, A_HEAD_DIM), A_KV_RANK),
        "a_w_out": nrm((na, A_WIDTH, D_MODEL), A_WIDTH),
        "b_w_in": nrm((nbl, D_MODEL, B_IN), D_MODEL),
        "b_lam_q1": 0.1 * jax.random.normal(next(ks), (nbl, B_HEAD_DIM), jnp.float32),
        "b_lam_k1": 0.1 * jax.random.normal(next(ks), (nbl, B_HEAD_DIM), jnp.float32),
        "b_lam_q2": 0.1 * jax.random.normal(next(ks), (nbl, B_HEAD_DIM), jnp.float32),
        "b_lam_k2": 0.1 * jax.random.normal(next(ks), (nbl, B_HEAD_DIM), jnp.float32),
        "b_subln": gain((nbl, 2 * B_HEAD_DIM)),
        "b_w_out": nrm((nbl, B_WIDTH, D_MODEL), B_WIDTH),
    }

def reference(x, c, rel_bias, mod_w, mod_b, pre_g, post_g,
              a_w_in, a_q_norm, a_kv_norm, a_kidx_norm, a_w_uq, a_w_qidx, a_w_uk, a_w_uv, a_w_out,
              b_w_in, b_lam_q1, b_lam_k1, b_lam_q2, b_lam_k2, b_subln, b_w_out):
    c_act = jax.nn.silu(c)
    for i in range(DEPTH):
        mod = (c_act @ mod_w[i] + mod_b[i])[:, None, :]
        shift = mod[..., :D_MODEL]
        scale = mod[..., D_MODEL:2 * D_MODEL]
        res_gate = mod[..., 2 * D_MODEL:]
        h = rms_norm(x, pre_g[i]) * (1.0 + scale) + shift
        if i % N_MIXERS == 0:
            j = i // N_MIXERS
            y = dsa_mixer(h, rel_bias, a_w_in[j], a_q_norm[j], a_kv_norm[j], a_kidx_norm[j],
                          a_w_uq[j], a_w_qidx[j], a_w_uk[j], a_w_uv[j], a_w_out[j])
        else:
            j = i // N_MIXERS
            lambda_init = 0.8 - 0.6 * math.exp(-0.3 * i)
            y = diff_mixer(h, rel_bias, b_w_in[j], b_lam_q1[j], b_lam_k1[j], b_lam_q2[j],
                           b_lam_k2[j], b_subln[j], b_w_out[j], lambda_init)
        x = x + res_gate * rms_norm(y, post_g[i])
    return x


_drawn_inputs = setup_inputs


def setup_inputs(seed=0):
    import zlib

    import numpy as np

    out = dict(_drawn_inputs(seed))
    spreads = {}
    factors = {'a_q_norm': 2.947,
     'a_kv_norm': 2.897,
     'a_kidx_norm': 2.892,
     'b_lam_q1': 5.671,
     'b_lam_k1': 8.0,
     'b_lam_q2': 8.0,
     'b_lam_k2': 8.0,
     'b_subln': 3.864}
    for name, (base, spread) in spreads.items():
        noise = np.random.default_rng([zlib.crc32(name.encode()), seed]).standard_normal(out[name].shape)
        drawn = base * np.exp(spread * noise) if base else spread * noise
        out[name] = __import__('jax').numpy.asarray(drawn.astype(out[name].dtype))
    for name, factor in factors.items():
        out[name] = (out[name] * factor).astype(out[name].dtype)
    return out
```

```python
import math
from contextlib import ExitStack

import concourse.bass as bass
import numpy as np
from concourse import mybir

F32 = mybir.dt.float32
F32R = mybir.dt.float32r
BF16 = mybir.dt.bfloat16
U16 = mybir.dt.uint16
I32 = mybir.dt.int32
ALU = mybir.AluOpType
ACT = mybir.ActivationFunctionType
AX = mybir.AxisListType
ds = bass.ds

P = 128
T = 2048
D = 1024
KD = D // P
NB = T // P
G = 4
GT = T // G
EPS = 1e-6
NBUCKETS, MAXDIST, NMAPS = 32, 128, 16
NEG = -1.0e30
LOWEST = -3.0e38
QR, KVR, ID, IH = D // 4, D // 8, 64, 8
SMALL = QR + KVR + ID + IH
TOPK = 256
HD = 64
LAMBDA_INIT = 0.8 - 0.6 * math.exp(-0.3)
NEAR = 2 * P


def bucket_onehot():
    n = np.maximum(255 - np.arange(384), 0)
    nf = np.maximum(n, 1).astype(np.float32)
    half = NBUCKETS // 2
    large = half + (np.log(nf / np.float32(half)) / np.float32(math.log(MAXDIST / half))
                    * np.float32(NBUCKETS - half)).astype(np.int32)
    b = np.where(n < half, n, np.minimum(large, NBUCKETS - 1))
    return (np.arange(NBUCKETS)[:, None] == b[None, :]).astype(np.float32)


def flat(ap):
    return ap.rearrange("p a b -> p (a b)")


class Semaphores:

    def __init__(self, nc):
        self.nc, self.held = nc, []

    def new(self, name):
        self.held.append(self.nc.alloc_semaphore(name=name))
        return self.held[-1]

    def retire(self):
        self.nc.clear_and_free_semaphores(self.held)
        self.nc.all_engine_barrier()
        self.held = []


class Stage:

    def __init__(self, nc, sems, name):
        self.nc, self.sems, self.name, self.ctx = nc, sems, name, ExitStack()

    def __enter__(self):
        return self

    def __exit__(self, *a):
        return self.ctx.__exit__(*a)

    def sb(self, name, shape, dt):
        return self.ctx.enter_context(self.nc.sbuf_tensor(f"{self.name}_sb_{name}", shape, dt))

    def ps(self, name, shape, dt=F32):
        return self.ctx.enter_context(self.nc.psum_tensor(f"{self.name}_ps_{name}", shape, dt))

    def sem(self, name):
        return self.sems.new(f"{self.name}_sem_{name}")

    def block(self):
        return self.ctx.enter_context(self.nc.Block())


def stage_modulation(nc, sems, ins, ada, neglam, gp_dram, bias_dram):
    with Stage(nc, sems, "mod") as st:
        w = st.sb("w", [P, 2, KD, D], F32)
        c = st.sb("c", [P, KD], F32)
        cact = st.sb("cact", [P, KD], F32)
        cwide = st.sb("cwide", [P, KD, P], F32)
        bcol = st.sb("bcol", [P, 2, 3 * KD], F32)
        preg = st.sb("preg", [P, 2, KD], F32)
        postg = st.sb("postg", [P, 2, D], F32)
        bgate = st.sb("bgate", [P, 2, D], F32)
        scale = st.sb("scale", [P, 2, KD], F32)
        gate = st.sb("gate", [P, 2, D], F32)
        gp = st.sb("gp", [P, 2, D], F32)
        relb = st.sb("relb", [NBUCKETS, NMAPS], F32)
        onehot = st.sb("onehot", [NBUCKETS, 384], F32)
        far = st.sb("far", [NMAPS, 1], F32)
        bvec = st.sb("bvec", [NMAPS, 384], F32)
        lams = st.sb("lams", [P, 4, HD], F32)
        lprod = st.sb("lprod", [P, 2, HD], F32)
        ldot = st.sb("ldot", [P, 2], F32)
        lexp = st.sb("lexp", [P, 2], F32)
        pcol = st.ps("pcol", [P, 2, 512])
        pgate = st.ps("pgate", [P, 2, 512])
        pbias = st.ps("pbias", [P, 512])
        small_in, w_in = st.sem("small_in"), [st.sem("w_in0"), st.sem("w_in1")]
        c_ready, cwide_ready, w_used, evacuated = (st.sem(x) for x in ("c_ready", "cwide_ready", "w_used", "evacuated"))
        bias_mm, bias_done, gate_step, stored, lam_dot, lam_exp, self_dve = (
            st.sem(x) for x in ("bias_mm", "bias_done", "gate_step", "stored", "lam_dot", "lam_exp", "self_dve"))
        block = st.block()

        @block.sync
        def _(sp):
            x = ins
            sp.dma_start(c[:], x["c"].rearrange("b (k p) -> p (b k)", p=P), allow_slow_non_contiguous=True).then_inc(small_in, 16)
            sp.dma_start(bcol[:], x["mod_b"].rearrange("l (k p) -> p l k", p=P), allow_slow_non_contiguous=True).then_inc(small_in, 16)
            sp.dma_start(preg[:], x["pre_g"].rearrange("l (k p) -> p l k", p=P), allow_slow_non_contiguous=True).then_inc(small_in, 16)
            for q in range(6):
                l, third = divmod(q, 3)
                if q >= 2:
                    sp.wait_ge(w_used, q - 1)
                sp.dma_start(w[:, q % 2], x["mod_w"][l].rearrange("(k p) n -> p k n", p=P)[:, :, third * D:(third + 1) * D]
                             ).then_inc(w_in[q % 2], 16)
                if q == 0:
                    sp.dma_start(postg[:], x["post_g"].rearrange("l n -> (l n)").partition_broadcast(P).rearrange("p (l n) -> p l n", l=2)).then_inc(small_in, 16)
                    for l in range(2):
                        sp.dma_start(bgate[:, l], x["mod_b"][l, 2 * D:3 * D].partition_broadcast(P)).then_inc(small_in, 16)
                    sp.dma_start(relb[:], x["rel_bias"]).then_inc(small_in, 16)
                    sp.dma_start(onehot[:], x["onehot"]).then_inc(small_in, 16)
                    for j, name in enumerate(("b_lam_q1", "b_lam_k1", "b_lam_q2", "b_lam_k2")):
                        sp.dma_start(lams[:, j], x[name][0].partition_broadcast(P)).then_inc(small_in, 16)
            sp.wait_ge(bias_done, 1)
            sp.dma_start(bias_dram, bvec[:].unsqueeze(1).to_broadcast([NMAPS, P, 384])).then_inc(stored, 16)
            for l in range(2):
                sp.wait_ge(gate_step, l + 1)
                sp.dma_start(gp_dram[l], gp[:, l]).then_inc(stored, 16)
            sp.wait_ge(stored, 48)

        ALL_SMALL = 16 * 12

        @block.scalar
        def _(act):
            act.wait_ge(small_in, ALL_SMALL)
            nc.scalar.activation(cact[:], c[:], ACT.Silu).then_inc(c_ready, 1)
            act.wait_ge(lam_dot, 2)
            nc.scalar.activation(lexp[:], ldot[:], ACT.Exp).then_inc(lam_exp, 1)

        @block.tensor
        def _(pe):
            pe.wait_ge(small_in, ALL_SMALL)
            nc.tensor.matmul(pbias[0:NMAPS, 0:384], relb[:], onehot[:], start=True, stop=True).then_inc(bias_mm, 1)
            pe.wait_ge(c_ready, 1)
            pe.wait_ge(cwide_ready, 1)
            for q in range(6):
                l, third = divmod(q, 3)
                pe.wait_ge(w_in[q % 2], 16 * (q // 2 + 1))
                if l == 1:
                    pe.wait_ge(evacuated, third + 1)
                if third < 2:
                    for f in range(KD):
                        for k in range(KD):
                            m = nc.tensor.matmul(pcol[:, third, f:f + 1], w[:, q % 2, k, f * P:(f + 1) * P],
                                                 cact[:, k:k + 1], start=(k == 0), stop=(k == KD - 1))
                else:
                    for n in range(2):
                        for k in range(KD):
                            m = nc.tensor.matmul(pgate[:, n, :], cwide[:, k, :], w[:, q % 2, k, n * 512:(n + 1) * 512],
                                                 start=(k == 0), stop=(k == KD - 1))
                m.then_inc(w_used, 1)

        @block.vector
        def _(dve):
            dve.wait_ge(small_in, ALL_SMALL)
            for j in range(2):
                nc.vector.tensor_tensor(lprod[:, j], lams[:, 2 * j], lams[:, 2 * j + 1], ALU.mult).then_inc(self_dve, 1)
            dve.wait_ge(self_dve, 2)
            for j in range(2):
                nc.vector.tensor_reduce(ldot[:, j:j + 1], lprod[:, j], AX.X, ALU.add).then_inc(lam_dot, 1)
            dve.wait_ge(bias_mm, 1)
            nc.vector.tensor_copy(far[:], pbias[0:NMAPS, 0:1]).then_inc(self_dve, 1)
            dve.wait_ge(self_dve, 3)
            nc.vector.tensor_scalar(bvec[:], pbias[0:NMAPS, 0:384], far[:], None, ALU.subtract).then_inc(self_dve, 1)
            dve.wait_ge(self_dve, 4)
            nc.vector.memset(bvec[:, 256:384], NEG).then_inc(bias_done, 1)
            dve.wait_ge(c_ready, 1)
            nc.vector.tensor_copy(cwide[:], cact[:].unsqueeze(2).to_broadcast([P, KD, P])).then_inc(cwide_ready, 1)
            dve.wait_ge(lam_exp, 1)
            nc.vector.tensor_scalar(neglam[:], lexp[:, 1:2], lexp[:, 0:1], -LAMBDA_INIT, ALU.subtract, ALU.add).then_inc(self_dve, 1)
            for q in range(6):
                l, third = divmod(q, 3)
                dve.wait_ge(w_used, q + 1)
                if third == 0:
                    nc.vector.tensor_tensor(ada[:, l, 1], pcol[:, 0, 0:KD], bcol[:, l, 0:KD], ALU.add).then_inc(evacuated, 1)
                elif third == 1:
                    nc.vector.tensor_tensor(scale[:, l], pcol[:, 1, 0:KD], bcol[:, l, KD:2 * KD], ALU.add).then_inc(evacuated, 1)
                    dve.wait_ge(evacuated, q + 1)
                    nc.vector.scalar_tensor_tensor(ada[:, l, 0], scale[:, l], 1.0, preg[:, l], ALU.add, ALU.mult).then_inc(self_dve, 1)
                else:
                    nc.vector.tensor_tensor(gate[:, l], flat(pgate[:]), bgate[:, l], ALU.add).then_inc(evacuated, 1)
                    dve.wait_ge(evacuated, q + 1)
                    nc.vector.tensor_tensor(gp[:, l], gate[:, l], postg[:, l], ALU.mult).then_inc(gate_step, 1)


def stage_input(nc, sems, name, x_dram, ada, layer, ident, hT):
    hT_hi, hT_lo = hT
    with Stage(nc, sems, name) as st:
        x = st.sb("x", [P, 4, D], F32)
        xn = st.sb("xn", [P, 4, D], F32)
        sq = st.sb("sq", [P, 4, D], BF16)
        h = st.sb("h", [P, 2, 512], F32)
        ss, ms, sd, rs = (st.sb(n, [P, 4], F32) for n in ("ss", "ms", "sd", "rs"))
        pt = st.ps("pt", [P, KD, 512])
        x_in = [st.sem(f"x_in{j}") for j in range(4)]
        squared, meaned, rooted, inverted, normed, turned, scaled, split_hi, split_lo = (
            st.sem(n) for n in ("squared", "meaned", "rooted", "inverted", "normed", "turned", "scaled", "split_hi", "split_lo"))
        idle_sp = st.sem("idle_sp")
        block = st.block()

        @block.sync
        def _(sp):
            with sp.Fori(0, G) as g:
                for j in range(4):
                    sp.wait_ge(normed, g * 4)
                    sp.sem_inc(idle_sp, 1)
                    sp.dma_start(x[:, j], x_dram[ds(g * 512 + j * P, P), :]).then_inc(x_in[j], 16)

        @block.scalar
        def _(act):
            with act.Fori(0, G) as g:
                for j in range(4):
                    act.wait_ge(x_in[j], g * 16 + 16)
                    act.wait_ge(meaned, g * 4)
                    nc.scalar.activation(sq[:, j], x[:, j], ACT.Square, accum_out=ss[:, j:j + 1]).then_inc(squared, 1)
                act.wait_ge(meaned, g * 4 + 4)
                act.wait_ge(inverted, g)
                nc.scalar.activation(sd[:], ms[:], ACT.Sqrt).then_inc(rooted, 1)
                for k in range(KD):
                    act.wait_ge(turned, g * KD + k + 1)
                    act.wait_ge(split_lo, g * KD + (k - 1 if k else 0))
                    nc.scalar.activation(h[:, k % 2], pt[:, k], ACT.Identity, scale=ada[:, layer, 0, k:k + 1],
                                         bias=ada[:, layer, 1, k:k + 1]).then_inc(scaled, 1)

        @block.tensor
        def _(pe):
            with pe.Fori(0, G) as g:
                pe.wait_ge(normed, g * 4 + 4)
                for k in range(KD):
                    pe.wait_ge(scaled, g * KD)
                    for j in range(4):
                        m = nc.tensor.transpose(pt[:, k, j * P:(j + 1) * P], xn[:, j, k * P:(k + 1) * P], ident[:])
                    m.then_inc(turned, 1)

        @block.vector
        def _(dve):
            with dve.Fori(0, G) as g:
                dve.wait_ge(squared, g * 4 + 4)
                dve.wait_ge(rooted, g)
                nc.vector.tensor_scalar(ms[:], ss[:], 1.0 / D, EPS, ALU.mult, ALU.add).then_inc(meaned, 4)
                dve.wait_ge(rooted, g + 1)
                dve.wait_ge(normed, g * 4)
                nc.vector.reciprocal(rs[:], sd[:]).then_inc(inverted, 1)
                dve.wait_ge(inverted, g + 1)
                dve.wait_ge(turned, g * KD)
                for j in range(4):
                    nc.vector.tensor_scalar(xn[:, j], x[:, j], rs[:, j:j + 1], None, ALU.mult).then_inc(normed, 1)
                for k in range(KD):
                    dve.wait_ge(scaled, g * KD + k + 1)
                    nc.vector.tensor_copy(hT_hi[:, k, ds(g * 512, 512)], h[:, k % 2]).then_inc(split_hi, 1)
                    dve.wait_ge(split_hi, g * KD + k + 1)
                    nc.vector.tensor_tensor(hT_lo[:, k, ds(g * 512, 512)], h[:, k % 2], hT_hi[:, k, ds(g * 512, 512)],
                                            ALU.subtract).then_inc(split_lo, 1)


def stage_project_T(nc, sems, name, xT, KB, jobs):
    xT_hi, xT_lo = xT
    with Stage(nc, sems, name) as st:
        w, w_hi, w_lo = (st.sb(n, [P, 2, KB, P], t) for n, t in (("w", F32), ("w_hi", F32R), ("w_lo", F32R)))
        any_split = any(j[4] is not None for j in jobs)
        o_plain = st.sb("o_plain", [P, 2, T], F32) if not all(j[4] is not None for j in jobs) else None
        o_hi = st.sb("o_hi", [P, 2, T], F32R) if any_split else None
        o_lo = st.sb("o_lo", [P, 2, T], F32R) if any_split else None
        acc = st.ps("acc", [P, 2, G, 512])
        idle_sp, idle_pool = st.sem("idle_sp"), st.sem("idle_pool")
        for n_job, (weights, blocks, scale, hi_dram, lo_dram) in enumerate(jobs):
            s = [st.sem(f"{n}{n_job}") for n in ("w_in0", "w_in1", "w_hi_done", "w_lo_done", "summed", "left_hi", "left_lo", "stored0", "stored1")]
            w_in, w_hi_done, w_lo_done, summed, left_hi, left_lo, stored = s[0:2], s[2], s[3], s[4], s[5], s[6], s[7:9]
            split = lo_dram is not None
            pairs = blocks // 2
            left = left_lo if split else left_hi
            with nc.Block() as block:
                @block.sync
                def _(sp):
                    for u in range(2):
                        sp.dma_start(w[:, u], weights(u)).then_inc(w_in[u], 16)

                    def store(i, u):
                        sp.wait_ge(left, (i + 1) * 8 + 4 * u + 4)
                        sp.sem_inc(idle_sp, 1)
                        for dram, buf in ([(hi_dram, o_hi), (lo_dram, o_lo)] if split else [(hi_dram, o_plain)]):
                            src = buf[:, u].bitcast(F32) if split else buf[:, u]
                            sp.dma_start(dram[ds((i * 2 + u) * P, P), :], src).then_inc(stored[u], 16)
                    if pairs > 1:
                        with sp.Fori(0, pairs - 1) as i:
                            for u in range(2):
                                sp.wait_ge(w_lo_done, i * 2 + u + 1)
                                sp.sem_inc(idle_sp, 1)
                                sp.dma_start(w[:, u], weights(i * 2 + (2 + u))).then_inc(w_in[u], 16)
                                store(i, u)
                    for u in range(2):
                        store(pairs - 1, u)
                    for u in range(2):
                        sp.wait_ge(stored[u], pairs * (32 if split else 16))

                @block.gpsimd
                def _(pool):
                    pool.sem_inc(summed, 8)
                    with pool.Fori(0, pairs) as i:
                        for u in range(2):
                            pool.wait_ge(w_in[u], i * 16 + 16)
                            pool.wait_ge(summed, i * 8 + 4 * u + 4)
                            pool.sem_inc(idle_pool, 1)
                            nc.gpsimd.tensor_copy(w_hi[:, u], w[:, u]).then_inc(w_hi_done, 1)
                            pool.wait_ge(w_hi_done, i * 2 + u + 1)
                            nc.gpsimd.tensor_tensor(w_lo[:, u], w[:, u], w_hi[:, u], ALU.subtract).then_inc(w_lo_done, 1)

                @block.tensor
                def _(pe):
                    pe.sem_inc(left, 8)
                    with pe.Fori(0, pairs) as i:
                        for u in range(2):
                            pe.wait_ge(w_lo_done, i * 2 + u + 1)
                            for g in range(G):
                                pe.wait_ge(left, i * 8 + 4 * u + g + 1)
                                terms = [(a, b, k) for a, b in ((w_hi, xT_hi), (w_lo, xT_hi), (w_hi, xT_lo)) for k in range(KB)]
                                for n, (a, b, k) in enumerate(terms):
                                    m = nc.tensor.matmul(acc[:, u, g], a[:, u, k], b[:, k, g * 512:(g + 1) * 512],
                                                         start=(n == 0), stop=(n == len(terms) - 1))
                                m.then_inc(summed, 1)

                @block.scalar
                def _(act):
                    with act.Fori(0, pairs) as i:
                        for u in range(2):
                            act.wait_ge(stored[u], i * (32 if split else 16))
                            for g in range(G):
                                act.wait_ge(summed, (i + 1) * 8 + 4 * u + g + 1)
                                if split:
                                    nc.scalar.activation(o_hi[:, u, g * 512:(g + 1) * 512], acc[:, u, g], ACT.Copy,
                                                         scale=scale).then_inc(left_hi, 1)
                                else:
                                    nc.scalar.activation(o_plain[:, u, g * 512:(g + 1) * 512], acc[:, u, g], ACT.Silu).then_inc(left_hi, 1)

                if split:
                    @block.vector
                    def _(dve):
                        with dve.Fori(0, pairs) as i:
                            for u in range(2):
                                for g in range(G):
                                    dve.wait_ge(left_hi, i * 8 + 4 * u + g + 1)
                                    nc.vector.scalar_tensor_tensor(o_lo[:, u, g * 512:(g + 1) * 512], acc[:, u, g], scale,
                                                                   o_hi[:, u, g * 512:(g + 1) * 512], ALU.mult, ALU.subtract).then_inc(left_lo, 1)


def stage_project_v(nc, sems, name, xT, KB, weights, hi_dram, lo_dram):
    xT_hi, xT_lo = xT
    with Stage(nc, sems, name) as st:
        w = st.sb("w", [P, KB, 512], F32)
        w_hi, w_lo = (st.sb(n, [P, KB, 512], F32R) for n in ("w_hi", "w_lo"))
        o_hi, o_lo = (st.sb(n, [P, 2, 512], F32R) for n in ("o_hi", "o_lo"))
        acc = st.ps("acc", [P, 4, 512])
        w_in, w_hi_done, w_lo_done, summed, left_hi, left_lo = (st.sem(n) for n in ("w_in", "w_hi_done", "w_lo_done", "summed", "left_hi", "left_lo"))
        stored = [st.sem("stored0"), st.sem("stored1")]
        idle_pool = st.sem("idle_pool")
        idle_sp = st.sem("idle_sp")
        block = st.block()

        @block.sync
        def _(sp):
            with sp.Fori(0, 2) as n:
                sp.wait_ge(w_lo_done, n)
                sp.sem_inc(idle_sp, 1)
                sp.dma_start(w[:], weights(n)).then_inc(w_in, 16)
                for tb in range(NB):
                    sp.wait_ge(left_lo, n * NB + tb + 1)
                    sp.sem_inc(idle_sp, 1)
                    for dram, buf in ((hi_dram, o_hi), (lo_dram, o_lo)):
                        sp.dma_start(dram[tb * P:(tb + 1) * P, ds(n * 512, 512)], buf[:, tb % 2].bitcast(F32)).then_inc(stored[tb % 2], 16)
            for u in range(2):
                sp.wait_ge(stored[u], 2 * (NB // 2) * 32)

        @block.gpsimd
        def _(pool):
            with pool.Fori(0, 2) as n:
                pool.wait_ge(w_in, n * 16 + 16)
                pool.wait_ge(summed, n * NB)
                pool.sem_inc(idle_pool, 1)
                nc.gpsimd.tensor_copy(w_hi[:], w[:]).then_inc(w_hi_done, 1)
                pool.wait_ge(w_hi_done, n + 1)
                nc.gpsimd.tensor_tensor(w_lo[:], w[:], w_hi[:], ALU.subtract).then_inc(w_lo_done, 1)

        @block.tensor
        def _(pe):
            with pe.Fori(0, 2) as n:
                pe.wait_ge(w_lo_done, n + 1)
                for tb in range(NB):
                    pe.wait_ge(left_lo, n * NB + max(tb - 3, 0))
                    terms = [(a, b, k) for a, b in ((xT_hi, w_hi), (xT_lo, w_hi), (xT_hi, w_lo)) for k in range(KB)]
                    for j, (a, b, k) in enumerate(terms):
                        m = nc.tensor.matmul(acc[:, tb % 4], a[:, k, tb * P:(tb + 1) * P], b[:, k], start=(j == 0), stop=(j == len(terms) - 1))
                    m.then_inc(summed, 1)

        @block.scalar
        def _(act):
            with act.Fori(0, 2) as n:
                for tb in range(NB):
                    act.wait_ge(summed, n * NB + tb + 1)
                    act.wait_ge(stored[tb % 2], n * (NB // 2 * 32) + (tb // 2) * 32)
                    nc.scalar.activation(o_hi[:, tb % 2], acc[:, tb % 4], ACT.Copy).then_inc(left_hi, 1)

        @block.vector
        def _(dve):
            with dve.Fori(0, 2) as n:
                for tb in range(NB):
                    dve.wait_ge(left_hi, n * NB + tb + 1)
                    nc.vector.tensor_tensor(o_lo[:, tb % 2], acc[:, tb % 4], o_hi[:, tb % 2], ALU.subtract).then_inc(left_lo, 1)


def stage_narrow(nc, sems, ins, hT, ident, widx, cqT, ckvT, kidxT):
    hT_hi, hT_lo = hT
    with Stage(nc, sems, "narrow") as st:
        w = st.sb("w", [P, 2, SMALL], F32)
        w_hi, w_lo = (st.sb(n, [P, KD, SMALL], F32R) for n in ("w_hi", "w_lo"))
        sq = st.sb("sq", [P, QR], F32)
        norm = st.sb("norm", [P, 2, QR + KVR + ID], F32)
        gain = st.sb("gain", [P, 4], F32)
        inv_n = st.sb("inv_n", [P, 3], F32)
        ss, ms, mse, sd, rs = (st.sb(n, [P, 3], F32) for n in ("ss", "ms", "mse", "sd", "rs"))
        o_hi, o_lo = (st.sb(n, [P, 2, 4, P], F32R) for n in ("o_hi", "o_lo"))
        acc = st.ps("acc", [P, 2, 512])
        pt = st.ps("pt", [P, 2, 4, P])
        w_in = [st.sem("w_in0"), st.sem("w_in1")]
        gains_in, consts, w_hi_done, w_lo_done, summed, squared, rooted, inverted, normed, turned, left_hi, left_lo, chain = (
            st.sem(n) for n in ("gains_in", "consts", "w_hi_done", "w_lo_done", "summed", "squared", "rooted", "inverted", "normed",
                                "turned", "left_hi", "left_lo", "chain"))
        stored = [st.sem("stored0"), st.sem("stored1")]
        block = st.block()
        segs = [(0, QR), (QR, QR + KVR), (QR + KVR, QR + KVR + ID)]

        @block.sync
        def _(sp):
            win = ins["a_w_in"][0].rearrange("(k p) n -> k p n", p=P)
            for k in range(KD):
                if k >= 2:
                    sp.wait_ge(w_lo_done, k - 1)
                sp.dma_start(w[:, k % 2], win[k, :, 0:SMALL]).then_inc(w_in[k % 2], 16)
                if k == 1:
                    sp.dma_start(gain[:, 0:2], ins["a_q_norm"][0].rearrange("(k p) -> p k", p=P), allow_slow_non_contiguous=True).then_inc(gains_in, 16)
                    sp.dma_start(gain[:, 2:3], ins["a_kv_norm"].rearrange("o p -> p o"), allow_slow_non_contiguous=True).then_inc(gains_in, 16)
                    sp.dma_start(gain[0:ID, 3:4], ins["a_kidx_norm"].rearrange("o p -> p o"), allow_slow_non_contiguous=True).then_inc(gains_in, 16)
            for tb in range(NB):
                sp.wait_ge(left_lo, 6 * tb + 6)
                cols = slice(tb * P, (tb + 1) * P)
                for part, buf in ((0, o_hi), (1, o_lo)):
                    for j in range(2):
                        sp.dma_start(cqT[part, j * P:(j + 1) * P, cols], buf[:, tb % 2, j].bitcast(F32)).then_inc(stored[tb % 2], 16)
                    sp.dma_start(ckvT[part, :, cols], buf[:, tb % 2, 2].bitcast(F32)).then_inc(stored[tb % 2], 16)
                    sp.dma_start(kidxT[part, :, cols], buf[0:ID, tb % 2, 3].bitcast(F32)).then_inc(stored[tb % 2], 16)
            for u in range(2):
                sp.wait_ge(stored[u], NB // 2 * 128)

        @block.gpsimd
        def _(pool):
            for j, (a, b) in enumerate(segs):
                nc.gpsimd.memset(inv_n[:, j:j + 1], 1.0 / (b - a)).then_inc(consts, 1)
            for k in range(KD):
                pool.wait_ge(w_in[k % 2], 16 * (k // 2 + 1))
                nc.gpsimd.tensor_copy(w_hi[:, k], w[:, k % 2]).then_inc(w_hi_done, 1)
                pool.wait_ge(w_hi_done, k + 1)
                nc.gpsimd.tensor_tensor(w_lo[:, k], w[:, k % 2], w_hi[:, k], ALU.subtract).then_inc(w_lo_done, 1)

        @block.tensor
        def _(pe):
            def project(tb):
                if tb >= 2:
                    pe.wait_ge(normed, 4 * (tb - 1))
                terms = [(a, b, k) for k in range(KD) for a, b in ((hT_hi, w_hi), (hT_lo, w_hi), (hT_hi, w_lo))]
                for n, (a, b, k) in enumerate(terms):
                    if tb == 0 and n % 3 == 0:
                        pe.wait_ge(w_lo_done, k + 1)
                    m = nc.tensor.matmul(acc[:, tb % 2, 0:SMALL], a[:, k, tb * P:(tb + 1) * P], b[:, k],
                                         start=(n == 0), stop=(n == len(terms) - 1))
                m.then_inc(summed, 1)

            def turn(tb):
                pe.wait_ge(normed, 4 * tb + 4)
                if tb >= 2:
                    pe.wait_ge(left_lo, 6 * (tb - 1))
                for j in range(3):
                    nc.tensor.transpose(pt[:, tb % 2, j], norm[:, tb % 2, j * P:(j + 1) * P], ident[:])
                nc.tensor.transpose(pt[0:ID, tb % 2, 3], norm[:, tb % 2, 3 * P:3 * P + ID], ident[:]).then_inc(turned, 1)

            for tb in range(NB):
                project(tb)
                if tb:
                    turn(tb - 1)
            turn(NB - 1)

        parts = [(j, P if j < 3 else ID) for j in range(4)]

        @block.scalar
        def _(act):
            act.wait_ge(gains_in, 48)
            act.wait_ge(consts, 3)

            def leave(tb):
                act.wait_ge(turned, tb + 1)
                if tb >= 2:
                    act.wait_ge(stored[tb % 2], 128 * (tb // 2))
                for j, rows in parts:
                    nc.scalar.activation(o_hi[0:rows, tb % 2, j], pt[0:rows, tb % 2, j], ACT.Copy,
                                         scale=gain[0:rows, j:j + 1]).then_inc(left_hi, 1)

            for tb in range(NB):
                act.wait_ge(summed, tb + 1)
                if tb:
                    act.wait_ge(inverted, tb)
                for j, (a, b) in enumerate(segs):
                    if tb or j:
                        act.wait_ge(squared, 3 * tb + j)
                    nc.scalar.activation(sq[:, 0:b - a], acc[:, tb % 2, a:b], ACT.Square, accum_out=ss[:, j:j + 1]).then_inc(squared, 1)
                act.wait_ge(chain, 2 * tb + 2)
                nc.scalar.activation(sd[:], mse[:], ACT.Sqrt).then_inc(rooted, 1)
                if tb:
                    leave(tb - 1)
            leave(NB - 1)

        @block.vector
        def _(dve):
            dve.wait_ge(gains_in, 48)
            dve.wait_ge(consts, 3)

            def leave(tb):
                dve.wait_ge(left_hi, 4 * tb + 4)
                for j, rows in parts:
                    m = nc.vector.scalar_tensor_tensor(o_lo[0:rows, tb % 2, j], pt[0:rows, tb % 2, j], gain[0:rows, j:j + 1],
                                                       o_hi[0:rows, tb % 2, j], ALU.mult, ALU.subtract)
                    m.then_inc(left_lo, 3 if j == 3 else 1)

            for tb in range(NB):
                dve.wait_ge(squared, 3 * tb + 3)
                nc.vector.tensor_tensor(ms[:], ss[:], inv_n[:], ALU.mult).then_inc(chain, 1)
                dve.wait_ge(chain, 2 * tb + 1)
                nc.vector.tensor_scalar(mse[:], ms[:], EPS, None, ALU.add).then_inc(chain, 1)
                dve.wait_ge(rooted, tb + 1)
                if tb:
                    dve.wait_ge(normed, 4 * tb)
                nc.vector.reciprocal(rs[:], sd[:]).then_inc(inverted, 1)
                dve.wait_ge(inverted, tb + 1)
                if tb >= 2:
                    dve.wait_ge(turned, tb - 1)
                for j, (a, b) in enumerate(segs):
                    nc.vector.tensor_scalar(norm[:, tb % 2, a:b], acc[:, tb % 2, a:b], rs[:, j:j + 1], None, ALU.mult).then_inc(normed, 1)
                nc.vector.tensor_scalar(widx[:, tb], acc[:, tb % 2, SMALL - IH:SMALL], IH ** -0.5 * ID ** -0.5, None,
                                        ALU.mult).then_inc(normed, 1)
                if tb:
                    leave(tb - 1)
            leave(NB - 1)


def near_start(b):
    return max(b - 1, 0) * P


def mask_offset(b):
    return P * sum(i + 1 for i in range(2, b))


def chunks(b):
    n = (b + 1) * P
    return [(c, min(c + 512, n)) for c in range(0, n, 512)]


def quads(b):
    return [(j, min(j + 4, b + 1)) for j in range(0, b + 1, 4)]


NCH = [len(chunks(b)) for b in range(NB)]
CH_BEFORE = [sum(NCH[:b]) for b in range(NB + 1)]
PVQ_BEFORE = [sum(range(1, g + 1)) for g in range(G + 1)]


SR, TR, OR = 4, 2, 2
LR, LR2 = 4, 2


def pieces(b):
    out, ns = [], near_start(b)
    for i, (a, z) in enumerate(chunks(b)):
        if a < ns:
            out.append((i, a, min(z, ns), False))
        if z > ns:
            out.append((i, max(a, ns), z, True))
    return out


def stage_attention(nc, sems, name, heads, M, ident, bias_dram, q_dram, k_dram, v_dram, o_dram, sums, mask=None, neglam=None):
    V2 = M == 1
    width = HD if V2 else P
    NU = M * NB
    NCHUNK = M * CH_BEFORE[NB]
    NQUAD = CH_BEFORE[NB]
    NPV = PVQ_BEFORE[G]
    assert NCHUNK % SR == 0 and NQUAD % TR == 0 and NB % LR == 0

    def chained(b):
        return sum((not near and z != chunks(b)[i][1]) or (near and V2 and b >= 2) for i, a, z, near in pieces(b))
    unit = lambda b, m: b * M + m
    chain_before = lambda b, m: M * sum(chained(x) for x in range(b)) + m * chained(b)
    NCHAIN = chain_before(NB, 0)

    with Stage(nc, sems, name) as st:
        q = st.sb("q", [P, M, T], F32R)
        k_hh, k_ll = (st.sb(n, [P, M, T], F32R) for n in ("k_hh", "k_ll"))
        v = st.sb("v", [P, 1 if V2 else 2, NB, P], F32R)
        near = st.sb("near", [P, M, NEAR], F32)
        lg = st.sb("lg", [P, LR, T], F32)
        lg2 = st.sb("lg2", [P, LR2, T], F32) if M == 2 else None
        pT_hi, pT_lo = (st.sb(n, [P, NB, 512], F32R) for n in ("pT_hi", "pT_lo"))
        o_sb = st.sb("o_sb", [P, OR, 512], F32)
        o_half = st.sb("o_half", [HD, OR, 512], F32) if V2 else None
        mx = st.sb("mx", [P, NU, 8], F32)
        negm = st.sb("negm", [P, NU], F32)
        rec, ratio = (st.sb(n, [P, NB], F32) if M == 2 else None for n in ("rec", "ratio"))
        s_ps, t_ps, o_ps = st.ps("s", [P, SR, 512]), st.ps("t", [P, TR, 4, P]), st.ps("o", [P, OR, 512])
        qk_in, v_in, s_done, s_left, dve_chain, max_done, exp_done, mixed, mix_chain, turned, t_hi, t_lo, pv_quad, half_done, o_left = (
            st.sem(n) for n in ("qk_in", "v_in", "s_done", "s_left", "dve_chain", "max_done", "exp_done", "mixed", "mix_chain",
                                "turned", "t_hi", "t_lo", "pv_quad", "half_done", "o_left"))
        o_stored = [st.sem("o_stored0"), st.sem("o_stored1")]
        idle_sp, idle_dve = st.sem("idle_sp"), st.sem("idle_dve")
        QK_IN = 16 * 7 * M
        block = st.block()

        @block.sync
        def _(sp):
            def load_qk(h):
                for m in range(M):
                    rows = ds((h * M + m) * HD, HD)
                    for part in range(2):
                        half = slice(part * HD, (part + 1) * HD)
                        sp.dma_start(q[half, m].bitcast(F32), q_dram[part, rows, :]).then_inc(qk_in, 16)
                        sp.dma_start(k_hh[half, m].bitcast(F32), k_dram[0, rows, :]).then_inc(qk_in, 16)
                        sp.dma_start(k_ll[half, m].bitcast(F32), k_dram[1, rows, :]).then_inc(qk_in, 16)
                    sp.dma_start(near[:, m], bass.AP(bias_dram.tensor, (h * M + m) * (P * 384) + P - 1, [[383, P], [1, NEAR]])).then_inc(qk_in, 16)

            def load_v(h):
                for part in range(2):
                    dst = v[:, 0, :, part * HD:(part + 1) * HD] if V2 else v[:, part]
                    sp.dma_start(dst.bitcast(F32), v_dram[part].rearrange("(j p) e -> p j e", p=P)[:, :, ds(h * width, width)]).then_inc(v_in, 16)

            def store(h, g):
                sp.wait_ge(o_left, OR + h * G + g + 1)
                sp.sem_inc(idle_sp, 1)
                sp.dma_start(o_dram[ds(h * width, width), g * 512:(g + 1) * 512], o_sb[0:width, g % 2]).then_inc(o_stored[g % 2], 16)

            load_qk(0)
            load_v(0)
            with sp.Fori(0, heads - 1) as h:
                for g in range(G - 1):
                    store(h, g)
                sp.wait_ge(s_left, SR + h * NCHUNK + NCHUNK)
                sp.sem_inc(idle_sp, 1)
                load_qk(h + 1)
                sp.wait_ge(pv_quad, NPV + h * NPV + NPV)
                sp.sem_inc(idle_sp, 1)
                load_v(h + 1)
                store(h, G - 1)
            for g in range(G):
                store(heads - 1, g)
            for u in range(2):
                sp.wait_ge(o_stored[u], heads * 2 * 16)

        @block.tensor
        def _(pe):
            pe.sem_inc(s_left, SR)
            pe.sem_inc(t_lo, TR)
            pe.sem_inc(o_left, OR)

            def logits(h, b):
                for m in range(M):
                    for i, (a, z) in enumerate(chunks(b)):
                        n = M * CH_BEFORE[b] + m * NCH[b] + i
                        out = s_ps[:, n % SR, 0:z - a]
                        pe.wait_ge(s_left, h * NCHUNK + n + 1)
                        nc.tensor.matmul(out, q[:, m, b * P:(b + 1) * P], k_hh[:, m, a:z], start=True, stop=False)
                        nc.tensor.matmul(out, q[:, m, b * P:(b + 1) * P], k_ll[:, m, a:z], start=False, stop=True).then_inc(s_done, 1)

            def turn(h, b):
                if M == 2:
                    pe.wait_ge(mixed, LR2 + h * NB + b + 1)
                else:
                    pe.wait_ge(exp_done, h * NB + b + 1)
                for i, (a, z) in enumerate(quads(b)):
                    n = CH_BEFORE[b] + i
                    pe.wait_ge(t_lo, h * NQUAD + n + 1)
                    for j in range(a, z):
                        x = nc.tensor.transpose(t_ps[:, n % TR, j - a], lg[:, b % LR, j * P:(j + 1) * P], ident[:])
                    x.then_inc(turned, 1)

            def values(h, g):
                pe.wait_ge(o_left, h * G + g + 1)
                if g == 0:
                    pe.wait_ge(v_in, h * 32 + 32)
                last = 4 * g + 3
                terms = [(0, pT_hi), (0, pT_lo)] if V2 else [(0, pT_hi), (0, pT_lo), (1, pT_hi)]
                for j in range(last + 1):
                    if j % 4 == 0:
                        pe.wait_ge(t_lo, TR + h * NQUAD + CH_BEFORE[last] + j // 4 + 1)
                    a = max(j - 4 * g, 0) * P
                    for i, (part, p) in enumerate(terms):
                        x = nc.tensor.matmul(o_ps[:, g % 2, a:512], v[:, part, j], p[:, j, a:512],
                                             start=(j == 0 and i == 0), stop=(j == last and i == len(terms) - 1))
                    if j % 4 == 3:
                        x.then_inc(pv_quad, 1)

            with pe.Fori(0, heads) as h:
                pe.wait_ge(qk_in, h * QK_IN + QK_IN)
                for b in range(NB):
                    logits(h, b)
                    if b >= 2:
                        turn(h, b - 2)
                        if (b - 2) % 4 == 3:
                            values(h, (b - 2) // 4)
                turn(h, NB - 2)
                turn(h, NB - 1)
                values(h, G - 1)

        @block.vector
        def _(dve):
            dve.sem_inc(turned, NQUAD)
            dve.sem_inc(mixed, LR2)

            def logits(h, b, m):
                u, dst, slot = unit(b, m), (lg if m == 0 else lg2), b % (LR if m == 0 else LR2)
                if m == 0:
                    before = NQUAD + CH_BEFORE[b - LR + 1] if b >= LR else CH_BEFORE[NB - LR + b + 1]
                    dve.wait_ge(turned, h * NQUAD + before)
                else:
                    dve.wait_ge(mixed, h * NB + b + 1)
                nchain, ncol = chain_before(b, m), 0
                for i, a, z, is_near in pieces(b):
                    n = M * CH_BEFORE[b] + m * NCH[b] + i
                    c0 = i * 512
                    src, out = s_ps[:, n % SR, a - c0:z - c0], dst[:, slot, a:z]
                    top = mx[:, u, ncol:ncol + 1]
                    ends = z == chunks(b)[i][1]
                    ncol += 1
                    dve.wait_ge(s_done, h * NCHUNK + n + 1)
                    if is_near:
                        off = P * (1 - b) if b < 1 else -P * (b - 1)
                        if a == near_start(b):
                            dve.wait_ge(qk_in, h * QK_IN + QK_IN)
                        tab = near[:, m, a + off:z + off]
                        if V2 and b >= 2:
                            nc.vector.tensor_tensor(out, src, tab, ALU.add).then_inc(s_left, 1)
                            dve.wait_ge(s_left, SR + h * NCHUNK + n + 1)
                            dve.sem_inc(idle_dve, 1)
                            sel = mask[:, mask_offset(b) + a:mask_offset(b) + z]
                            nc.vector.tensor_tensor_reduce(out, out, sel, 1.0, 2 * NEG, ALU.add, ALU.max, top).then_inc(dve_chain, 1)
                            nchain += 1
                        else:
                            dve.sem_inc(idle_dve, 1)
                            nc.vector.tensor_tensor_reduce(out, src, tab, 1.0, 2 * NEG, ALU.add, ALU.max, top).then_inc(s_left, 1)
                    else:
                        if V2:
                            dve.sem_inc(idle_dve, 1)
                            sel = mask[:, mask_offset(b) + a:mask_offset(b) + z]
                            x = nc.vector.tensor_tensor_reduce(out, src, sel, 1.0, 2 * NEG, ALU.add, ALU.max, top)
                        else:
                            x = nc.vector.tensor_scalar(out, src, 1.0, 2 * NEG, ALU.mult, ALU.max, accum_out=top)
                        if ends:
                            x.then_inc(s_left, 1)
                        else:
                            x.then_inc(dve_chain, 1)
                            nchain += 1
                dve.wait_ge(s_left, SR + h * NCHUNK + M * CH_BEFORE[b] + (m + 1) * NCH[b])
                dve.wait_ge(dve_chain, h * NCHAIN + nchain)
                nc.vector.tensor_reduce(negm[:, u:u + 1], mx[:, u, 0:ncol], AX.X, ALU.max, negate=True).then_inc(max_done, 1)

            def mix(h, b):
                l1, l2 = sums[:, b, ds(h * 2, 1)], sums[:, b, ds(h * 2 + 1, 1)]
                dve.wait_ge(exp_done, h * NU + 2 * b + 2)
                nc.vector.reciprocal(rec[:, b:b + 1], l2).then_inc(mix_chain, 1)
                dve.wait_ge(mix_chain, h * (2 * NB) + 2 * b + 1)
                nc.vector.scalar_tensor_tensor(ratio[:, b:b + 1], l1, rec[:, b:b + 1], neglam[:], ALU.mult, ALU.mult).then_inc(mix_chain, 1)
                dve.wait_ge(mix_chain, h * (2 * NB) + 2 * b + 2)
                n = (b + 1) * P
                nc.vector.scalar_tensor_tensor(lg[:, b % LR, 0:n], lg2[:, b % LR2, 0:n], ratio[:, b:b + 1], lg[:, b % LR, 0:n],
                                               ALU.mult, ALU.add).then_inc(mixed, 1)

            def split_lo(h, b):
                g, c = b // 4, (b % 4) * P
                for i, (a, z) in enumerate(quads(b)):
                    n = CH_BEFORE[b] + i
                    dve.wait_ge(t_hi, h * NQUAD + n + 1)
                    nc.vector.tensor_tensor(pT_lo[:, a:z, c:c + P], t_ps[:, n % TR, 0:z - a], pT_hi[:, a:z, c:c + P],
                                            ALU.subtract).then_inc(t_lo, 1)

            def output(h, g):
                if V2:
                    dve.wait_ge(half_done, h * G + g + 1)
                    dve.wait_ge(o_stored[g % 2], h * 32 + (g // 2) * 16)
                    nc.vector.tensor_tensor(o_sb[0:HD, g % 2], o_ps[0:HD, g % 2], o_half[:, g % 2], ALU.add).then_inc(o_left, 1)

            with dve.Fori(0, heads) as h:
                for b in range(NB + 2):
                    if b < NB:
                        for m in range(M):
                            logits(h, b, m)
                    if M == 2 and 1 <= b <= NB:
                        mix(h, b - 1)
                    if b >= 2:
                        if b - 3 >= 0 and (b - 3) % 4 == 3:
                            output(h, (b - 3) // 4)
                        split_lo(h, b - 2)
                output(h, G - 1)

        @block.scalar
        def _(act):
            act.sem_inc(pv_quad, NPV)

            def exps(h, b, m):
                u, buf, slot, n = unit(b, m), (lg if m == 0 else lg2), b % (LR if m == 0 else LR2), (b + 1) * P
                act.wait_ge(max_done, h * NU + u + 1)
                nc.scalar.activation(buf[:, slot, 0:n], buf[:, slot, 0:n], ACT.Exp, bias=negm[:, u:u + 1],
                                     accum_out=sums[:, b, ds(h * M + m, 1)]).then_inc(exp_done, 1)

            def split_hi(h, b):
                g, c = b // 4, (b % 4) * P
                for i, (a, z) in enumerate(quads(b)):
                    n = CH_BEFORE[b] + i
                    act.wait_ge(turned, NQUAD + h * NQUAD + n + 1)
                    used = NPV + PVQ_BEFORE[g - 1] + i + 1 if i < g else PVQ_BEFORE[G - 1] + i + 1
                    act.wait_ge(pv_quad, h * NPV + used)
                    nc.scalar.activation(pT_hi[:, a:z, c:c + P], t_ps[:, n % TR, 0:z - a], ACT.Copy).then_inc(t_hi, 1)

            def output(h, g):
                act.wait_ge(pv_quad, NPV + h * NPV + PVQ_BEFORE[g + 1])
                if V2:
                    act.wait_ge(o_left, h * G + g + 1)
                    nc.scalar.activation(o_half[:, g % 2], o_ps[HD:P, g % 2], ACT.Copy).then_inc(half_done, 1)
                else:
                    act.wait_ge(o_stored[g % 2], h * 32 + (g // 2) * 16)
                    nc.scalar.activation(o_sb[:, g % 2], o_ps[:, g % 2], ACT.Copy).then_inc(o_left, 1)

            with act.Fori(0, heads) as h:
                for b in range(NB + 2):
                    if b < NB:
                        for m in range(M):
                            exps(h, b, m)
                    if b >= 2:
                        if b - 3 >= 0 and (b - 3) % 4 == 3:
                            output(h, (b - 3) // 4)
                        split_hi(h, b - 2)
                output(h, G - 1)


SELECTING = range(2, NB)
KEYS = mask_offset(NB)


def stage_select(nc, sems, widx, qidx, kidxT, mask):
    with Stage(nc, sems, "select") as st:
        k_hh, k_ll = (st.sb(n, [P, T], F32R) for n in ("k_hh", "k_ll"))
        q = st.sb("q", [P, 2, IH, P], F32R)
        relu = st.sb("relu", [P, 2, T], F32)
        score = st.sb("score", [P, T], F32)
        causal = st.sb("causal", [P, P], F32)
        flip = st.sb("flip", [P, T], I32)
        key = st.sb("key", [P, 2, T], I32)
        k_up, k_down = (st.sb(n, [P, KEYS], U16) for n in ("k_up", "k_down"))
        NS = len(SELECTING)
        cand, cnt, need, ge, moved, top, low = (st.sb(n, [P, NS], F32) for n in ("cand", "cnt", "need", "ge", "moved", "top", "low"))
        bit, half = st.sb("bit", [P, 1], F32), st.sb("half", [P, 1], F32)
        above, equal, taken, kept = (st.sb(n, [P, T], BF16) for n in ("above", "equal", "taken", "kept"))
        s_ps = st.ps("s", [P, 2, 4 * 512])
        k_in, scored, relued, summed, keyed, packed, causal_step, chain, counted = (
            st.sem(n) for n in ("k_in", "scored", "relued", "summed", "keyed", "packed", "causal_step", "chain", "counted"))
        q_in = [st.sem("q_in0"), st.sem("q_in1")]
        units = [(i, b, h) for i, b in enumerate(SELECTING) for h in range(IH)]
        block = st.block()

        @block.sync
        def _(sp):
            for part in range(2):
                rows = slice(part * ID, (part + 1) * ID)
                sp.dma_start(k_hh[rows].bitcast(F32), kidxT[0]).then_inc(k_in, 16)
                sp.dma_start(k_ll[rows].bitcast(F32), kidxT[1]).then_inc(k_in, 16)
            for i, b in enumerate(SELECTING):
                if i >= 2:
                    sp.wait_ge(scored, IH * (i - 1))
                for part in range(2):
                    sp.dma_start(q[part * ID:(part + 1) * ID, i % 2].bitcast(F32),
                                 qidx[part].rearrange("(h d) t -> d h t", d=ID)[:, :, b * P:(b + 1) * P]).then_inc(q_in[i % 2], 16)

        @block.gpsimd
        def _(pool):
            nc.gpsimd.memset(causal[:], 0.0).then_inc(causal_step, 1)
            pool.wait_ge(causal_step, 1)
            nc.gpsimd.affine_select(out=causal[:], in_=causal[:], compare_op=ALU.is_ge, fill=LOWEST, base=0,
                                    pattern=[[-1, P]], channel_multiplier=1).then_inc(causal_step, 1)

        @block.tensor
        def _(pe):
            pe.wait_ge(k_in, 64)
            for n, (i, b, h) in enumerate(units):
                if h == 0:
                    pe.wait_ge(q_in[i % 2], 32 * (i // 2 + 1))
                if n >= 2:
                    pe.wait_ge(relued, n - 1)
                for a, z in chunks(b):
                    out = s_ps[:, n % 2, a:z]
                    nc.tensor.matmul(out, q[:, i % 2, h], k_hh[:, a:z], start=True, stop=False)
                    x = nc.tensor.matmul(out, q[:, i % 2, h], k_ll[:, a:z], start=False, stop=True)
                x.then_inc(scored, 1)

        @block.scalar
        def _(act):
            def pack(i):
                b = SELECTING[i]
                n, o = (b + 1) * P, mask_offset(b)
                act.wait_ge(keyed, i + 1)
                halves = key[:, i % 2].bitcast(U16).rearrange("p (s two) -> p s two", two=2)
                nc.scalar.activation(k_up[:, o:o + n], halves[:, 0:n, 1], ACT.Copy).then_inc(packed, 1)
                nc.scalar.activation(k_down[:, o:o + n], halves[:, 0:n, 0], ACT.Copy).then_inc(packed, 1)

            for n, (i, b, h) in enumerate(units):
                act.wait_ge(scored, n + 1)
                if n >= 2:
                    act.wait_ge(summed, n - 1)
                nc.scalar.activation(relu[:, n % 2, 0:(b + 1) * P], s_ps[:, n % 2, 0:(b + 1) * P], ACT.Relu).then_inc(relued, 1)
                if h == 3 and i:
                    pack(i - 1)
            pack(NS - 1)

        @block.vector
        def _(dve):
            done = [0]

            def step(x):
                x.then_inc(chain, 1)
                done[0] += 1
                dve.wait_ge(chain, done[0])

            for n, (i, b, h) in enumerate(units):
                w, N = widx[:, b, h:h + 1], (b + 1) * P
                dve.wait_ge(relued, n + 1)
                if n:
                    dve.wait_ge(summed, n)
                if h == 0:
                    if i:
                        dve.wait_ge(keyed, i)
                    nc.vector.tensor_scalar(score[:, 0:N], relu[:, n % 2, 0:N], w, 0.0, ALU.mult, ALU.add).then_inc(summed, 1)
                else:
                    nc.vector.scalar_tensor_tensor(score[:, 0:N], relu[:, n % 2, 0:N], w, score[:, 0:N], ALU.mult, ALU.add).then_inc(summed, 1)
                if h == IH - 1:
                    dve.wait_ge(causal_step, 2)
                    dve.wait_ge(summed, n + 1)
                    step(nc.vector.tensor_tensor(score[:, N - P:N], score[:, N - P:N], causal[:], ALU.add))
                    step(nc.vector.tensor_scalar(flip[:, 0:N], score[:, 0:N].bitcast(I32), 31, -2 ** 31, ALU.arith_shift_right, ALU.bitwise_or))
                    if i >= 2:
                        dve.wait_ge(packed, 2 * (i - 1))
                    nc.vector.tensor_tensor(key[:, i % 2, 0:N], score[:, 0:N].bitcast(I32), flip[:, 0:N], ALU.bitwise_xor).then_inc(keyed, 1)

            step(nc.vector.memset(need[:], float(TOPK)))
            dve.wait_ge(packed, 2 * NS)
            cols = [(i, mask_offset(b), (b + 1) * P) for i, b in enumerate(SELECTING)]
            counts = [0]

            def count(keys, op, against):
                for i, o, N in cols:
                    nc.vector.tensor_scalar(mask[:, o:o + N], keys[:, o:o + N], against[:, i:i + 1], 0.0, op, ALU.add,
                                            accum_out=cnt[:, i:i + 1]).then_inc(counted, 1)

            STEPS, SMALL_STEPS = 16, 5
            for phase, keys, found in ((0, k_up, top), (1, k_down, low)):
                step(nc.vector.memset(cand[:], 32768.0))
                step(nc.vector.memset(bit[:], 32768.0))
                step(nc.vector.memset(half[:], 16384.0))
                c0, n0 = done[0], counts[0]
                with dve.Fori(0, STEPS) as s:
                    count(keys, ALU.is_ge, cand)
                    dve.wait_ge(counted, s * NS + (n0 + NS))
                    ops = [lambda: nc.vector.tensor_tensor(ge[:], cnt[:], need[:], ALU.is_ge),
                           lambda: nc.vector.scalar_tensor_tensor(moved[:], ge[:], bit[:], cand[:], ALU.mult, ALU.add),
                           lambda: nc.vector.tensor_scalar(cand[:], moved[:], half[:], None, ALU.subtract),
                           lambda: nc.vector.tensor_scalar(bit[:], bit[:], 0.5, None, ALU.mult),
                           lambda: nc.vector.tensor_scalar(half[:], half[:], 0.5, None, ALU.mult)]
                    for j, op in enumerate(ops):
                        op().then_inc(chain, 1)
                        dve.wait_ge(chain, s * SMALL_STEPS + (c0 + j + 1))
                done[0] += STEPS * SMALL_STEPS
                counts[0] += STEPS * NS
                step(nc.vector.tensor_scalar(found[:], cand[:], 0.5, None, ALU.subtract))
                if phase == 0:
                    count(k_up, ALU.is_gt, top)
                    counts[0] += NS
                    dve.wait_ge(counted, counts[0])
                    step(nc.vector.tensor_scalar(need[:], cnt[:], -1.0, float(TOPK), ALU.mult, ALU.add))
                    for i, o, N in cols:
                        x = nc.vector.scalar_tensor_tensor(k_down[:, o:o + N], k_up[:, o:o + N], top[:, i:i + 1], k_down[:, o:o + N],
                                                           ALU.is_equal, ALU.mult)
                        x.then_inc(chain, 1)
                        done[0] += 1
                    dve.wait_ge(chain, done[0])

            up_dist, dist, rank = relu[:, 0], relu[:, 1], score
            for i, o, N in cols:
                step(nc.vector.tensor_scalar(up_dist[:, 0:N], k_up[:, o:o + N], top[:, i:i + 1], 131072.0, ALU.subtract, ALU.mult))
                step(nc.vector.scalar_tensor_tensor(dist[:, 0:N], k_down[:, o:o + N], low[:, i:i + 1], up_dist[:, 0:N], ALU.subtract, ALU.add))
                step(nc.vector.tensor_scalar(above[:, 0:N], dist[:, 0:N], 0.0, 0.0, ALU.is_gt, ALU.add, accum_out=cnt[:, i:i + 1]))
                step(nc.vector.tensor_scalar(equal[:, 0:N], dist[:, 0:N], 0.0, None, ALU.is_equal))
                step(nc.vector.tensor_scalar(need[:, i:i + 1], cnt[:, i:i + 1], -1.0, float(TOPK), ALU.mult, ALU.add))
                step(nc.vector.tensor_tensor_scan(rank[:, 0:N], equal[:, 0:N], equal[:, 0:N], 0.0, ALU.add, ALU.max))
                step(nc.vector.scalar_tensor_tensor(taken[:, 0:N], rank[:, 0:N], need[:, i:i + 1], equal[:, 0:N], ALU.is_le, ALU.mult))
                step(nc.vector.tensor_tensor(kept[:, 0:N], above[:, 0:N], taken[:, 0:N], ALU.add))
                step(nc.vector.tensor_scalar(mask[:, o:o + N], kept[:, 0:N], -1.0, -NEG, ALU.add, ALU.mult))


def stage_output(nc, sems, name, M, x_dram, dst, weights, o_dram, gate_dram, gp_row, sums, ident, subln=None):
    heads = NMAPS // M
    with Stage(nc, sems, name) as st:
        w = st.sb("w", [P, 2, D], F32)
        w_hi, w_lo = (st.sb(n, [P, KD, D], F32R) for n in ("w_hi", "w_lo"))
        gp = st.sb("gp", [P, D], F32)
        inv = st.sb("inv", [P, 4, heads], F32)
        inv_wide = st.sb("inv_wide", [P, 4, D], F32)
        o, gate, scaled, gated = (st.sb(n, [P, 2, 512], F32) for n in ("o", "gate", "scaled", "gated"))
        og_hi, og_lo = (st.sb(n, [P, KD, 512], F32R) for n in ("og_hi", "og_lo"))
        x = st.sb("x", [P, 4, D], F32)
        z = st.sb("z", [P, 2, D], F32)
        out = st.sb("out", [P, 2, D], F32)
        ysq = st.sb("ysq", [P, D], BF16)
        ss, ms, sd, rs = (st.sb(n, [P, 4], F32) for n in ("ss", "ms", "sd", "rs"))
        if M == 2:
            ones, gcol = st.sb("ones", [P, P], F32), st.sb("gcol", [P, 1], F32)
            hsq, hms, hsd, hrs, hn = (st.sb(n, [P, 512], F32) for n in ("hsq", "hms", "hsd", "hrs", "hn"))
        inv_ps = st.ps("inv", [P, 2, 512])
        head_ps = st.ps("head", [P, 512])
        y_ps = st.ps("y", [P, 2, 2, 512])
        w_in = [st.sem("w_in0"), st.sem("w_in1")]
        o_in = [st.sem("o_in0"), st.sem("o_in1")]
        x_in = st.sem("x_in")
        names = ("consts_in", "w_hi_done", "w_lo_done", "inverted", "widened", "turned", "scaled_done", "gated_done", "og_hi_done", "og_lo_done",
                 "y_done", "ysq_done", "meaned", "rooted", "rs_done", "normed", "added", "h_sq", "h_sum", "h_mean", "h_root", "h_inv", "h_norm", "gcol_done")
        (consts_in, w_hi_done, w_lo_done, inverted, widened, turned, scaled_done, gated_done, og_hi_done, og_lo_done,
         y_done, ysq_done, meaned, rooted, rs_done, normed, added, h_sq, h_sum, h_mean, h_root, h_inv, h_norm, gcol_done) = (st.sem(n) for n in names)
        stored = [st.sem("stored0"), st.sem("stored1")]
        idle_sp = st.sem("idle_sp")
        block = st.block()

        @block.sync
        def _(sp):
            sp.dma_start(gp[:], gp_row).then_inc(consts_in, 16)
            if M == 2:
                sp.dma_start(gcol[:], subln.rearrange("o p -> p o"), allow_slow_non_contiguous=True).then_inc(consts_in, 16)
            for k in range(KD):
                if k >= 2:
                    sp.wait_ge(w_lo_done, k - 1)
                sp.dma_start(w[:, k % 2], weights[k * P:(k + 1) * P, :]).then_inc(w_in[k % 2], 16)
            with sp.Fori(0, G) as g:
                for k in range(KD):
                    sp.wait_ge(gated_done, g * KD + max(k - 1, 0))
                    sp.sem_inc(idle_sp, 1)
                    for dram, buf in ((o_dram, o), (gate_dram, gate)):
                        sp.dma_start(buf[:, k % 2], dram[k * P:(k + 1) * P, ds(g * 512, 512)]).then_inc(o_in[k % 2], 16)
                sp.wait_ge(added, g * 4)
                sp.sem_inc(idle_sp, 1)
                for j in range(4):
                    sp.dma_start(x[:, j], x_dram[ds(g * 512 + j * P, P), :]).then_inc(x_in, 16)
                for j in range(4):
                    sp.wait_ge(added, g * 4 + j + 1)
                    sp.sem_inc(idle_sp, 1)
                    sp.dma_start(dst[ds(g * 512 + j * P, P), :], out[:, j % 2]).then_inc(stored[j % 2], 16)
            for u in range(2):
                sp.wait_ge(stored[u], G * 2 * 16)

        @block.gpsimd
        def _(pool):
            for k in range(KD):
                pool.wait_ge(w_in[k % 2], 16 * (k // 2 + 1))
                nc.gpsimd.tensor_copy(w_hi[:, k], w[:, k % 2]).then_inc(w_hi_done, 1)
                pool.wait_ge(w_hi_done, k + 1)
                nc.gpsimd.tensor_tensor(w_lo[:, k], w[:, k % 2], w_hi[:, k], ALU.subtract).then_inc(w_lo_done, 1)

        @block.tensor
        def _(pe):
            with pe.Fori(0, G) as g:
                def turn(k):
                    pe.wait_ge(scaled_done, g * KD + max(k - 1, 0))
                    for j in range(4):
                        m = nc.tensor.transpose(inv_ps[:, k % 2, j * P:(j + 1) * P], inv_wide[:, j, k * P:(k + 1) * P], ident[:])
                    m.then_inc(turned, 1)
                pe.wait_ge(widened, g * 4 + 4)
                for k in range(KD):
                    turn(k)
                    if M == 2:
                        if k == 0:
                            pe.wait_ge(gcol_done, 2)
                        pe.wait_ge(h_sq, g * KD + k + 1)
                        pe.wait_ge(h_mean, g * KD + k)
                        nc.tensor.matmul(head_ps[:], ones[:], hsq[:], start=True, stop=True).then_inc(h_sum, 1)
                for j in range(4):
                    pe.wait_ge(normed, g * 4 + max(j - 1, 0))
                    for n in range(2):
                        terms = [(a, b, k) for k in range(KD) for a, b in ((og_hi, w_hi), (og_lo, w_hi), (og_hi, w_lo))]
                        for i, (a, b, k) in enumerate(terms):
                            if j == 0 and n == 0 and i % 3 == 0:
                                pe.wait_ge(og_lo_done, g * KD + k + 1)
                                pe.wait_ge(w_lo_done, k + 1)
                            m = nc.tensor.matmul(y_ps[:, j % 2, n], a[:, k, j * P:(j + 1) * P], b[:, k, n * 512:(n + 1) * 512],
                                                 start=(i == 0), stop=(i == len(terms) - 1))
                    m.then_inc(y_done, 1)

        @block.scalar
        def _(act):
            with act.Fori(0, G) as g:
                for k in range(KD):
                    if M == 2:
                        act.wait_ge(scaled_done, g * KD + k + 1)
                        act.wait_ge(h_sum, g * KD + k)
                        nc.scalar.activation(hsq[:], scaled[:, k % 2], ACT.Square).then_inc(h_sq, 1)
                        act.wait_ge(h_mean, g * KD + k + 1)
                        act.wait_ge(h_inv, g * KD + k)
                        nc.scalar.activation(hsd[:], hms[:], ACT.Sqrt).then_inc(h_root, 1)
                    act.wait_ge(gated_done, g * KD + k + 1)
                    act.wait_ge(y_done, g * 4)
                    nc.scalar.activation(og_hi[:, k], gated[:, k % 2], ACT.Copy).then_inc(og_hi_done, 1)
                for j in range(4):
                    act.wait_ge(y_done, g * 4 + j + 1)
                    act.wait_ge(ysq_done, g * 4 + j)
                    act.wait_ge(rs_done, g * 4)
                    nc.scalar.activation(ysq[:], flat(y_ps[:, j % 2]), ACT.Square, accum_out=ss[:, j:j + 1]).then_inc(ysq_done, 1)
                    act.wait_ge(meaned, g * 4 + j + 1)
                    nc.scalar.activation(sd[:, j:j + 1], ms[:, j:j + 1], ACT.Sqrt).then_inc(rooted, 1)

        @block.vector
        def _(dve):
            dve.wait_ge(consts_in, 16 * M)
            if M == 2:
                nc.vector.memset(ones[:], 1.0 / P).then_inc(gcol_done, 1)
                nc.vector.tensor_scalar(gcol[:], gcol[:], 1.0 - LAMBDA_INIT, None, ALU.mult).then_inc(gcol_done, 1)
                dve.wait_ge(gcol_done, 2)
            with dve.Fori(0, G) as g:
                dve.wait_ge(widened, g * 4)
                for j in range(4):
                    l1 = sums.rearrange("p b (h m) -> p b h m", m=M)[:, ds(g * 4 + j, 1), :, 0].rearrange("p o h -> p (o h)")
                    nc.vector.reciprocal(inv[:, j], l1).then_inc(inverted, 1)
                dve.wait_ge(inverted, g * 4 + 4)
                dve.wait_ge(turned, g * KD)
                for j in range(4):
                    nc.vector.tensor_copy(inv_wide[:, j].rearrange("p (h e) -> p h e", h=heads),
                                          inv[:, j].unsqueeze(2).to_broadcast([P, heads, D // heads])).then_inc(widened, 1)
                for k in range(KD):
                    u = k % 2
                    dve.wait_ge(o_in[u], g * 128 + (k // 2 + 1) * 32)
                    dve.wait_ge(turned, g * KD + k + 1)
                    if M == 2:
                        dve.wait_ge(h_sq, g * KD + max(k - 1, 0))
                    dve.wait_ge(gated_done, g * KD + max(k - 1, 0) if k else g * KD)
                    nc.vector.tensor_tensor(scaled[:, u], inv_ps[:, u], o[:, u], ALU.mult).then_inc(scaled_done, 1)
                    dve.wait_ge(scaled_done, g * KD + k + 1)
                    src = scaled[:, u]
                    if M == 2:
                        dve.wait_ge(h_sum, g * KD + k + 1)
                        dve.wait_ge(h_root, g * KD + k)
                        nc.vector.tensor_scalar(hms[:], head_ps[:], EPS, None, ALU.add).then_inc(h_mean, 1)
                        dve.wait_ge(h_root, g * KD + k + 1)
                        dve.wait_ge(h_norm, g * KD + k)
                        nc.vector.reciprocal(hrs[:], hsd[:]).then_inc(h_inv, 1)
                        dve.wait_ge(h_inv, g * KD + k + 1)
                        dve.wait_ge(gated_done, g * KD + k)
                        nc.vector.scalar_tensor_tensor(hn[:], scaled[:, u], gcol[:], hrs[:], ALU.mult, ALU.mult).then_inc(h_norm, 1)
                        dve.wait_ge(h_norm, g * KD + k + 1)
                        src = hn[:]
                    dve.wait_ge(og_lo_done, g * KD + max(k - 1, 0) if k else g * KD)
                    nc.vector.tensor_tensor(gated[:, u], src, gate[:, u], ALU.mult).then_inc(gated_done, 1)
                    dve.wait_ge(og_hi_done, g * KD + k + 1)
                    nc.vector.tensor_tensor(og_lo[:, k], gated[:, u], og_hi[:, k], ALU.subtract).then_inc(og_lo_done, 1)
                dve.wait_ge(x_in, g * 64 + 64)
                for j in range(4):
                    dve.wait_ge(ysq_done, g * 4 + j + 1)
                    dve.wait_ge(rooted, g * 4 + j)
                    nc.vector.tensor_scalar(ms[:, j:j + 1], ss[:, j:j + 1], 1.0 / D, EPS, ALU.mult, ALU.add).then_inc(meaned, 1)
                    dve.wait_ge(rooted, g * 4 + j + 1)
                    dve.wait_ge(normed, g * 4 + j)
                    nc.vector.reciprocal(rs[:, j:j + 1], sd[:, j:j + 1]).then_inc(rs_done, 1)
                    dve.wait_ge(rs_done, g * 4 + j + 1)
                    dve.wait_ge(added, g * 4 + max(j - 1, 0))
                    nc.vector.scalar_tensor_tensor(z[:, j % 2], flat(y_ps[:, j % 2]), rs[:, j:j + 1], gp[:], ALU.mult, ALU.mult).then_inc(normed, 1)
                    dve.wait_ge(normed, g * 4 + j + 1)
                    dve.wait_ge(stored[j % 2], g * 32 + (j // 2) * 16)
                    nc.vector.tensor_tensor(out[:, j % 2], z[:, j % 2], x[:, j], ALU.add).then_inc(added, 1)


def stage_identity(nc, sems, ident):
    with Stage(nc, sems, "identity") as st:
        made = st.sem("made")
        block = st.block()

        @block.gpsimd
        def _(pool):
            nc.gpsimd.memset(ident[:], 0.0).then_inc(made, 1)
            pool.wait_ge(made, 1)
            nc.gpsimd.affine_select(out=ident[:], in_=ident[:], compare_op=ALU.not_equal, fill=1.0, base=0,
                                    pattern=[[-1, P]], channel_multiplier=1).then_inc(made, 1)
            pool.wait_ge(made, 2)


def program(nc, ins, out):
    scratch = lambda name, shape: nc.dram_tensor(f"scratch_{name}", shape, F32).ap()
    gp_dram, bias_dram = scratch("gp", (2, P, D)), scratch("bias", (NMAPS, P, 384))
    qT, kT, v = scratch("qT", (2, D, T)), scratch("kT", (2, D, T)), scratch("v", (2, T, D))
    gateT, oT, x1 = scratch("gateT", (D, T)), scratch("oT", (D, T)), scratch("x1", (T, D))
    cqT, ckvT, kidxT, qidx = scratch("cqT", (2, QR, T)), scratch("ckvT", (2, KVR, T)), scratch("kidxT", (2, ID, T)), scratch("qidx", (2, IH * ID, T))
    sems = Semaphores(nc)
    with ExitStack() as keep:
        sb = lambda ctx, name, shape, dt: ctx.enter_context(nc.sbuf_tensor(name, shape, dt))
        ident, ada, neglam = sb(keep, "ident", [P, P], F32), sb(keep, "ada", [P, 2, 2, KD], F32), sb(keep, "neglam", [P, 1], F32)
        sums, widx = sb(keep, "sums", [P, NB, NMAPS], F32), sb(keep, "widx", [P, NB, IH], F32)
        stage_identity(nc, sems, ident)
        stage_modulation(nc, sems, ins, ada, neglam, gp_dram, bias_dram)

        with ExitStack() as c:
            hT = [sb(c, f"a_{n}", [P, KD, T], F32R) for n in ("hT_hi", "hT_lo")]
            stage_input(nc, sems, "a_in", ins["x"][0], ada, 0, ident, hT)
            win = ins["a_w_in"][0].rearrange("(k p) n -> p k n", p=P)
            stage_project_T(nc, sems, "a_gate", hT, KD, [(lambda b: win[:, :, ds(b * P + SMALL, P)], KD, 1.0, gateT, None)])
            stage_narrow(nc, sems, ins, hT, ident, widx, cqT, ckvT, kidxT)
        with ExitStack() as c:
            cq = [sb(c, f"cq_{n}", [P, 2, T], F32R) for n in ("hi", "lo")]
            ckv = [sb(c, f"ckv_{n}", [P, 1, T], F32R) for n in ("hi", "lo")]
            loaded = sems.new("latents_loaded")
            with nc.Block() as block:
                @block.sync
                def _(sp):
                    for part in range(2):
                        sp.dma_start(cq[part].bitcast(F32)[:], cqT[part].rearrange("(k p) t -> p k t", p=P)).then_inc(loaded, 16)
                        sp.dma_start(ckv[part].bitcast(F32)[:, 0], ckvT[part]).then_inc(loaded, 16)
                    sp.wait_ge(loaded, 64)
            wq, wqi = (ins[n][0].rearrange("(k p) n -> p k n", p=P) for n in ("a_w_uq", "a_w_qidx"))
            wk = ins["a_w_uk"][0].rearrange("h r d -> r h d")
            wv = ins["a_w_uv"][0].rearrange("h r d -> r h d")
            stage_project_T(nc, sems, "a_q", cq, 2, [(lambda b: wq[:, :, ds(b * P, P)], 8, HD ** -0.5, qT[0], qT[1]),
                                                     (lambda b: wqi[:, :, ds(b * P, P)], 4, 1.0, qidx[0], qidx[1])])
            stage_project_T(nc, sems, "a_k", ckv, 1, [(lambda b: wk[:, ds(b * 2, 2), :], 8, 1.0, kT[0], kT[1])])
            stage_project_v(nc, sems, "a_v", ckv, 1, lambda n: wv[:, ds(n * 8, 8), :], v[0], v[1])
        sems.retire()
        with ExitStack() as c:
            mask = sb(c, "mask", [P, KEYS], BF16)
            stage_select(nc, sems, widx, qidx, kidxT, mask)
            stage_attention(nc, sems, "a_att", 16, 1, ident, bias_dram, qT, kT, v, oT, sums, mask=mask)
        stage_output(nc, sems, "a_out", 1, ins["x"][0], x1, ins["a_w_out"][0], oT, gateT, gp_dram[0], sums, ident)

        sems.retire()

        with ExitStack() as c:
            hT = [sb(c, f"b_{n}", [P, KD, T], F32R) for n in ("hT_hi", "hT_lo")]
            stage_input(nc, sems, "b_in", x1, ada, 1, ident, hT)
            win = ins["b_w_in"][0].rearrange("(k p) n -> p k n", p=P)
            stage_project_T(nc, sems, "b_qkg", hT, KD, [(lambda b: win[:, :, ds(b * P, P)], KD, HD ** -0.5, qT[0], qT[1]),
                                                        (lambda b: win[:, :, ds(b * P + D, P)], KD, 1.0, kT[0], kT[1]),
                                                        (lambda b: win[:, :, ds(b * P + 3 * D, P)], KD, 1.0, gateT, None)])
            stage_project_v(nc, sems, "b_v", hT, KD, lambda n: win[:, :, ds(n * 512 + 2 * D, 512)], v[0], v[1])
        stage_attention(nc, sems, "b_att", 8, 2, ident, bias_dram, qT, kT, v, oT, sums, neglam=neglam)
        stage_output(nc, sems, "b_out", 2, x1, out, ins["b_w_out"][0], oT, gateT, gp_dram[1], sums, ident, subln=ins["b_subln"])


_INS = ["x", "c", "rel_bias", "mod_w", "mod_b", "pre_g", "post_g", "a_w_in", "a_q_norm", "a_kv_norm", "a_kidx_norm", "a_w_uq",
        "a_w_qidx", "a_w_uk", "a_w_uv", "a_w_out", "b_w_in", "b_lam_q1", "b_lam_k1", "b_lam_q2", "b_lam_k2", "b_subln", "b_w_out"]


def kernel(**inputs):
    import concourse.bacc as bacc
    from concourse.bass_utils import run_bass_kernel_spmd

    nc = bacc.Bacc("TRN2", target_bir_lowering=False, num_devices=1)
    arrays = {name: np.ascontiguousarray(inputs[name]) for name in _INS}
    arrays["onehot"] = bucket_onehot()
    ins = {name: nc.dram_tensor(f"in_{name}", a.shape, mybir.dt.from_np(a.dtype), kind="ExternalInput").ap() for name, a in arrays.items()}
    out = nc.dram_tensor("out_dram", (1, T, D), F32, kind="ExternalOutput").ap()
    program(nc, ins, out[0])
    r = run_bass_kernel_spmd(nc, [{f"in_{name}": a for name, a in arrays.items()}], core_ids=[0])
    return r.results[0]["out_dram"]
```

```python
import math
from contextlib import ExitStack

import concourse.bass as bass
import numpy as np
from concourse import mybir

F32 = mybir.dt.float32
F32R = mybir.dt.float32r
BF16 = mybir.dt.bfloat16
U16 = mybir.dt.uint16
I32 = mybir.dt.int32
ALU = mybir.AluOpType
ACT = mybir.ActivationFunctionType
AX = mybir.AxisListType
ds = bass.ds

P = 128
T = 2048
D = 1024
KD = D // P
NB = T // P
G = 4
GT = T // G
EPS = 1e-6
NBUCKETS, MAXDIST, NMAPS = 32, 128, 16
NEG = -1.0e30
LOWEST = -3.0e38
QR, KVR, ID, IH = D // 4, D // 8, 64, 8
SMALL = QR + KVR + ID + IH
TOPK = 256
HD = 64
LAMBDA_INIT = 0.8 - 0.6 * math.exp(-0.3)
NEAR = 2 * P


def bucket_onehot():
    n = np.maximum(255 - np.arange(384), 0)
    nf = np.maximum(n, 1).astype(np.float32)
    half = NBUCKETS // 2
    large = half + (np.log(nf / np.float32(half)) / np.float32(math.log(MAXDIST / half))
                    * np.float32(NBUCKETS - half)).astype(np.int32)
    b = np.where(n < half, n, np.minimum(large, NBUCKETS - 1))
    return (np.arange(NBUCKETS)[:, None] == b[None, :]).astype(np.float32)


def flat(ap):
    return ap.rearrange("p a b -> p (a b)")


class Semaphores:

    def __init__(self, nc):
        self.nc, self.held = nc, []

    def new(self, name):
        self.held.append(self.nc.alloc_semaphore(name=name))
        return self.held[-1]

    def retire(self):
        self.nc.clear_and_free_semaphores(self.held)
        self.nc.all_engine_barrier()
        self.held = []


class Stage:

    def __init__(self, nc, sems, name):
        self.nc, self.sems, self.name, self.ctx, self.own = nc, sems, name, ExitStack(), []

    def __enter__(self):
        return self

    def __exit__(self, *a):
        return self.ctx.__exit__(*a)

    def sb(self, name, shape, dt):
        return self.ctx.enter_context(self.nc.sbuf_tensor(f"{self.name}_sb_{name}", shape, dt))

    def ps(self, name, shape, dt=F32):
        return self.ctx.enter_context(self.nc.psum_tensor(f"{self.name}_ps_{name}", shape, dt))

    def sem(self, name):
        self.own.append(self.sems.new(f"{self.name}_sem_{name}"))
        return self.own[-1]

    def start_at_one(self, engine):
        for s in self.own:
            engine.sem_inc(s, 1)

    def block(self):
        return self.ctx.enter_context(self.nc.Block())


def stage_modulation(nc, sems, ins, ada, neglam, gp_dram, bias_dram):
    with Stage(nc, sems, "mod") as st:
        w = st.sb("w", [P, 2, KD, D], F32)
        c = st.sb("c", [P, KD], F32)
        cact = st.sb("cact", [P, KD], F32)
        cwide = st.sb("cwide", [P, KD, P], F32)
        bcol = st.sb("bcol", [P, 2, 3 * KD], F32)
        preg = st.sb("preg", [P, 2, KD], F32)
        postg = st.sb("postg", [P, 2, D], F32)
        bgate = st.sb("bgate", [P, 2, D], F32)
        scale = st.sb("scale", [P, 2, KD], F32)
        gate = st.sb("gate", [P, 2, D], F32)
        gp = st.sb("gp", [P, 2, D], F32)
        relb = st.sb("relb", [NBUCKETS, NMAPS], F32)
        onehot = st.sb("onehot", [NBUCKETS, 384], F32)
        far = st.sb("far", [NMAPS, 1], F32)
        bvec = st.sb("bvec", [NMAPS, 384], F32)
        lams = st.sb("lams", [P, 4, HD], F32)
        lprod = st.sb("lprod", [P, 2, HD], F32)
        ldot = st.sb("ldot", [P, 2], F32)
        lexp = st.sb("lexp", [P, 2], F32)
        pcol = st.ps("pcol", [P, 2, 512])
        pgate = st.ps("pgate", [P, 2, 512])
        pbias = st.ps("pbias", [P, 512])
        small_in, w_in = st.sem("small_in"), [st.sem("w_in0"), st.sem("w_in1")]
        c_ready, cwide_ready, w_used, evacuated = (st.sem(x) for x in ("c_ready", "cwide_ready", "w_used", "evacuated"))
        bias_mm, bias_done, gate_step, stored, lam_dot, lam_exp, self_dve = (
            st.sem(x) for x in ("bias_mm", "bias_done", "gate_step", "stored", "lam_dot", "lam_exp", "self_dve"))
        block = st.block()

        @block.sync
        def _(sp):
            x = ins
            sp.dma_start(c[:], x["c"].rearrange("b (k p) -> p (b k)", p=P), allow_slow_non_contiguous=True).then_inc(small_in, 16)
            sp.dma_start(bcol[:], x["mod_b"].rearrange("l (k p) -> p l k", p=P), allow_slow_non_contiguous=True).then_inc(small_in, 16)
            sp.dma_start(preg[:], x["pre_g"].rearrange("l (k p) -> p l k", p=P), allow_slow_non_contiguous=True).then_inc(small_in, 16)
            for q in range(6):
                l, third = divmod(q, 3)
                if q >= 2:
                    sp.wait_ge(w_used, q - 1)
                sp.dma_start(w[:, q % 2], x["mod_w"][l].rearrange("(k p) n -> p k n", p=P)[:, :, third * D:(third + 1) * D]
                             ).then_inc(w_in[q % 2], 16)
                if q == 0:
                    sp.dma_start(postg[:], x["post_g"].rearrange("l n -> (l n)").partition_broadcast(P).rearrange("p (l n) -> p l n", l=2)).then_inc(small_in, 16)
                    for l in range(2):
                        sp.dma_start(bgate[:, l], x["mod_b"][l, 2 * D:3 * D].partition_broadcast(P)).then_inc(small_in, 16)
                    sp.dma_start(relb[:], x["rel_bias"]).then_inc(small_in, 16)
                    sp.dma_start(onehot[:], x["onehot"]).then_inc(small_in, 16)
                    for j, name in enumerate(("b_lam_q1", "b_lam_k1", "b_lam_q2", "b_lam_k2")):
                        sp.dma_start(lams[:, j], x[name][0].partition_broadcast(P)).then_inc(small_in, 16)
            sp.wait_ge(bias_done, 1)
            sp.dma_start(bias_dram, bvec[:].unsqueeze(1).to_broadcast([NMAPS, P, 384])).then_inc(stored, 16)
            for l in range(2):
                sp.wait_ge(gate_step, l + 1)
                sp.dma_start(gp_dram[l], gp[:, l]).then_inc(stored, 16)
            sp.wait_ge(stored, 48)

        ALL_SMALL = 16 * 12

        @block.scalar
        def _(act):
            act.wait_ge(small_in, ALL_SMALL)
            nc.scalar.activation(cact[:], c[:], ACT.Silu).then_inc(c_ready, 1)
            act.wait_ge(lam_dot, 2)
            nc.scalar.activation(lexp[:], ldot[:], ACT.Exp).then_inc(lam_exp, 1)

        @block.tensor
        def _(pe):
            pe.wait_ge(small_in, ALL_SMALL)
            nc.tensor.matmul(pbias[0:NMAPS, 0:384], relb[:], onehot[:], start=True, stop=True).then_inc(bias_mm, 1)
            pe.wait_ge(c_ready, 1)
            pe.wait_ge(cwide_ready, 1)
            for q in range(6):
                l, third = divmod(q, 3)
                pe.wait_ge(w_in[q % 2], 16 * (q // 2 + 1))
                if l == 1:
                    pe.wait_ge(evacuated, third + 1)
                if third < 2:
                    for f in range(KD):
                        for k in range(KD):
                            m = nc.tensor.matmul(pcol[:, third, f:f + 1], w[:, q % 2, k, f * P:(f + 1) * P],
                                                 cact[:, k:k + 1], start=(k == 0), stop=(k == KD - 1))
                else:
                    for n in range(2):
                        for k in range(KD):
                            m = nc.tensor.matmul(pgate[:, n, :], cwide[:, k, :], w[:, q % 2, k, n * 512:(n + 1) * 512],
                                                 start=(k == 0), stop=(k == KD - 1))
                m.then_inc(w_used, 1)

        @block.vector
        def _(dve):
            dve.wait_ge(small_in, ALL_SMALL)
            for j in range(2):
                nc.vector.tensor_tensor(lprod[:, j], lams[:, 2 * j], lams[:, 2 * j + 1], ALU.mult).then_inc(self_dve, 1)
            dve.wait_ge(self_dve, 2)
            for j in range(2):
                nc.vector.tensor_reduce(ldot[:, j:j + 1], lprod[:, j], AX.X, ALU.add).then_inc(lam_dot, 1)
            dve.wait_ge(bias_mm, 1)
            nc.vector.tensor_copy(far[:], pbias[0:NMAPS, 0:1]).then_inc(self_dve, 1)
            dve.wait_ge(self_dve, 3)
            nc.vector.tensor_scalar(bvec[:], pbias[0:NMAPS, 0:384], far[:], None, ALU.subtract).then_inc(self_dve, 1)
            dve.wait_ge(self_dve, 4)
            nc.vector.memset(bvec[:, 256:384], NEG).then_inc(bias_done, 1)
            dve.wait_ge(c_ready, 1)
            nc.vector.tensor_copy(cwide[:], cact[:].unsqueeze(2).to_broadcast([P, KD, P])).then_inc(cwide_ready, 1)
            dve.wait_ge(lam_exp, 1)
            nc.vector.tensor_scalar(neglam[:], lexp[:, 1:2], lexp[:, 0:1], -LAMBDA_INIT, ALU.subtract, ALU.add).then_inc(self_dve, 1)
            for q in range(6):
                l, third = divmod(q, 3)
                dve.wait_ge(w_used, q + 1)
                if third == 0:
                    nc.vector.tensor_tensor(ada[:, l, 1], pcol[:, 0, 0:KD], bcol[:, l, 0:KD], ALU.add).then_inc(evacuated, 1)
                elif third == 1:
                    nc.vector.tensor_tensor(scale[:, l], pcol[:, 1, 0:KD], bcol[:, l, KD:2 * KD], ALU.add).then_inc(evacuated, 1)
                    dve.wait_ge(evacuated, q + 1)
                    nc.vector.scalar_tensor_tensor(ada[:, l, 0], scale[:, l], 1.0, preg[:, l], ALU.add, ALU.mult).then_inc(self_dve, 1)
                else:
                    nc.vector.tensor_tensor(gate[:, l], flat(pgate[:]), bgate[:, l], ALU.add).then_inc(evacuated, 1)
                    dve.wait_ge(evacuated, q + 1)
                    nc.vector.tensor_tensor(gp[:, l], gate[:, l], postg[:, l], ALU.mult).then_inc(gate_step, 1)


def stage_input(nc, sems, name, x_dram, ada, layer, ident, hT):
    hT_hi, hT_lo = hT
    with Stage(nc, sems, name) as st:
        x = st.sb("x", [P, 4, D], F32)
        xn = st.sb("xn", [P, 4, D], F32)
        sq = st.sb("sq", [P, 4, D], BF16)
        h = st.sb("h", [P, 2, 512], F32)
        ss, ms, sd, rs = (st.sb(n, [P, 4], F32) for n in ("ss", "ms", "sd", "rs"))
        pt = st.ps("pt", [P, KD, 512])
        x_in = [st.sem(f"x_in{j}") for j in range(4)]
        squared, meaned, rooted, inverted, normed, turned, scaled, split_hi, split_lo = (
            st.sem(n) for n in ("squared", "meaned", "rooted", "inverted", "normed", "turned", "scaled", "split_hi", "split_lo"))
        idle_sp = st.sem("idle_sp")
        block = st.block()

        @block.sync
        def _(sp):
            with sp.Fori(0, G) as g:
                for j in range(4):
                    sp.wait_ge(normed, 1 + g * 4)
                    sp.sem_inc(idle_sp, 1)
                    sp.dma_start(x[:, j], x_dram[ds(g * 512 + j * P, P), :]).then_inc(x_in[j], 16)

        @block.gpsimd
        def _(pool):
            st.start_at_one(pool)

        @block.scalar
        def _(act):
            with act.Fori(0, G) as g:
                for j in range(4):
                    act.wait_ge(x_in[j], 1 + g * 16 + 16)
                    act.wait_ge(meaned, 1 + g * 4)
                    nc.scalar.activation(sq[:, j], x[:, j], ACT.Square, accum_out=ss[:, j:j + 1]).then_inc(squared, 1)
                act.wait_ge(meaned, 1 + g * 4 + 4)
                act.wait_ge(inverted, 1 + g)
                nc.scalar.activation(sd[:], ms[:], ACT.Sqrt).then_inc(rooted, 1)
                for k in range(KD):
                    act.wait_ge(turned, 1 + g * KD + k + 1)
                    act.wait_ge(split_lo, 1 + g * KD + (k - 1 if k else 0))
                    nc.scalar.activation(h[:, k % 2], pt[:, k], ACT.Identity, scale=ada[:, layer, 0, k:k + 1],
                                         bias=ada[:, layer, 1, k:k + 1]).then_inc(scaled, 1)

        @block.tensor
        def _(pe):
            with pe.Fori(0, G) as g:
                pe.wait_ge(normed, 1 + g * 4 + 4)
                for k in range(KD):
                    pe.wait_ge(scaled, 1 + g * KD)
                    for j in range(4):
                        m = nc.tensor.transpose(pt[:, k, j * P:(j + 1) * P], xn[:, j, k * P:(k + 1) * P], ident[:])
                    m.then_inc(turned, 1)

        @block.vector
        def _(dve):
            with dve.Fori(0, G) as g:
                dve.wait_ge(squared, 1 + g * 4 + 4)
                dve.wait_ge(rooted, 1 + g)
                nc.vector.tensor_scalar(ms[:], ss[:], 1.0 / D, EPS, ALU.mult, ALU.add).then_inc(meaned, 4)
                dve.wait_ge(rooted, 1 + g + 1)
                dve.wait_ge(normed, 1 + g * 4)
                nc.vector.reciprocal(rs[:], sd[:]).then_inc(inverted, 1)
                dve.wait_ge(inverted, 1 + g + 1)
                dve.wait_ge(turned, 1 + g * KD)
                for j in range(4):
                    nc.vector.tensor_scalar(xn[:, j], x[:, j], rs[:, j:j + 1], None, ALU.mult).then_inc(normed, 1)
                for k in range(KD):
                    dve.wait_ge(scaled, 1 + g * KD + k + 1)
                    nc.vector.tensor_copy(hT_hi[:, k, ds(g * 512, 512)], h[:, k % 2]).then_inc(split_hi, 1)
                    dve.wait_ge(split_hi, 1 + g * KD + k + 1)
                    nc.vector.tensor_tensor(hT_lo[:, k, ds(g * 512, 512)], h[:, k % 2], hT_hi[:, k, ds(g * 512, 512)],
                                            ALU.subtract).then_inc(split_lo, 1)


def stage_project_T(nc, sems, name, xT, KB, jobs):
    xT_hi, xT_lo = xT
    with Stage(nc, sems, name) as st:
        w, w_hi, w_lo = (st.sb(n, [P, 2, KB, P], t) for n, t in (("w", F32), ("w_hi", F32R), ("w_lo", F32R)))
        any_split = any(j[4] is not None for j in jobs)
        o_plain = st.sb("o_plain", [P, 2, T], F32) if not all(j[4] is not None for j in jobs) else None
        o_hi = st.sb("o_hi", [P, 2, T], F32R) if any_split else None
        o_lo = st.sb("o_lo", [P, 2, T], F32R) if any_split else None
        acc = st.ps("acc", [P, 2, G, 512])
        idle_sp, idle_pool = st.sem("idle_sp"), st.sem("idle_pool")
        for n_job, (weights, blocks, scale, hi_dram, lo_dram) in enumerate(jobs):
            s = [st.sem(f"{n}{n_job}") for n in ("w_in0", "w_in1", "w_hi_done", "w_lo_done", "summed", "left_hi", "left_lo", "stored0", "stored1")]
            w_in, w_hi_done, w_lo_done, summed, left_hi, left_lo, stored = s[0:2], s[2], s[3], s[4], s[5], s[6], s[7:9]
            split = lo_dram is not None
            pairs = blocks // 2
            left = left_lo if split else left_hi
            with nc.Block() as block:
                @block.sync
                def _(sp):
                    for u in range(2):
                        sp.dma_start(w[:, u], weights(u)).then_inc(w_in[u], 16)

                    def store(i, u):
                        sp.wait_ge(left, 1 + (i + 1) * 8 + 4 * u + 4)
                        sp.sem_inc(idle_sp, 1)
                        for dram, buf in ([(hi_dram, o_hi), (lo_dram, o_lo)] if split else [(hi_dram, o_plain)]):
                            src = buf[:, u].bitcast(F32) if split else buf[:, u]
                            sp.dma_start(dram[ds((i * 2 + u) * P, P), :], src).then_inc(stored[u], 16)
                    if pairs > 1:
                        with sp.Fori(0, pairs - 1) as i:
                            for u in range(2):
                                sp.wait_ge(w_lo_done, 1 + i * 2 + u + 1)
                                sp.sem_inc(idle_sp, 1)
                                sp.dma_start(w[:, u], weights(i * 2 + (2 + u))).then_inc(w_in[u], 16)
                                store(i, u)
                    for u in range(2):
                        store(pairs - 1, u)
                    for u in range(2):
                        sp.wait_ge(stored[u], 1 + pairs * (32 if split else 16))

                @block.gpsimd
                def _(pool):
                    for x in s:
                        pool.sem_inc(x, 1)
                    pool.sem_inc(summed, 8)
                    with pool.Fori(0, pairs) as i:
                        for u in range(2):
                            pool.wait_ge(w_in[u], 1 + i * 16 + 16)
                            pool.wait_ge(summed, 1 + i * 8 + 4 * u + 4)
                            pool.sem_inc(idle_pool, 1)
                            nc.gpsimd.tensor_copy(w_hi[:, u], w[:, u]).then_inc(w_hi_done, 1)
                            pool.wait_ge(w_hi_done, 1 + i * 2 + u + 1)
                            nc.gpsimd.tensor_tensor(w_lo[:, u], w[:, u], w_hi[:, u], ALU.subtract).then_inc(w_lo_done, 1)

                @block.tensor
                def _(pe):
                    pe.sem_inc(left, 8)
                    with pe.Fori(0, pairs) as i:
                        for u in range(2):
                            pe.wait_ge(w_lo_done, 1 + i * 2 + u + 1)
                            for g in range(G):
                                pe.wait_ge(left, 1 + i * 8 + 4 * u + g + 1)
                                terms = [(a, b, k) for a, b in ((w_hi, xT_hi), (w_lo, xT_hi), (w_hi, xT_lo)) for k in range(KB)]
                                for n, (a, b, k) in enumerate(terms):
                                    m = nc.tensor.matmul(acc[:, u, g], a[:, u, k], b[:, k, g * 512:(g + 1) * 512],
                                                         start=(n == 0), stop=(n == len(terms) - 1))
                                m.then_inc(summed, 1)

                @block.scalar
                def _(act):
                    with act.Fori(0, pairs) as i:
                        for u in range(2):
                            act.wait_ge(stored[u], 1 + i * (32 if split else 16))
                            for g in range(G):
                                act.wait_ge(summed, 1 + (i + 1) * 8 + 4 * u + g + 1)
                                if split:
                                    nc.scalar.activation(o_hi[:, u, g * 512:(g + 1) * 512], acc[:, u, g], ACT.Copy,
                                                         scale=scale).then_inc(left_hi, 1)
                                else:
                                    nc.scalar.activation(o_plain[:, u, g * 512:(g + 1) * 512], acc[:, u, g], ACT.Silu).then_inc(left_hi, 1)

                if split:
                    @block.vector
                    def _(dve):
                        with dve.Fori(0, pairs) as i:
                            for u in range(2):
                                for g in range(G):
                                    dve.wait_ge(left_hi, 1 + i * 8 + 4 * u + g + 1)
                                    nc.vector.scalar_tensor_tensor(o_lo[:, u, g * 512:(g + 1) * 512], acc[:, u, g], scale,
                                                                   o_hi[:, u, g * 512:(g + 1) * 512], ALU.mult, ALU.subtract).then_inc(left_lo, 1)


def stage_project_v(nc, sems, name, xT, KB, weights, hi_dram, lo_dram):
    xT_hi, xT_lo = xT
    with Stage(nc, sems, name) as st:
        w = st.sb("w", [P, KB, 512], F32)
        w_hi, w_lo = (st.sb(n, [P, KB, 512], F32R) for n in ("w_hi", "w_lo"))
        o_hi, o_lo = (st.sb(n, [P, 2, 512], F32R) for n in ("o_hi", "o_lo"))
        acc = st.ps("acc", [P, 4, 512])
        w_in, w_hi_done, w_lo_done, summed, left_hi, left_lo = (st.sem(n) for n in ("w_in", "w_hi_done", "w_lo_done", "summed", "left_hi", "left_lo"))
        stored = [st.sem("stored0"), st.sem("stored1")]
        idle_pool = st.sem("idle_pool")
        idle_sp = st.sem("idle_sp")
        block = st.block()

        @block.sync
        def _(sp):
            with sp.Fori(0, 2) as n:
                sp.wait_ge(w_lo_done, 1 + n)
                sp.sem_inc(idle_sp, 1)
                sp.dma_start(w[:], weights(n)).then_inc(w_in, 16)
                for tb in range(NB):
                    sp.wait_ge(left_lo, 1 + n * NB + tb + 1)
                    sp.sem_inc(idle_sp, 1)
                    for dram, buf in ((hi_dram, o_hi), (lo_dram, o_lo)):
                        sp.dma_start(dram[tb * P:(tb + 1) * P, ds(n * 512, 512)], buf[:, tb % 2].bitcast(F32)).then_inc(stored[tb % 2], 16)
            for u in range(2):
                sp.wait_ge(stored[u], 1 + 2 * (NB // 2) * 32)

        @block.gpsimd
        def _(pool):
            st.start_at_one(pool)
            with pool.Fori(0, 2) as n:
                pool.wait_ge(w_in, 1 + n * 16 + 16)
                pool.wait_ge(summed, 1 + n * NB)
                pool.sem_inc(idle_pool, 1)
                nc.gpsimd.tensor_copy(w_hi[:], w[:]).then_inc(w_hi_done, 1)
                pool.wait_ge(w_hi_done, 1 + n + 1)
                nc.gpsimd.tensor_tensor(w_lo[:], w[:], w_hi[:], ALU.subtract).then_inc(w_lo_done, 1)

        @block.tensor
        def _(pe):
            with pe.Fori(0, 2) as n:
                pe.wait_ge(w_lo_done, 1 + n + 1)
                for tb in range(NB):
                    pe.wait_ge(left_lo, 1 + n * NB + max(tb - 3, 0))
                    terms = [(a, b, k) for a, b in ((xT_hi, w_hi), (xT_lo, w_hi), (xT_hi, w_lo)) for k in range(KB)]
                    for j, (a, b, k) in enumerate(terms):
                        m = nc.tensor.matmul(acc[:, tb % 4], a[:, k, tb * P:(tb + 1) * P], b[:, k], start=(j == 0), stop=(j == len(terms) - 1))
                    m.then_inc(summed, 1)

        @block.scalar
        def _(act):
            with act.Fori(0, 2) as n:
                for tb in range(NB):
                    act.wait_ge(summed, 1 + n * NB + tb + 1)
                    act.wait_ge(stored[tb % 2], 1 + n * (NB // 2 * 32) + (tb // 2) * 32)
                    nc.scalar.activation(o_hi[:, tb % 2], acc[:, tb % 4], ACT.Copy).then_inc(left_hi, 1)

        @block.vector
        def _(dve):
            with dve.Fori(0, 2) as n:
                for tb in range(NB):
                    dve.wait_ge(left_hi, 1 + n * NB + tb + 1)
                    nc.vector.tensor_tensor(o_lo[:, tb % 2], acc[:, tb % 4], o_hi[:, tb % 2], ALU.subtract).then_inc(left_lo, 1)


def stage_narrow(nc, sems, ins, hT, ident, widx, cqT, ckvT, kidxT):
    hT_hi, hT_lo = hT
    with Stage(nc, sems, "narrow") as st:
        w = st.sb("w", [P, 2, SMALL], F32)
        w_hi, w_lo = (st.sb(n, [P, KD, SMALL], F32R) for n in ("w_hi", "w_lo"))
        sq = st.sb("sq", [P, QR], F32)
        norm = st.sb("norm", [P, 2, QR + KVR + ID], F32)
        gain = st.sb("gain", [P, 4], F32)
        inv_n = st.sb("inv_n", [P, 3], F32)
        ss, ms, mse, sd, rs = (st.sb(n, [P, 3], F32) for n in ("ss", "ms", "mse", "sd", "rs"))
        o_hi, o_lo = (st.sb(n, [P, 2, 4, P], F32R) for n in ("o_hi", "o_lo"))
        acc = st.ps("acc", [P, 2, 512])
        pt = st.ps("pt", [P, 2, 4, P])
        w_in = [st.sem("w_in0"), st.sem("w_in1")]
        gains_in, consts, w_hi_done, w_lo_done, summed, squared, rooted, inverted, normed, turned, left_hi, left_lo, chain = (
            st.sem(n) for n in ("gains_in", "consts", "w_hi_done", "w_lo_done", "summed", "squared", "rooted", "inverted", "normed",
                                "turned", "left_hi", "left_lo", "chain"))
        stored = [st.sem("stored0"), st.sem("stored1")]
        block = st.block()
        segs = [(0, QR), (QR, QR + KVR), (QR + KVR, QR + KVR + ID)]

        @block.sync
        def _(sp):
            win = ins["a_w_in"][0].rearrange("(k p) n -> k p n", p=P)
            for k in range(KD):
                if k >= 2:
                    sp.wait_ge(w_lo_done, k - 1)
                sp.dma_start(w[:, k % 2], win[k, :, 0:SMALL]).then_inc(w_in[k % 2], 16)
                if k == 1:
                    sp.dma_start(gain[:, 0:2], ins["a_q_norm"][0].rearrange("(k p) -> p k", p=P), allow_slow_non_contiguous=True).then_inc(gains_in, 16)
                    sp.dma_start(gain[:, 2:3], ins["a_kv_norm"].rearrange("o p -> p o"), allow_slow_non_contiguous=True).then_inc(gains_in, 16)
                    sp.dma_start(gain[0:ID, 3:4], ins["a_kidx_norm"].rearrange("o p -> p o"), allow_slow_non_contiguous=True).then_inc(gains_in, 16)
            for tb in range(NB):
                sp.wait_ge(left_lo, 6 * tb + 6)
                cols = slice(tb * P, (tb + 1) * P)
                for part, buf in ((0, o_hi), (1, o_lo)):
                    for j in range(2):
                        sp.dma_start(cqT[part, j * P:(j + 1) * P, cols], buf[:, tb % 2, j].bitcast(F32)).then_inc(stored[tb % 2], 16)
                    sp.dma_start(ckvT[part, :, cols], buf[:, tb % 2, 2].bitcast(F32)).then_inc(stored[tb % 2], 16)
                    sp.dma_start(kidxT[part, :, cols], buf[0:ID, tb % 2, 3].bitcast(F32)).then_inc(stored[tb % 2], 16)
            for u in range(2):
                sp.wait_ge(stored[u], NB // 2 * 128)

        @block.gpsimd
        def _(pool):
            for j, (a, b) in enumerate(segs):
                nc.gpsimd.memset(inv_n[:, j:j + 1], 1.0 / (b - a)).then_inc(consts, 1)
            for k in range(KD):
                pool.wait_ge(w_in[k % 2], 16 * (k // 2 + 1))
                nc.gpsimd.tensor_copy(w_hi[:, k], w[:, k % 2]).then_inc(w_hi_done, 1)
                pool.wait_ge(w_hi_done, k + 1)
                nc.gpsimd.tensor_tensor(w_lo[:, k], w[:, k % 2], w_hi[:, k], ALU.subtract).then_inc(w_lo_done, 1)

        @block.tensor
        def _(pe):
            def project(tb):
                if tb >= 2:
                    pe.wait_ge(normed, 4 * (tb - 1))
                terms = [(a, b, k) for k in range(KD) for a, b in ((hT_hi, w_hi), (hT_lo, w_hi), (hT_hi, w_lo))]
                for n, (a, b, k) in enumerate(terms):
                    if tb == 0 and n % 3 == 0:
                        pe.wait_ge(w_lo_done, k + 1)
                    m = nc.tensor.matmul(acc[:, tb % 2, 0:SMALL], a[:, k, tb * P:(tb + 1) * P], b[:, k],
                                         start=(n == 0), stop=(n == len(terms) - 1))
                m.then_inc(summed, 1)

            def turn(tb):
                pe.wait_ge(normed, 4 * tb + 4)
                if tb >= 2:
                    pe.wait_ge(left_lo, 6 * (tb - 1))
                for j in range(3):
                    nc.tensor.transpose(pt[:, tb % 2, j], norm[:, tb % 2, j * P:(j + 1) * P], ident[:])
                nc.tensor.transpose(pt[0:ID, tb % 2, 3], norm[:, tb % 2, 3 * P:3 * P + ID], ident[:]).then_inc(turned, 1)

            for tb in range(NB):
                project(tb)
                if tb:
                    turn(tb - 1)
            turn(NB - 1)

        parts = [(j, P if j < 3 else ID) for j in range(4)]

        @block.scalar
        def _(act):
            act.wait_ge(gains_in, 48)
            act.wait_ge(consts, 3)

            def leave(tb):
                act.wait_ge(turned, tb + 1)
                if tb >= 2:
                    act.wait_ge(stored[tb % 2], 128 * (tb // 2))
                for j, rows in parts:
                    nc.scalar.activation(o_hi[0:rows, tb % 2, j], pt[0:rows, tb % 2, j], ACT.Copy,
                                         scale=gain[0:rows, j:j + 1]).then_inc(left_hi, 1)

            for tb in range(NB):
                act.wait_ge(summed, tb + 1)
                if tb:
                    act.wait_ge(inverted, tb)
                for j, (a, b) in enumerate(segs):
                    if tb or j:
                        act.wait_ge(squared, 3 * tb + j)
                    nc.scalar.activation(sq[:, 0:b - a], acc[:, tb % 2, a:b], ACT.Square, accum_out=ss[:, j:j + 1]).then_inc(squared, 1)
                act.wait_ge(chain, 2 * tb + 2)
                nc.scalar.activation(sd[:], mse[:], ACT.Sqrt).then_inc(rooted, 1)
                if tb:
                    leave(tb - 1)
            leave(NB - 1)

        @block.vector
        def _(dve):
            dve.wait_ge(gains_in, 48)
            dve.wait_ge(consts, 3)

            def leave(tb):
                dve.wait_ge(left_hi, 4 * tb + 4)
                for j, rows in parts:
                    m = nc.vector.scalar_tensor_tensor(o_lo[0:rows, tb % 2, j], pt[0:rows, tb % 2, j], gain[0:rows, j:j + 1],
                                                       o_hi[0:rows, tb % 2, j], ALU.mult, ALU.subtract)
                    m.then_inc(left_lo, 3 if j == 3 else 1)

            for tb in range(NB):
                dve.wait_ge(squared, 3 * tb + 3)
                nc.vector.tensor_tensor(ms[:], ss[:], inv_n[:], ALU.mult).then_inc(chain, 1)
                dve.wait_ge(chain, 2 * tb + 1)
                nc.vector.tensor_scalar(mse[:], ms[:], EPS, None, ALU.add).then_inc(chain, 1)
                dve.wait_ge(rooted, tb + 1)
                if tb:
                    dve.wait_ge(normed, 4 * tb)
                nc.vector.reciprocal(rs[:], sd[:]).then_inc(inverted, 1)
                dve.wait_ge(inverted, tb + 1)
                if tb >= 2:
                    dve.wait_ge(turned, tb - 1)
                for j, (a, b) in enumerate(segs):
                    nc.vector.tensor_scalar(norm[:, tb % 2, a:b], acc[:, tb % 2, a:b], rs[:, j:j + 1], None, ALU.mult).then_inc(normed, 1)
                nc.vector.tensor_scalar(widx[:, tb], acc[:, tb % 2, SMALL - IH:SMALL], IH ** -0.5 * ID ** -0.5, None,
                                        ALU.mult).then_inc(normed, 1)
                if tb:
                    leave(tb - 1)
            leave(NB - 1)


def near_start(b):
    return max(b - 1, 0) * P


def mask_offset(b):
    return P * sum(i + 1 for i in range(2, b))


def chunks(b):
    n = (b + 1) * P
    return [(c, min(c + 512, n)) for c in range(0, n, 512)]


def quads(b):
    return [(j, min(j + 4, b + 1)) for j in range(0, b + 1, 4)]


SR, TR, OR = 2, 4, 2
LR, LR2 = 4, 2
LAG = 2
PAIR = 2 * P
PAIRS = [1, 3, 5, 7, 6, 4, 2, 0]
ORDER = [2 * r + i for r in PAIRS for i in range(2)]
NCH = [len(chunks(b)) for b in ORDER]
BEFORE = [sum(NCH[:p]) for p in range(NB + 1)]
NPVQ = [(2 * r + 5) // 4 for r in PAIRS]
PV_BEFORE = [sum(NPVQ[:r]) for r in range(len(PAIRS) + 1)]
LAST_PAIR = {4: 3, 5: 2, 6: 1, 7: 0}


def pieces(b, i):
    a, z = chunks(b)[i]
    ns = near_start(b)
    return ([(a, min(z, ns), False)] if a < ns else []) + ([(max(a, ns), z, True)] if z > ns else [])


def stage_attention(nc, sems, name, heads, M, ident, bias_dram, q_dram, k_dram, v_dram, o_dram, sums, mask=None, neglam=None):
    V2 = M == 1
    width = HD if V2 else P
    NCHUNK = M * BEFORE[NB]
    NQUAD = BEFORE[NB]
    NPV = PV_BEFORE[-1]
    NPAIR = len(PAIRS)
    PLACES = NB + LAG + 1
    SPLIT = [sum(1 for i in range(NCH[p]) if len(pieces(ORDER[p], i)) == 2) for p in range(NB)]
    NSPLIT = M * sum(SPLIT)
    assert NCHUNK % SR == 0 and NQUAD % TR == 0 and NB % LR == 0
    with_mask = lambda p: V2 and ORDER[p] >= 2
    NMASKED = [sum(with_mask(x) for x in range(p)) for p in range(NB + 1)]
    NM = 4

    with Stage(nc, sems, name) as st:
        q = st.sb("q", [P, 2, M, 2, PAIR], F32R)
        k = st.sb("k", [P, 2, M, T], F32R)
        v = st.sb("v", [P, 1 if V2 else 2, NB, P], F32R)
        near, near_next = (st.sb(n, [P, M, NEAR], F32) for n in ("near", "near_next"))
        near_mask = st.sb("near_mask", [P, NM, NEAR], F32) if V2 else None
        lg = st.sb("lg", [P, LR, T], F32)
        lg2 = st.sb("lg2", [P, LR2, T], F32) if M == 2 else None
        pT_hi, pT_lo = (st.sb(n, [P, 2, NB, PAIR], F32R) for n in ("pT_hi", "pT_lo"))
        o_sb = st.sb("o_sb", [P, OR, PAIR], F32)
        o_half = st.sb("o_half", [HD, OR, PAIR], F32) if V2 else None
        mx = st.sb("mx", [P, NB, M, 8], F32)
        negm = st.sb("negm", [P, NB, M], F32)
        rec, ratio = (st.sb(n, [P, NB], F32) if M == 2 else None for n in ("rec", "ratio"))
        s_ps, t_ps, o_ps = st.ps("s", [P, SR, 512]), st.ps("t", [P, TR, 4, P]), st.ps("o", [P, OR, 512])
        k_in, near_in, near_done, s_done, s_left, dve_chain, max_done, exp_done, mixed, mix_chain, turned, t_hi, t_lo, pv_quad, half_done, o_left, masked, mx_set = (
            st.sem(n) for n in ("k_in", "near_in", "near_done", "s_done", "s_left", "dve_chain", "max_done", "exp_done", "mixed", "mix_chain",
                                "turned", "t_hi", "t_lo", "pv_quad", "half_done", "o_left", "masked", "mx_set"))
        q_in, v_in, o_stored = ([st.sem(f"{n}{u}") for u in range(c)] for n, c in (("q_in", 2), ("v_in", 4), ("o_stored", 2)))
        idle_sp, idle_dve, idle_pool = st.sem("idle_sp"), st.sem("idle_dve"), st.sem("idle_pool")
        block = st.block()
        chunk_no = lambda p, i, m: M * (BEFORE[p] + i) + m
        values_here = lambda p: [(r, range(NPVQ[r] // 2) if p - LAG == 2 * r + 2 and r < NPAIR - 1 else range(NPVQ[r] // 2, NPVQ[r]) if r < NPAIR - 1
                                  else range(NPVQ[r])) for r in range(NPAIR)
                                 if p - LAG in ((2 * r + 2, 2 * r + 3) if r < NPAIR - 1 else (2 * r + 2,))]
        outputs_here = lambda p: [r for r in range(NPAIR) if p - LAG == 2 * r + 4]
        outputs_after = [r for r in range(NPAIR) if 2 * r + 4 + LAG >= PLACES]

        @block.sync
        def _(sp):
            def load_q(h, r):
                cols = slice(PAIRS[r] * PAIR, (PAIRS[r] + 1) * PAIR)
                for m in range(M):
                    rows = ds((h * M + m) * HD, HD)
                    sp.dma_start(q[:, r % 2, m, 0].bitcast(F32), q_dram[0:2, rows, cols]).then_inc(q_in[r % 2], 16)
                    for part in range(2):
                        sp.dma_start(q[(1 - part) * HD:(2 - part) * HD, r % 2, m, 1].bitcast(F32), q_dram[part, rows, cols]).then_inc(q_in[r % 2], 16)

            def load_k(h):
                for m in range(M):
                    dst = k[:, ds(h % 2, 1), m].rearrange("p o t -> p (o t)")
                    sp.dma_start(dst.bitcast(F32), k_dram[0:2, ds((h * M + m) * HD, HD), :]).then_inc(k_in, 16)

            def load_near(h):
                for m in range(M):
                    sp.dma_start(near_next[:, m], bass.AP(bias_dram.tensor, (h * M + m) * (P * 384) + P - 1, [[383, P], [1, NEAR]])).then_inc(near_in, 16)

            def load_v(h, c):
                for part in range(2):
                    dst = v[:, 0, 4 * c:4 * c + 4, part * HD:(part + 1) * HD] if V2 else v[:, part, 4 * c:4 * c + 4]
                    sp.dma_start(dst.bitcast(F32), v_dram[part, c * 512:(c + 1) * 512].rearrange("(j p) e -> p j e", p=P)[:, :, ds(h * width, width)]
                                 ).then_inc(v_in[c], 16)

            def store(h, r, last):
                sp.wait_ge(o_left, OR + h * NPAIR + r + 1)
                sp.sem_inc(idle_sp, 1)
                cols = slice(PAIRS[r] * PAIR, (PAIRS[r] + 1) * PAIR)
                sp.dma_start(o_dram[ds(h * width, width), cols], o_sb[0:width, r % 2]).then_inc(o_stored[r % 2], 16)
                if r in LAST_PAIR and not last:
                    load_v(h + 1, LAST_PAIR[r])

            def head(h, last):
                for r in range(NPAIR):
                    sp.wait_ge(s_done, h * NCHUNK + M * BEFORE[2 * r + 2])
                    sp.sem_inc(idle_sp, 1)
                    if r + 2 < NPAIR:
                        load_q(h, r + 2)
                    elif not last:
                        load_q(h + 1, r + 2 - NPAIR)
                    if r == 0:
                        if not last:
                            load_k(h + 1)
                        sp.wait_ge(near_done, h + 1)
                        sp.sem_inc(idle_sp, 1)
                        load_near(h if last else h + 1)
                    if r >= 3:
                        store(h, r - 3, last)
                for r in range(NPAIR - 3, NPAIR):
                    store(h, r, last)

            load_q(0, 0)
            load_k(0)
            load_near(0)
            load_q(0, 1)
            for c in range(4):
                load_v(0, c)
            with sp.Fori(0, heads - 1) as h:
                head(h, False)
            head(heads - 1, True)
            for u in range(2):
                sp.wait_ge(o_stored[u], 1 + heads * NPAIR // 2 * 16)
            sp.wait_ge(near_in, (heads + 1) * 16 * M)

        if V2:
            @block.gpsimd
            def _(pool):
                with pool.Fori(0, heads) as h:
                    pool.wait_ge(near_done, h + 1)
                    for p in range(NB):
                        if with_mask(p):
                            n, b = NMASKED[p], ORDER[p]
                            used = [x for x in range(p) if with_mask(x) and NMASKED[x] == n - NM]
                            if used:
                                pool.wait_ge(s_left, SR + h * NCHUNK + BEFORE[used[0] + 1])
                            pool.sem_inc(idle_pool, 1)
                            o = mask_offset(b) + near_start(b)
                            nc.gpsimd.tensor_tensor(near_mask[:, n % NM], near[:, 0], mask[:, o:o + NEAR], ALU.add).then_inc(masked, 1)

        @block.tensor
        def _(pe):
            pe.sem_inc(s_left, SR)
            pe.sem_inc(t_lo, TR)
            pe.sem_inc(o_left, OR)

            def logits(h, p, i):
                b, (a, z) = ORDER[p], chunks(ORDER[p])[i]
                for m in range(M):
                    n = chunk_no(p, i, m)
                    out, cols = s_ps[:, n % SR, 0:z - a], slice((b % 2) * P, (b % 2 + 1) * P)
                    keys = k[:, ds(h % 2, 1), m, a:z].rearrange("p o t -> p (o t)")
                    pe.wait_ge(s_left, h * NCHUNK + n + 1)
                    nc.tensor.matmul(out, q[:, p // 2 % 2, m, 0, cols], keys, start=True, stop=False)
                    nc.tensor.matmul(out, q[:, p // 2 % 2, m, 1, cols], keys, start=False, stop=True).then_inc(s_done, 1)

            def turn(h, p, i):
                n, (a, z) = BEFORE[p] + i, quads(ORDER[p])[i]
                if i == 0 and M == 2:
                    pe.wait_ge(mixed, LR2 + h * NB + p + 1)
                elif i == 0:
                    pe.wait_ge(exp_done, h * NB + p + 1)
                pe.wait_ge(t_lo, h * NQUAD + n + 1)
                for j in range(a, z):
                    x = nc.tensor.transpose(t_ps[:, n % TR, j - a], lg[:, p % LR, j * P:(j + 1) * P], ident[:])
                x.then_inc(turned, 1)

            def values(h, r, c):
                last = 2 * PAIRS[r] + 1
                if c == 0:
                    pe.wait_ge(o_left, h * NPAIR + r + 1)
                if r == c:
                    pe.wait_ge(v_in[c], h * 32 + 32)
                pe.wait_ge(t_lo, TR + h * NQUAD + BEFORE[2 * r + 1] + c + 1)
                terms = [(0, pT_hi), (0, pT_lo)] if V2 else [(0, pT_hi), (0, pT_lo), (1, pT_hi)]
                for j in range(4 * c, min(4 * c + 4, last + 1)):
                    a = P if j == last else 0
                    for i, (part, pT) in enumerate(terms):
                        x = nc.tensor.matmul(o_ps[:, r % 2, a:PAIR], v[:, part, j], pT[:, r % 2, j, a:PAIR],
                                             start=(j == 0 and i == 0), stop=(j == last and i == len(terms) - 1))
                x.then_inc(pv_quad, 1)

            with pe.Fori(0, heads) as h:
                pe.wait_ge(k_in, h * 16 * M + 16 * M)
                for p in range(PLACES):
                    if p < NB and p % 2 == 0:
                        pe.wait_ge(q_in[p // 2 % 2], h * (4 * 48 * M) + (p // 4 + 1) * 48 * M)
                    t = p - LAG
                    for i in range(4):
                        if p < NB and i < NCH[p]:
                            logits(h, p, i)
                        if 0 <= t < NB and i < NCH[t]:
                            turn(h, t, i)
                    for r, cs in values_here(p):
                        for c in cs:
                            values(h, r, c)

        @block.vector
        def _(dve):
            dve.sem_inc(turned, NQUAD)
            dve.sem_inc(mixed, LR2)
            dve.sem_inc(dve_chain, 1)
            for u in range(2):
                dve.sem_inc(o_stored[u], 1)

            def logits(h, p, i, m):
                b, n, c0 = ORDER[p], chunk_no(p, i, m), i * 512
                dst, slot, top = (lg, p % LR, mx[:, p, m]) if m == 0 else (lg2, p % LR2, mx[:, p, m])
                if i == 0 and m == 0:
                    dve.wait_ge(turned, h * NQUAD + (NQUAD + BEFORE[p - LR + 1] if p >= LR else BEFORE[NB - LR + p + 1]))
                elif i == 0:
                    dve.wait_ge(mixed, h * NB + p + 1)
                if i == 0 and p == 0:
                    dve.wait_ge(near_done, h + 1)
                dve.wait_ge(s_done, h * NCHUNK + n + 1)
                for a, z, is_near in pieces(b, i):
                    src, out = s_ps[:, n % SR, a - c0:z - c0], dst[:, slot, a:z]
                    col = 2 * i + is_near
                    ends = z == chunks(b)[i][1]
                    tab = None
                    if is_near:
                        off = P * (1 - b)
                        tab = near[:, m, a + off:z + off]
                        if with_mask(p):
                            dve.wait_ge(masked, h * NMASKED[NB] + NMASKED[p] + 1)
                            tab = near_mask[:, NMASKED[p] % NM, a + off:z + off]
                    elif V2:
                        tab = mask[:, mask_offset(b) + a:mask_offset(b) + z]
                    if tab is not None:
                        dve.sem_inc(idle_dve, 1)
                        x = nc.vector.tensor_tensor_reduce(out, src, tab, 1.0, 2 * NEG, ALU.add, ALU.max, top[:, col:col + 1])
                    else:
                        x = nc.vector.tensor_scalar(out, src, 1.0, 2 * NEG, ALU.mult, ALU.max, accum_out=top[:, col:col + 1])
                    x.then_inc(s_left if ends else dve_chain, 1)

            def maximum(h, p):
                dve.wait_ge(s_left, SR + h * NCHUNK + M * BEFORE[p + 1])
                dve.wait_ge(dve_chain, 1 + h * NSPLIT + M * sum(SPLIT[:p + 1]))
                nc.vector.tensor_reduce(negm[:, p], mx[:, p], AX.X, ALU.max, negate=True).then_inc(max_done, 1)

            def mix(h, p):
                b, n = ORDER[p], (ORDER[p] + 1) * P
                l1, l2 = sums[:, b, ds(h * 2, 1)], sums[:, b, ds(h * 2 + 1, 1)]
                dve.wait_ge(exp_done, h * 2 * NB + 2 * p + 2)
                nc.vector.reciprocal(rec[:, p:p + 1], l2).then_inc(mix_chain, 1)
                dve.wait_ge(mix_chain, h * (2 * NB) + 2 * p + 1)
                nc.vector.scalar_tensor_tensor(ratio[:, p:p + 1], l1, rec[:, p:p + 1], neglam[:], ALU.mult, ALU.mult).then_inc(mix_chain, 1)
                dve.wait_ge(mix_chain, h * (2 * NB) + 2 * p + 2)
                nc.vector.scalar_tensor_tensor(lg[:, p % LR, 0:n], lg2[:, p % LR2, 0:n], ratio[:, p:p + 1], lg[:, p % LR, 0:n],
                                               ALU.mult, ALU.add).then_inc(mixed, 1)

            def split_lo(h, p, i):
                n, (a, z), c = BEFORE[p] + i, quads(ORDER[p])[i], (ORDER[p] % 2) * P
                dve.wait_ge(t_hi, h * NQUAD + n + 1)
                nc.vector.tensor_tensor(pT_lo[:, p // 2 % 2, a:z, c:c + P], t_ps[:, n % TR, 0:z - a], pT_hi[:, p // 2 % 2, a:z, c:c + P],
                                        ALU.subtract).then_inc(t_lo, 1)

            def output(h, r):
                if V2:
                    dve.wait_ge(half_done, h * NPAIR + r + 1)
                    dve.wait_ge(o_stored[r % 2], 1 + h * (NPAIR // 2 * 16) + (r // 2) * 16)
                    nc.vector.tensor_tensor(o_sb[0:HD, r % 2], o_ps[0:HD, r % 2, 0:PAIR], o_half[:, r % 2], ALU.add).then_inc(o_left, 1)

            nc.vector.memset(mx[:], 2 * NEG).then_inc(mx_set, 1)
            dve.wait_ge(mx_set, 1)
            with dve.Fori(0, heads) as h:
                for p in range(PLACES):
                    t = p - LAG
                    for i in range(5):
                        if p < NB and i < NCH[p]:
                            for m in range(M):
                                logits(h, p, i, m)
                        if 0 <= t < NB and 1 <= i <= NCH[t]:
                            split_lo(h, t, i - 1)
                    if p < NB:
                        maximum(h, p)
                    for r in outputs_here(p):
                        output(h, r)
                    if M == 2 and 1 <= p <= NB:
                        mix(h, p - 1)
                for r in outputs_after:
                    output(h, r)

        @block.scalar
        def _(act):
            act.sem_inc(pv_quad, NPV)

            def copy_near(h):
                nc.scalar.activation(near[:], near_next[:], ACT.Copy).then_inc(near_done, 1)

            def exps(h, p, m):
                b, n = ORDER[p], (ORDER[p] + 1) * P
                buf = lg[:, p % LR, 0:n] if m == 0 else lg2[:, p % LR2, 0:n]
                if m == 0:
                    act.wait_ge(max_done, h * NB + p + 1)
                nc.scalar.activation(buf, buf, ACT.Exp, bias=negm[:, p, m:m + 1], accum_out=sums[:, b, ds(h * M + m, 1)]).then_inc(exp_done, 1)

            def split_hi(h, p, i):
                n, (a, z), c, r = BEFORE[p] + i, quads(ORDER[p])[i], (ORDER[p] % 2) * P, p // 2
                act.wait_ge(turned, NQUAD + h * NQUAD + n + 1)
                if i == 0 and p % 2 == 0:
                    act.wait_ge(pv_quad, h * NPV + (NPV + PV_BEFORE[r - 1] if r >= 2 else PV_BEFORE[NPAIR + r - 1]))
                nc.scalar.activation(pT_hi[:, r % 2, a:z, c:c + P], t_ps[:, n % TR, 0:z - a], ACT.Copy).then_inc(t_hi, 1)

            def output(h, r):
                act.wait_ge(pv_quad, NPV + h * NPV + PV_BEFORE[r + 1])
                if V2:
                    act.wait_ge(o_left, h * NPAIR + r + 1)
                    nc.scalar.activation(o_half[:, r % 2], o_ps[HD:P, r % 2, 0:PAIR], ACT.Copy).then_inc(half_done, 1)
                else:
                    act.wait_ge(o_stored[r % 2], 1 + h * (NPAIR // 2 * 16) + (r // 2) * 16)
                    nc.scalar.activation(o_sb[:, r % 2], o_ps[:, r % 2, 0:PAIR], ACT.Copy).then_inc(o_left, 1)

            act.wait_ge(near_in, 16 * M)
            copy_near(0)
            with act.Fori(0, heads) as h:
                for p in range(PLACES):
                    t = p - LAG
                    for m in range(M):
                        if 1 <= p <= NB:
                            exps(h, p - 1, m)
                    if p == NB:
                        act.wait_ge(near_in, h * 16 * M + 32 * M)
                        copy_near(h)
                    for i in range(4):
                        if 0 <= t < NB and i < NCH[t]:
                            split_hi(h, t, i)
                    for r in outputs_here(p):
                        output(h, r)
                for r in outputs_after:
                    output(h, r)


SELECTING = range(2, NB)
KEYS = mask_offset(NB)


def stage_select(nc, sems, widx, qidx, kidxT, mask):
    with Stage(nc, sems, "select") as st:
        k_hh, k_ll = (st.sb(n, [P, T], F32R) for n in ("k_hh", "k_ll"))
        q = st.sb("q", [P, 2, IH, P], F32R)
        relu = st.sb("relu", [P, 2, T], F32)
        score = st.sb("score", [P, T], F32)
        causal = st.sb("causal", [P, P], F32)
        flip = st.sb("flip", [P, T], I32)
        key = st.sb("key", [P, 2, T], I32)
        k_up, k_down = (st.sb(n, [P, KEYS], U16) for n in ("k_up", "k_down"))
        NS = len(SELECTING)
        cand, cnt, need, ge, moved, top, low = (st.sb(n, [P, NS], F32) for n in ("cand", "cnt", "need", "ge", "moved", "top", "low"))
        bit, half = st.sb("bit", [P, 1], F32), st.sb("half", [P, 1], F32)
        above, equal, taken, kept = (st.sb(n, [P, T], BF16) for n in ("above", "equal", "taken", "kept"))
        s_ps = st.ps("s", [P, 2, 4 * 512])
        k_in, scored, relued, summed, keyed, packed, causal_step, chain, counted = (
            st.sem(n) for n in ("k_in", "scored", "relued", "summed", "keyed", "packed", "causal_step", "chain", "counted"))
        q_in = [st.sem("q_in0"), st.sem("q_in1")]
        units = [(i, b, h) for i, b in enumerate(SELECTING) for h in range(IH)]
        block = st.block()

        @block.sync
        def _(sp):
            for part in range(2):
                rows = slice(part * ID, (part + 1) * ID)
                sp.dma_start(k_hh[rows].bitcast(F32), kidxT[0]).then_inc(k_in, 16)
                sp.dma_start(k_ll[rows].bitcast(F32), kidxT[1]).then_inc(k_in, 16)
            for i, b in enumerate(SELECTING):
                if i >= 2:
                    sp.wait_ge(scored, IH * (i - 1))
                for part in range(2):
                    sp.dma_start(q[part * ID:(part + 1) * ID, i % 2].bitcast(F32),
                                 qidx[part].rearrange("(h d) t -> d h t", d=ID)[:, :, b * P:(b + 1) * P]).then_inc(q_in[i % 2], 16)

        @block.gpsimd
        def _(pool):
            nc.gpsimd.memset(causal[:], 0.0).then_inc(causal_step, 1)
            pool.wait_ge(causal_step, 1)
            nc.gpsimd.affine_select(out=causal[:], in_=causal[:], compare_op=ALU.is_ge, fill=LOWEST, base=0,
                                    pattern=[[-1, P]], channel_multiplier=1).then_inc(causal_step, 1)

        @block.tensor
        def _(pe):
            pe.wait_ge(k_in, 64)
            for n, (i, b, h) in enumerate(units):
                if h == 0:
                    pe.wait_ge(q_in[i % 2], 32 * (i // 2 + 1))
                if n >= 2:
                    pe.wait_ge(relued, n - 1)
                for a, z in chunks(b):
                    out = s_ps[:, n % 2, a:z]
                    nc.tensor.matmul(out, q[:, i % 2, h], k_hh[:, a:z], start=True, stop=False)
                    x = nc.tensor.matmul(out, q[:, i % 2, h], k_ll[:, a:z], start=False, stop=True)
                x.then_inc(scored, 1)

        @block.scalar
        def _(act):
            def pack(i):
                b = SELECTING[i]
                n, o = (b + 1) * P, mask_offset(b)
                act.wait_ge(keyed, i + 1)
                halves = key[:, i % 2].bitcast(U16).rearrange("p (s two) -> p s two", two=2)
                nc.scalar.activation(k_up[:, o:o + n], halves[:, 0:n, 1], ACT.Copy).then_inc(packed, 1)
                nc.scalar.activation(k_down[:, o:o + n], halves[:, 0:n, 0], ACT.Copy).then_inc(packed, 1)

            for n, (i, b, h) in enumerate(units):
                act.wait_ge(scored, n + 1)
                if n >= 2:
                    act.wait_ge(summed, n - 1)
                nc.scalar.activation(relu[:, n % 2, 0:(b + 1) * P], s_ps[:, n % 2, 0:(b + 1) * P], ACT.Relu).then_inc(relued, 1)
                if h == 3 and i:
                    pack(i - 1)
            pack(NS - 1)

        @block.vector
        def _(dve):
            done = [0]

            def step(x):
                x.then_inc(chain, 1)
                done[0] += 1
                dve.wait_ge(chain, done[0])

            for n, (i, b, h) in enumerate(units):
                w, N = widx[:, b, h:h + 1], (b + 1) * P
                dve.wait_ge(relued, n + 1)
                if n:
                    dve.wait_ge(summed, n)
                if h == 0:
                    if i:
                        dve.wait_ge(keyed, i)
                    nc.vector.tensor_scalar(score[:, 0:N], relu[:, n % 2, 0:N], w, 0.0, ALU.mult, ALU.add).then_inc(summed, 1)
                else:
                    nc.vector.scalar_tensor_tensor(score[:, 0:N], relu[:, n % 2, 0:N], w, score[:, 0:N], ALU.mult, ALU.add).then_inc(summed, 1)
                if h == IH - 1:
                    dve.wait_ge(causal_step, 2)
                    dve.wait_ge(summed, n + 1)
                    step(nc.vector.tensor_tensor(score[:, N - P:N], score[:, N - P:N], causal[:], ALU.add))
                    step(nc.vector.tensor_scalar(flip[:, 0:N], score[:, 0:N].bitcast(I32), 31, -2 ** 31, ALU.arith_shift_right, ALU.bitwise_or))
                    if i >= 2:
                        dve.wait_ge(packed, 2 * (i - 1))
                    nc.vector.tensor_tensor(key[:, i % 2, 0:N], score[:, 0:N].bitcast(I32), flip[:, 0:N], ALU.bitwise_xor).then_inc(keyed, 1)

            step(nc.vector.memset(need[:], float(TOPK)))
            dve.wait_ge(packed, 2 * NS)
            cols = [(i, mask_offset(b), (b + 1) * P) for i, b in enumerate(SELECTING)]
            counts = [0]

            def count(keys, op, against):
                for i, o, N in cols:
                    nc.vector.tensor_scalar(mask[:, o:o + N], keys[:, o:o + N], against[:, i:i + 1], 0.0, op, ALU.add,
                                            accum_out=cnt[:, i:i + 1]).then_inc(counted, 1)

            STEPS, SMALL_STEPS = 16, 5
            for phase, keys, found in ((0, k_up, top), (1, k_down, low)):
                step(nc.vector.memset(cand[:], 32768.0))
                step(nc.vector.memset(bit[:], 32768.0))
                step(nc.vector.memset(half[:], 16384.0))
                c0, n0 = done[0], counts[0]
                with dve.Fori(0, STEPS) as s:
                    count(keys, ALU.is_ge, cand)
                    dve.wait_ge(counted, s * NS + (n0 + NS))
                    ops = [lambda: nc.vector.tensor_tensor(ge[:], cnt[:], need[:], ALU.is_ge),
                           lambda: nc.vector.scalar_tensor_tensor(moved[:], ge[:], bit[:], cand[:], ALU.mult, ALU.add),
                           lambda: nc.vector.tensor_scalar(cand[:], moved[:], half[:], None, ALU.subtract),
                           lambda: nc.vector.tensor_scalar(bit[:], bit[:], 0.5, None, ALU.mult),
                           lambda: nc.vector.tensor_scalar(half[:], half[:], 0.5, None, ALU.mult)]
                    for j, op in enumerate(ops):
                        op().then_inc(chain, 1)
                        dve.wait_ge(chain, s * SMALL_STEPS + (c0 + j + 1))
                done[0] += STEPS * SMALL_STEPS
                counts[0] += STEPS * NS
                step(nc.vector.tensor_scalar(found[:], cand[:], 0.5, None, ALU.subtract))
                if phase == 0:
                    count(k_up, ALU.is_gt, top)
                    counts[0] += NS
                    dve.wait_ge(counted, counts[0])
                    step(nc.vector.tensor_scalar(need[:], cnt[:], -1.0, float(TOPK), ALU.mult, ALU.add))
                    for i, o, N in cols:
                        x = nc.vector.scalar_tensor_tensor(k_down[:, o:o + N], k_up[:, o:o + N], top[:, i:i + 1], k_down[:, o:o + N],
                                                           ALU.is_equal, ALU.mult)
                        x.then_inc(chain, 1)
                        done[0] += 1
                    dve.wait_ge(chain, done[0])

            up_dist, dist, rank = relu[:, 0], relu[:, 1], score
            for i, o, N in cols:
                step(nc.vector.tensor_scalar(up_dist[:, 0:N], k_up[:, o:o + N], top[:, i:i + 1], 131072.0, ALU.subtract, ALU.mult))
                step(nc.vector.scalar_tensor_tensor(dist[:, 0:N], k_down[:, o:o + N], low[:, i:i + 1], up_dist[:, 0:N], ALU.subtract, ALU.add))
                step(nc.vector.tensor_scalar(above[:, 0:N], dist[:, 0:N], 0.0, 0.0, ALU.is_gt, ALU.add, accum_out=cnt[:, i:i + 1]))
                step(nc.vector.tensor_scalar(equal[:, 0:N], dist[:, 0:N], 0.0, None, ALU.is_equal))
                step(nc.vector.tensor_scalar(need[:, i:i + 1], cnt[:, i:i + 1], -1.0, float(TOPK), ALU.mult, ALU.add))
                step(nc.vector.tensor_tensor_scan(rank[:, 0:N], equal[:, 0:N], equal[:, 0:N], 0.0, ALU.add, ALU.max))
                step(nc.vector.scalar_tensor_tensor(taken[:, 0:N], rank[:, 0:N], need[:, i:i + 1], equal[:, 0:N], ALU.is_le, ALU.mult))
                step(nc.vector.tensor_tensor(kept[:, 0:N], above[:, 0:N], taken[:, 0:N], ALU.add))
                step(nc.vector.tensor_scalar(mask[:, o:o + N], kept[:, 0:N], -1.0, -NEG, ALU.add, ALU.mult))


def stage_output(nc, sems, name, M, x_dram, dst, weights, o_dram, gate_dram, gp_row, sums, ident, subln=None):
    heads = NMAPS // M
    with Stage(nc, sems, name) as st:
        w = st.sb("w", [P, 2, D], F32)
        w_hi, w_lo = (st.sb(n, [P, KD, D], F32R) for n in ("w_hi", "w_lo"))
        gp = st.sb("gp", [P, D], F32)
        inv = st.sb("inv", [P, 4, heads], F32)
        inv_wide = st.sb("inv_wide", [P, 4, D], F32)
        o, gate, scaled, gated = (st.sb(n, [P, 2, 512], F32) for n in ("o", "gate", "scaled", "gated"))
        og_hi, og_lo = (st.sb(n, [P, KD, 512], F32R) for n in ("og_hi", "og_lo"))
        x = st.sb("x", [P, 4, D], F32)
        z = st.sb("z", [P, 2, D], F32)
        out = st.sb("out", [P, 2, D], F32)
        ysq = st.sb("ysq", [P, D], BF16)
        ss, ms, sd, rs = (st.sb(n, [P, 4], F32) for n in ("ss", "ms", "sd", "rs"))
        if M == 2:
            ones, gcol = st.sb("ones", [P, P], F32), st.sb("gcol", [P, 1], F32)
            hsq, hms, hsd, hrs, hn = (st.sb(n, [P, 512], F32) for n in ("hsq", "hms", "hsd", "hrs", "hn"))
        inv_ps = st.ps("inv", [P, 2, 512])
        head_ps = st.ps("head", [P, 512])
        y_ps = st.ps("y", [P, 2, 2, 512])
        w_in = [st.sem("w_in0"), st.sem("w_in1")]
        o_in = [st.sem("o_in0"), st.sem("o_in1")]
        x_in = st.sem("x_in")
        names = ("consts_in", "w_hi_done", "w_lo_done", "inverted", "widened", "turned", "scaled_done", "gated_done", "og_hi_done", "og_lo_done",
                 "y_done", "ysq_done", "meaned", "rooted", "rs_done", "normed", "added", "h_sq", "h_sum", "h_mean", "h_root", "h_inv", "h_norm", "gcol_done")
        (consts_in, w_hi_done, w_lo_done, inverted, widened, turned, scaled_done, gated_done, og_hi_done, og_lo_done,
         y_done, ysq_done, meaned, rooted, rs_done, normed, added, h_sq, h_sum, h_mean, h_root, h_inv, h_norm, gcol_done) = (st.sem(n) for n in names)
        stored = [st.sem("stored0"), st.sem("stored1")]
        idle_sp = st.sem("idle_sp")
        block = st.block()

        @block.sync
        def _(sp):
            sp.dma_start(gp[:], gp_row).then_inc(consts_in, 16)
            if M == 2:
                sp.dma_start(gcol[:], subln.rearrange("o p -> p o"), allow_slow_non_contiguous=True).then_inc(consts_in, 16)
            for k in range(KD):
                if k >= 2:
                    sp.wait_ge(w_lo_done, 1 + k - 1)
                sp.dma_start(w[:, k % 2], weights[k * P:(k + 1) * P, :]).then_inc(w_in[k % 2], 16)
            with sp.Fori(0, G) as g:
                for k in range(KD):
                    sp.wait_ge(gated_done, 1 + g * KD + max(k - 1, 0))
                    sp.sem_inc(idle_sp, 1)
                    for dram, buf in ((o_dram, o), (gate_dram, gate)):
                        sp.dma_start(buf[:, k % 2], dram[k * P:(k + 1) * P, ds(g * 512, 512)]).then_inc(o_in[k % 2], 16)
                sp.wait_ge(added, 1 + g * 4)
                sp.sem_inc(idle_sp, 1)
                for j in range(4):
                    sp.dma_start(x[:, j], x_dram[ds(g * 512 + j * P, P), :]).then_inc(x_in, 16)
                for j in range(4):
                    sp.wait_ge(added, 1 + g * 4 + j + 1)
                    sp.sem_inc(idle_sp, 1)
                    sp.dma_start(dst[ds(g * 512 + j * P, P), :], out[:, j % 2]).then_inc(stored[j % 2], 16)
            for u in range(2):
                sp.wait_ge(stored[u], 1 + G * 2 * 16)

        @block.gpsimd
        def _(pool):
            st.start_at_one(pool)
            for k in range(KD):
                pool.wait_ge(w_in[k % 2], 1 + 16 * (k // 2 + 1))
                nc.gpsimd.tensor_copy(w_hi[:, k], w[:, k % 2]).then_inc(w_hi_done, 1)
                pool.wait_ge(w_hi_done, 1 + k + 1)
                nc.gpsimd.tensor_tensor(w_lo[:, k], w[:, k % 2], w_hi[:, k], ALU.subtract).then_inc(w_lo_done, 1)

        @block.tensor
        def _(pe):
            with pe.Fori(0, G) as g:
                def turn(k):
                    pe.wait_ge(scaled_done, 1 + g * KD + max(k - 1, 0))
                    for j in range(4):
                        m = nc.tensor.transpose(inv_ps[:, k % 2, j * P:(j + 1) * P], inv_wide[:, j, k * P:(k + 1) * P], ident[:])
                    m.then_inc(turned, 1)
                pe.wait_ge(widened, 1 + g * 4 + 4)
                for k in range(KD):
                    turn(k)
                    if M == 2:
                        if k == 0:
                            pe.wait_ge(gcol_done, 1 + 2)
                        pe.wait_ge(h_sq, 1 + g * KD + k + 1)
                        pe.wait_ge(h_mean, 1 + g * KD + k)
                        nc.tensor.matmul(head_ps[:], ones[:], hsq[:], start=True, stop=True).then_inc(h_sum, 1)
                for j in range(4):
                    pe.wait_ge(normed, 1 + g * 4 + max(j - 1, 0))
                    for n in range(2):
                        terms = [(a, b, k) for k in range(KD) for a, b in ((og_hi, w_hi), (og_lo, w_hi), (og_hi, w_lo))]
                        for i, (a, b, k) in enumerate(terms):
                            if j == 0 and n == 0 and i % 3 == 0:
                                pe.wait_ge(og_lo_done, 1 + g * KD + k + 1)
                                pe.wait_ge(w_lo_done, 1 + k + 1)
                            m = nc.tensor.matmul(y_ps[:, j % 2, n], a[:, k, j * P:(j + 1) * P], b[:, k, n * 512:(n + 1) * 512],
                                                 start=(i == 0), stop=(i == len(terms) - 1))
                    m.then_inc(y_done, 1)

        @block.scalar
        def _(act):
            with act.Fori(0, G) as g:
                for k in range(KD):
                    if M == 2:
                        act.wait_ge(scaled_done, 1 + g * KD + k + 1)
                        act.wait_ge(h_sum, 1 + g * KD + k)
                        nc.scalar.activation(hsq[:], scaled[:, k % 2], ACT.Square).then_inc(h_sq, 1)
                        act.wait_ge(h_mean, 1 + g * KD + k + 1)
                        act.wait_ge(h_inv, 1 + g * KD + k)
                        nc.scalar.activation(hsd[:], hms[:], ACT.Sqrt).then_inc(h_root, 1)
                    act.wait_ge(gated_done, 1 + g * KD + k + 1)
                    act.wait_ge(y_done, 1 + g * 4)
                    nc.scalar.activation(og_hi[:, k], gated[:, k % 2], ACT.Copy).then_inc(og_hi_done, 1)
                for j in range(4):
                    act.wait_ge(y_done, 1 + g * 4 + j + 1)
                    act.wait_ge(ysq_done, 1 + g * 4 + j)
                    act.wait_ge(rs_done, 1 + g * 4)
                    nc.scalar.activation(ysq[:], flat(y_ps[:, j % 2]), ACT.Square, accum_out=ss[:, j:j + 1]).then_inc(ysq_done, 1)
                    act.wait_ge(meaned, 1 + g * 4 + j + 1)
                    nc.scalar.activation(sd[:, j:j + 1], ms[:, j:j + 1], ACT.Sqrt).then_inc(rooted, 1)

        @block.vector
        def _(dve):
            dve.wait_ge(consts_in, 1 + 16 * M)
            if M == 2:
                nc.vector.memset(ones[:], 1.0 / P).then_inc(gcol_done, 1)
                nc.vector.tensor_scalar(gcol[:], gcol[:], 1.0 - LAMBDA_INIT, None, ALU.mult).then_inc(gcol_done, 1)
                dve.wait_ge(gcol_done, 1 + 2)
            with dve.Fori(0, G) as g:
                dve.wait_ge(widened, 1 + g * 4)
                for j in range(4):
                    l1 = sums.rearrange("p b (h m) -> p b h m", m=M)[:, ds(g * 4 + j, 1), :, 0].rearrange("p o h -> p (o h)")
                    nc.vector.reciprocal(inv[:, j], l1).then_inc(inverted, 1)
                dve.wait_ge(inverted, 1 + g * 4 + 4)
                dve.wait_ge(turned, 1 + g * KD)
                for j in range(4):
                    nc.vector.tensor_copy(inv_wide[:, j].rearrange("p (h e) -> p h e", h=heads),
                                          inv[:, j].unsqueeze(2).to_broadcast([P, heads, D // heads])).then_inc(widened, 1)
                for k in range(KD):
                    u = k % 2
                    dve.wait_ge(o_in[u], 1 + g * 128 + (k // 2 + 1) * 32)
                    dve.wait_ge(turned, 1 + g * KD + k + 1)
                    if M == 2:
                        dve.wait_ge(h_sq, 1 + g * KD + max(k - 1, 0))
                    dve.wait_ge(gated_done, 1 + g * KD + max(k - 1, 0) if k else g * KD)
                    nc.vector.tensor_tensor(scaled[:, u], inv_ps[:, u], o[:, u], ALU.mult).then_inc(scaled_done, 1)
                    dve.wait_ge(scaled_done, 1 + g * KD + k + 1)
                    src = scaled[:, u]
                    if M == 2:
                        dve.wait_ge(h_sum, 1 + g * KD + k + 1)
                        dve.wait_ge(h_root, 1 + g * KD + k)
                        nc.vector.tensor_scalar(hms[:], head_ps[:], EPS, None, ALU.add).then_inc(h_mean, 1)
                        dve.wait_ge(h_root, 1 + g * KD + k + 1)
                        dve.wait_ge(h_norm, 1 + g * KD + k)
                        nc.vector.reciprocal(hrs[:], hsd[:]).then_inc(h_inv, 1)
                        dve.wait_ge(h_inv, 1 + g * KD + k + 1)
                        dve.wait_ge(gated_done, 1 + g * KD + k)
                        nc.vector.scalar_tensor_tensor(hn[:], scaled[:, u], gcol[:], hrs[:], ALU.mult, ALU.mult).then_inc(h_norm, 1)
                        dve.wait_ge(h_norm, 1 + g * KD + k + 1)
                        src = hn[:]
                    dve.wait_ge(og_lo_done, 1 + g * KD + max(k - 1, 0) if k else g * KD)
                    nc.vector.tensor_tensor(gated[:, u], src, gate[:, u], ALU.mult).then_inc(gated_done, 1)
                    dve.wait_ge(og_hi_done, 1 + g * KD + k + 1)
                    nc.vector.tensor_tensor(og_lo[:, k], gated[:, u], og_hi[:, k], ALU.subtract).then_inc(og_lo_done, 1)
                dve.wait_ge(x_in, 1 + g * 64 + 64)
                for j in range(4):
                    dve.wait_ge(ysq_done, 1 + g * 4 + j + 1)
                    dve.wait_ge(rooted, 1 + g * 4 + j)
                    nc.vector.tensor_scalar(ms[:, j:j + 1], ss[:, j:j + 1], 1.0 / D, EPS, ALU.mult, ALU.add).then_inc(meaned, 1)
                    dve.wait_ge(rooted, 1 + g * 4 + j + 1)
                    dve.wait_ge(normed, 1 + g * 4 + j)
                    nc.vector.reciprocal(rs[:, j:j + 1], sd[:, j:j + 1]).then_inc(rs_done, 1)
                    dve.wait_ge(rs_done, 1 + g * 4 + j + 1)
                    dve.wait_ge(added, 1 + g * 4 + max(j - 1, 0))
                    nc.vector.scalar_tensor_tensor(z[:, j % 2], flat(y_ps[:, j % 2]), rs[:, j:j + 1], gp[:], ALU.mult, ALU.mult).then_inc(normed, 1)
                    dve.wait_ge(normed, 1 + g * 4 + j + 1)
                    dve.wait_ge(stored[j % 2], 1 + g * 32 + (j // 2) * 16)
                    nc.vector.tensor_tensor(out[:, j % 2], z[:, j % 2], x[:, j], ALU.add).then_inc(added, 1)


def stage_identity(nc, sems, ident):
    with Stage(nc, sems, "identity") as st:
        made = st.sem("made")
        block = st.block()

        @block.gpsimd
        def _(pool):
            nc.gpsimd.memset(ident[:], 0.0).then_inc(made, 1)
            pool.wait_ge(made, 1)
            nc.gpsimd.affine_select(out=ident[:], in_=ident[:], compare_op=ALU.not_equal, fill=1.0, base=0,
                                    pattern=[[-1, P]], channel_multiplier=1).then_inc(made, 1)
            pool.wait_ge(made, 2)


def program(nc, ins, out):
    scratch = lambda name, shape: nc.dram_tensor(f"scratch_{name}", shape, F32).ap()
    gp_dram, bias_dram = scratch("gp", (2, P, D)), scratch("bias", (NMAPS, P, 384))
    qT, kT, v = scratch("qT", (2, D, T)), scratch("kT", (2, D, T)), scratch("v", (2, T, D))
    gateT, oT, x1 = scratch("gateT", (D, T)), scratch("oT", (D, T)), scratch("x1", (T, D))
    cqT, ckvT, kidxT, qidx = scratch("cqT", (2, QR, T)), scratch("ckvT", (2, KVR, T)), scratch("kidxT", (2, ID, T)), scratch("qidx", (2, IH * ID, T))
    sems = Semaphores(nc)
    with ExitStack() as keep:
        sb = lambda ctx, name, shape, dt: ctx.enter_context(nc.sbuf_tensor(name, shape, dt))
        ident, ada, neglam = sb(keep, "ident", [P, P], F32), sb(keep, "ada", [P, 2, 2, KD], F32), sb(keep, "neglam", [P, 1], F32)
        sums, widx = sb(keep, "sums", [P, NB, NMAPS], F32), sb(keep, "widx", [P, NB, IH], F32)
        stage_identity(nc, sems, ident)
        stage_modulation(nc, sems, ins, ada, neglam, gp_dram, bias_dram)

        with ExitStack() as c:
            hT = [sb(c, f"a_{n}", [P, KD, T], F32R) for n in ("hT_hi", "hT_lo")]
            stage_input(nc, sems, "a_in", ins["x"][0], ada, 0, ident, hT)
            win = ins["a_w_in"][0].rearrange("(k p) n -> p k n", p=P)
            stage_project_T(nc, sems, "a_gate", hT, KD, [(lambda b: win[:, :, ds(b * P + SMALL, P)], KD, 1.0, gateT, None)])
            stage_narrow(nc, sems, ins, hT, ident, widx, cqT, ckvT, kidxT)
        with ExitStack() as c:
            cq = [sb(c, f"cq_{n}", [P, 2, T], F32R) for n in ("hi", "lo")]
            ckv = [sb(c, f"ckv_{n}", [P, 1, T], F32R) for n in ("hi", "lo")]
            loaded = sems.new("latents_loaded")
            with nc.Block() as block:
                @block.sync
                def _(sp):
                    for part in range(2):
                        sp.dma_start(cq[part].bitcast(F32)[:], cqT[part].rearrange("(k p) t -> p k t", p=P)).then_inc(loaded, 16)
                        sp.dma_start(ckv[part].bitcast(F32)[:, 0], ckvT[part]).then_inc(loaded, 16)
                    sp.wait_ge(loaded, 64)
            wq, wqi = (ins[n][0].rearrange("(k p) n -> p k n", p=P) for n in ("a_w_uq", "a_w_qidx"))
            wk = ins["a_w_uk"][0].rearrange("h r d -> r h d")
            wv = ins["a_w_uv"][0].rearrange("h r d -> r h d")
            stage_project_T(nc, sems, "a_q", cq, 2, [(lambda b: wq[:, :, ds(b * P, P)], 8, HD ** -0.5, qT[0], qT[1]),
                                                     (lambda b: wqi[:, :, ds(b * P, P)], 4, 1.0, qidx[0], qidx[1])])
            stage_project_T(nc, sems, "a_k", ckv, 1, [(lambda b: wk[:, ds(b * 2, 2), :], 8, 1.0, kT[0], kT[1])])
            stage_project_v(nc, sems, "a_v", ckv, 1, lambda n: wv[:, ds(n * 8, 8), :], v[0], v[1])
        sems.retire()
        with ExitStack() as c:
            mask = sb(c, "mask", [P, KEYS], BF16)
            stage_select(nc, sems, widx, qidx, kidxT, mask)
            stage_attention(nc, sems, "a_att", 16, 1, ident, bias_dram, qT, kT, v, oT, sums, mask=mask)
        stage_output(nc, sems, "a_out", 1, ins["x"][0], x1, ins["a_w_out"][0], oT, gateT, gp_dram[0], sums, ident)

        sems.retire()

        with ExitStack() as c:
            hT = [sb(c, f"b_{n}", [P, KD, T], F32R) for n in ("hT_hi", "hT_lo")]
            stage_input(nc, sems, "b_in", x1, ada, 1, ident, hT)
            win = ins["b_w_in"][0].rearrange("(k p) n -> p k n", p=P)
            stage_project_T(nc, sems, "b_qkg", hT, KD, [(lambda b: win[:, :, ds(b * P, P)], KD, HD ** -0.5, qT[0], qT[1]),
                                                        (lambda b: win[:, :, ds(b * P + D, P)], KD, 1.0, kT[0], kT[1]),
                                                        (lambda b: win[:, :, ds(b * P + 3 * D, P)], KD, 1.0, gateT, None)])
            stage_project_v(nc, sems, "b_v", hT, KD, lambda n: win[:, :, ds(n * 512 + 2 * D, 512)], v[0], v[1])
        stage_attention(nc, sems, "b_att", 8, 2, ident, bias_dram, qT, kT, v, oT, sums, neglam=neglam)
        stage_output(nc, sems, "b_out", 2, x1, out, ins["b_w_out"][0], oT, gateT, gp_dram[1], sums, ident, subln=ins["b_subln"])


_INS = ["x", "c", "rel_bias", "mod_w", "mod_b", "pre_g", "post_g", "a_w_in", "a_q_norm", "a_kv_norm", "a_kidx_norm", "a_w_uq",
        "a_w_qidx", "a_w_uk", "a_w_uv", "a_w_out", "b_w_in", "b_lam_q1", "b_lam_k1", "b_lam_q2", "b_lam_k2", "b_subln", "b_w_out"]


def kernel(**inputs):
    import concourse.bacc as bacc
    from concourse.bass_utils import run_bass_kernel_spmd

    nc = bacc.Bacc("TRN2", target_bir_lowering=False, num_devices=1)
    arrays = {name: np.ascontiguousarray(inputs[name]) for name in _INS}
    arrays["onehot"] = bucket_onehot()
    ins = {name: nc.dram_tensor(f"in_{name}", a.shape, mybir.dt.from_np(a.dtype), kind="ExternalInput").ap() for name, a in arrays.items()}
    out = nc.dram_tensor("out_dram", (1, T, D), F32, kind="ExternalOutput").ap()
    program(nc, ins, out[0])
    r = run_bass_kernel_spmd(nc, [{f"in_{name}": a for name, a in arrays.items()}], core_ids=[0])
    return r.results[0]["out_dram"]
```

```python
import math
from contextlib import ExitStack

import concourse.bass as bass
import numpy as np
from concourse import mybir

F32 = mybir.dt.float32
F32R = mybir.dt.float32r
BF16 = mybir.dt.bfloat16
U16 = mybir.dt.uint16
I32 = mybir.dt.int32
ALU = mybir.AluOpType
ACT = mybir.ActivationFunctionType
AX = mybir.AxisListType
ds = bass.ds

P = 128
T = 2048
D = 1024
KD = D // P
NB = T // P
G = 4
GT = T // G
EPS = 1e-6
NBUCKETS, MAXDIST, NMAPS = 32, 128, 16
NEG = -1.0e30
LOWEST = -3.0e38
QR, KVR, ID, IH = D // 4, D // 8, 64, 8
SMALL = QR + KVR + ID + IH
TOPK = 256
HD = 64
LAMBDA_INIT = 0.8 - 0.6 * math.exp(-0.3)
NEAR = 2 * P


def bucket_onehot():
    n = np.maximum(255 - np.arange(384), 0)
    nf = np.maximum(n, 1).astype(np.float32)
    half = NBUCKETS // 2
    large = half + (np.log(nf / np.float32(half)) / np.float32(math.log(MAXDIST / half))
                    * np.float32(NBUCKETS - half)).astype(np.int32)
    b = np.where(n < half, n, np.minimum(large, NBUCKETS - 1))
    return (np.arange(NBUCKETS)[:, None] == b[None, :]).astype(np.float32)


def flat(ap):
    return ap.rearrange("p a b -> p (a b)")


class Semaphores:

    def __init__(self, nc):
        self.nc, self.held = nc, []

    def new(self, name):
        self.held.append(self.nc.alloc_semaphore(name=name))
        return self.held[-1]

    def retire(self):
        self.nc.clear_and_free_semaphores(self.held)
        self.nc.all_engine_barrier()
        self.held = []


class Stage:

    def __init__(self, nc, sems, name):
        self.nc, self.sems, self.name, self.ctx, self.own = nc, sems, name, ExitStack(), []

    def __enter__(self):
        return self

    def __exit__(self, *a):
        return self.ctx.__exit__(*a)

    def sb(self, name, shape, dt):
        return self.ctx.enter_context(self.nc.sbuf_tensor(f"{self.name}_sb_{name}", shape, dt))

    def ps(self, name, shape, dt=F32):
        return self.ctx.enter_context(self.nc.psum_tensor(f"{self.name}_ps_{name}", shape, dt))

    def sem(self, name):
        self.own.append(self.sems.new(f"{self.name}_sem_{name}"))
        return self.own[-1]

    def start_at_one(self, engine):
        for s in self.own:
            engine.sem_inc(s, 1)

    def block(self):
        return self.ctx.enter_context(self.nc.Block())


def chunk_place(chunk):
    return chunk // 6, chunk % 6 // 2, chunk % 2


EARLY, LATE = range(0, 4), range(4, 12)


class Modulation:

    def __init__(self, sb):
        self.cact, self.cwide = sb("mod_cact", [P, KD], F32), sb("mod_cwide", [P, KD, P], F32)
        self.bcol, self.preg = sb("mod_bcol", [P, 2, 3 * KD], F32), sb("mod_preg", [P, 2, KD], F32)

    def load(self, sp, w, w_in, w_used, mod_w, chunks):
        for n, chunk in enumerate(chunks):
            l, third, half = chunk_place(chunk)
            if n >= 2:
                sp.wait_ge(w_used, n - 1)
            c0 = third * D + half * 512
            sp.dma_start(w[:, n % 2], mod_w[l].rearrange("(k p) n -> p k n", p=P)[:, :, c0:c0 + 512]).then_inc(w_in[n % 2], 16)

    def multiply(self, nc, pe, w, w_in, w_used, chunks, pcol, pgate):
        for n, chunk in enumerate(chunks):
            l, third, half = chunk_place(chunk)
            pe.wait_ge(w_in[n % 2], 16 * (n // 2 + 1))
            if third < 2:
                for f in range(4):
                    for k in range(KD):
                        m = nc.tensor.matmul(pcol[:, third * KD + half * 4 + f:third * KD + half * 4 + f + 1],
                                             w[:, n % 2, k, f * P:(f + 1) * P], self.cact[:, k:k + 1], start=(k == 0), stop=(k == KD - 1))
            else:
                for k in range(KD):
                    m = nc.tensor.matmul(pgate[:, l, half], self.cwide[:, k], w[:, n % 2, k], start=(k == 0), stop=(k == KD - 1))
            m.then_inc(w_used, 1)

    def finish_columns(self, nc, dve, l, pcol, ada, scale, done):
        nc.vector.tensor_tensor(ada[:, l, 1], pcol[:, 0:KD], self.bcol[:, l, 0:KD], ALU.add).then_inc(done, 1)
        nc.vector.tensor_tensor(scale[:], pcol[:, KD:2 * KD], self.bcol[:, l, KD:2 * KD], ALU.add).then_inc(done, 1)
        dve.wait_ge(done, 2)
        nc.vector.scalar_tensor_tensor(ada[:, l, 0], scale[:], 1.0, self.preg[:, l], ALU.add, ALU.mult).then_inc(done, 1)


def stage_modulation(nc, sems, ins, modulation, ada, neglam, bias_dram):
    with Stage(nc, sems, "mod") as st:
        w = st.sb("w", [P, 2, KD, 512], F32)
        c = st.sb("c", [P, KD], F32)
        cact, cwide = modulation.cact, modulation.cwide
        scale = st.sb("scale", [P, KD], F32)
        relb = st.sb("relb", [NBUCKETS, NMAPS], F32)
        onehot = st.sb("onehot", [NBUCKETS, 384], F32)
        far = st.sb("far", [NMAPS, 1], F32)
        bvec = st.sb("bvec", [NMAPS, 384], F32)
        lams = st.sb("lams", [P, 4, HD], F32)
        lprod = st.sb("lprod", [P, 2, HD], F32)
        ldot, lexp = (st.sb(n, [P, 2], F32) for n in ("ldot", "lexp"))
        pcol, pbias = st.ps("pcol", [P, 512]), st.ps("pbias", [P, 512])
        c_in, small_in, c_ready, w_used, bias_mm, bias_done, stored, lam_dot, lam_exp, lam_done, self_dve, columns_done = (
            st.sem(x) for x in ("c_in", "small_in", "c_ready", "w_used", "bias_mm", "bias_done", "stored", "lam_dot", "lam_exp",
                                "lam_done", "self_dve", "columns_done"))
        w_in = [st.sem("w_in0"), st.sem("w_in1")]
        block = st.block()
        ALL_SMALL = 16 * 8

        @block.sync
        def _(sp):
            sp.dma_start(c[:], ins["c"].rearrange("b (k p) -> p (b k)", p=P), allow_slow_non_contiguous=True).then_inc(c_in, 16)
            modulation.load(sp, w, w_in, w_used, ins["mod_w"], EARLY[:2])
            sp.dma_start(modulation.bcol[:], ins["mod_b"].rearrange("l (k p) -> p l k", p=P), allow_slow_non_contiguous=True).then_inc(small_in, 16)
            sp.dma_start(modulation.preg[:], ins["pre_g"].rearrange("l (k p) -> p l k", p=P), allow_slow_non_contiguous=True).then_inc(small_in, 16)
            sp.dma_start(relb[:], ins["rel_bias"]).then_inc(small_in, 16)
            sp.dma_start(onehot[:], ins["onehot"]).then_inc(small_in, 16)
            for j, name in enumerate(("b_lam_q1", "b_lam_k1", "b_lam_q2", "b_lam_k2")):
                sp.dma_start(lams[:, j], ins[name][0].partition_broadcast(P)).then_inc(small_in, 16)
            for n in (2, 3):
                l, third, half = chunk_place(EARLY[n])
                sp.wait_ge(w_used, n - 1)
                c0 = third * D + half * 512
                sp.dma_start(w[:, n % 2], ins["mod_w"][l].rearrange("(k p) n -> p k n", p=P)[:, :, c0:c0 + 512]).then_inc(w_in[n % 2], 16)
            sp.wait_ge(bias_done, 1)
            sp.dma_start(bias_dram, bvec[:].unsqueeze(1).to_broadcast([NMAPS, P, 384])).then_inc(stored, 16)
            sp.wait_ge(stored, 16)

        @block.scalar
        def _(act):
            act.wait_ge(c_in, 16)
            nc.scalar.activation(cact[:], c[:], ACT.Silu).then_inc(c_ready, 1)
            act.wait_ge(lam_dot, 2)
            nc.scalar.activation(lexp[:], ldot[:], ACT.Exp).then_inc(lam_exp, 1)

        @block.tensor
        def _(pe):
            pe.wait_ge(c_ready, 1)
            modulation.multiply(nc, pe, w, w_in, w_used, EARLY, pcol, None)
            pe.wait_ge(small_in, ALL_SMALL)
            nc.tensor.matmul(pbias[0:NMAPS, 0:384], relb[:], onehot[:], start=True, stop=True).then_inc(bias_mm, 1)

        @block.vector
        def _(dve):
            dve.wait_ge(c_ready, 1)
            nc.vector.tensor_copy(cwide[:], cact[:].unsqueeze(2).to_broadcast([P, KD, P])).then_inc(self_dve, 1)
            dve.wait_ge(small_in, ALL_SMALL)
            for j in range(2):
                nc.vector.tensor_tensor(lprod[:, j], lams[:, 2 * j], lams[:, 2 * j + 1], ALU.mult).then_inc(self_dve, 1)
            dve.wait_ge(self_dve, 3)
            for j in range(2):
                nc.vector.tensor_reduce(ldot[:, j:j + 1], lprod[:, j], AX.X, ALU.add).then_inc(lam_dot, 1)
            dve.wait_ge(lam_exp, 1)
            nc.vector.tensor_scalar(neglam[:], lexp[:, 1:2], lexp[:, 0:1], -LAMBDA_INIT, ALU.subtract, ALU.add).then_inc(lam_done, 1)
            dve.wait_ge(w_used, len(EARLY))
            modulation.finish_columns(nc, dve, 0, pcol, ada, scale, columns_done)
            dve.wait_ge(bias_mm, 1)
            nc.vector.tensor_copy(far[:], pbias[0:NMAPS, 0:1]).then_inc(self_dve, 1)
            dve.wait_ge(self_dve, 4)
            nc.vector.tensor_scalar(bvec[:], pbias[0:NMAPS, 0:384], far[:], None, ALU.subtract).then_inc(self_dve, 1)
            dve.wait_ge(self_dve, 5)
            nc.vector.memset(bvec[:, 256:384], NEG).then_inc(bias_done, 1)


def stage_input(nc, sems, name, x_dram, ada, layer, ident, hT):
    hT_hi, hT_lo = hT
    with Stage(nc, sems, name) as st:
        x = st.sb("x", [P, 2, 4, D], F32)
        xn = st.sb("xn", [P, 4, D], F32)
        sq = st.sb("sq", [P, D], BF16)
        h = st.sb("h", [P, 2, 512], F32)
        eps = st.sb("eps", [P, 1], F32)
        ss, sd, rs = (st.sb(n, [P, 4], F32) for n in ("ss", "sd", "rs"))
        pt = st.ps("pt", [P, KD, 512])
        x_in = [st.sem(f"x_in{u}") for u in range(2)]
        eps_set, squared, rooted, inverted, normed, turned, scaled, split_hi, split_lo = (
            st.sem(n) for n in ("eps_set", "squared", "rooted", "inverted", "normed", "turned", "scaled", "split_hi", "split_lo"))
        idle_sp = st.sem("idle_sp")
        block = st.block()

        def groups(engine, step):
            with engine.Fori(0, G // 2 - 1) as i:
                step(i * 2, 0, False)
                step(i * 2 + 1, 1, False)
            step(G - 2, 0, False)
            step(G - 1, 1, True)

        @block.gpsimd
        def _(pool):
            st.start_at_one(pool)
            nc.gpsimd.memset(eps[:], EPS).then_inc(eps_set, 1)

        @block.sync
        def _(sp):
            def load(g, u):
                sp.dma_start(x[:, u], x_dram[ds(g * 512, 512), :].rearrange("(j p) n -> p j n", p=P)).then_inc(x_in[u], 16)

            def step(g, u, last):
                if not isinstance(g, int) or g + 2 < G:
                    sp.wait_ge(normed, g * 4 + 5)
                    sp.sem_inc(idle_sp, 1)
                    load(g + 2, u)

            for j in range(4):
                sp.dma_start(x[:, 0, j], x_dram[j * P:(j + 1) * P, :]).then_inc(x_in[0], 16)
            load(1, 1)
            groups(sp, step)

        @block.scalar
        def _(act):
            def square(g, u, j):
                if j == 0:
                    act.wait_ge(x_in[u], 1 + (g - u) * 8 + (64 if u == 0 else 16))
                    act.wait_ge(inverted, g + 1)
                act.wait_ge(squared, g * 4 + j + 1)
                nc.scalar.activation(sq[:], x[:, u, j], ACT.Square, accum_out=ss[:, j:j + 1]).then_inc(squared, 1)

            def root(g):
                act.wait_ge(squared, g * 4 + 5)
                nc.scalar.activation(sd[:], ss[:], ACT.Sqrt, bias=eps[:], scale=1.0 / D).then_inc(rooted, 1)

            def step(g, u, last):
                for k in range(KD):
                    act.wait_ge(turned, g * KD + k + 2)
                    act.wait_ge(split_lo, g * KD + (k if k else 1))
                    nc.scalar.activation(h[:, k % 2], pt[:, k], ACT.Identity, scale=ada[:, layer, 0, k:k + 1],
                                         bias=ada[:, layer, 1, k:k + 1]).then_inc(scaled, 1)
                    if k % 2 == 1 and not last:
                        square(g + 1, 1 - u, k // 2)
                if not last:
                    root(g + 1)

            act.wait_ge(eps_set, 2)
            for j in range(4):
                square(0, 0, j)
            root(0)
            groups(act, step)

        @block.tensor
        def _(pe):
            def step(g, u, last):
                for k in range(KD):
                    pe.wait_ge(normed, g * 4 + 5)
                    pe.wait_ge(scaled, g * KD + 1)
                    for j in range(4):
                        m = nc.tensor.transpose(pt[:, k, j * P:(j + 1) * P], xn[:, j, k * P:(k + 1) * P], ident[:])
                    m.then_inc(turned, 1)

            groups(pe, step)

        @block.vector
        def _(dve):
            def step(g, u, last):
                dve.wait_ge(rooted, g + 2)
                dve.wait_ge(normed, g * 4 + 1)
                nc.vector.reciprocal(rs[:], sd[:]).then_inc(inverted, 1)
                dve.wait_ge(inverted, g + 2)
                dve.wait_ge(turned, g * KD + 1)
                for j in range(4):
                    nc.vector.tensor_scalar(xn[:, j], x[:, u, j], rs[:, j:j + 1], None, ALU.mult).then_inc(normed, 1)
                for k in range(KD):
                    dve.wait_ge(scaled, g * KD + k + 2)
                    nc.vector.tensor_copy(hT_hi[:, k, ds(g * 512, 512)], h[:, k % 2]).then_inc(split_hi, 1)
                    dve.wait_ge(split_hi, g * KD + k + 2)
                    nc.vector.tensor_tensor(hT_lo[:, k, ds(g * 512, 512)], h[:, k % 2], hT_hi[:, k, ds(g * 512, 512)],
                                            ALU.subtract).then_inc(split_lo, 1)

            groups(dve, step)


class Job:

    def __init__(self, kind, xT, KB, weights, units, scale, hi_dram, lo_dram=None):
        self.kind, self.xT, self.KB, self.weights, self.pairs, self.scale = kind, xT, KB, weights, units // 2, scale
        self.hi_dram, self.lo_dram, self.split = hi_dram, lo_dram, kind != "silu"


def stage_project(nc, sems, name, jobs, beside=None):
    KBMAX = max(job.KB for job in jobs)
    with Stage(nc, sems, name) as st:
        w, w_hi, w_lo = (st.sb(n, [P, 2, KBMAX, P], t) for n, t in (("w", F32), ("w_hi", F32R), ("w_lo", F32R)))
        o_hi, o_lo = (st.sb(n, [P, G, 512], F32) for n in ("o_hi", "o_lo"))
        o_plain = st.sb("o_plain", [P, G, 512], F32) if beside else None
        acc = st.ps("acc", [P, 2, G, 512])
        w_hi_done, w_lo_done, summed, left_hi, left, lo_ready = (st.sem(n) for n in ("w_hi_done", "w_lo_done", "summed", "left_hi", "left", "lo_ready"))
        w_in, stored = ([st.sem(f"{n}{u}") for u in range(c)] for n, c in (("w_in", 2), ("stored", G)))
        idle_sp, idle_pool = st.sem("idle_sp"), st.sem("idle_pool")
        ready = lo_ready if beside else left
        CREDIT = 8

        base, store_base = [0], [0]
        for job in jobs:
            base.append(base[-1] + 2 * job.pairs)
            store_base.append(store_base[-1] + 2 * job.pairs * (32 if job.split else 16))
        block = st.block()

        def units(engine, unit, before_pair=None):
            for c, job in enumerate(jobs):
                with engine.Fori(0, job.pairs) as i:
                    if before_pair is not None:
                        before_pair(job, i, i * 2 + base[c])
                    for u in range(2):
                        unit(c, job, i, u, i * 2 + (base[c] + u))

        @block.sync
        def _(sp):
            def load(job, i, u):
                sp.dma_start(w[:, u, 0:job.KB], job.weights(i * 2 + u)).then_inc(w_in[u], 16)

            def store(job, i, u, n):
                for g in range(G):
                    sp.wait_ge(ready, n * 4 + (1 + CREDIT + g + 1))
                    sp.sem_inc(idle_sp, 1)
                    for dram, buf in ([(job.hi_dram, o_hi), (job.lo_dram, o_lo)] if job.split else [(job.hi_dram, o_lo)]):
                        if job.kind == "values":
                            t0 = u * (T // 2) + g * 2 * P
                            dst = dram[t0:t0 + 2 * P, ds(i * (2 * P), 2 * P)].rearrange("(j p) e -> p j e", p=P)
                            src = buf[:, g].rearrange("p (j e) -> p j e", j=2)
                        else:
                            dst, src = dram[ds((i * 2 + u) * P, P), g * 512:(g + 1) * 512], buf[:, g]
                        sp.dma_start(dst, src).then_inc(stored[g], 16)

            for u in range(2):
                load(jobs[0], 0, u)
            for c, job in enumerate(jobs):
                def pair(i, next_job, next_i):
                    for u in range(2):
                        n = i * 2 + (base[c] + u)
                        if next_job is not None:
                            sp.wait_ge(w_lo_done, n + 2)
                            sp.sem_inc(idle_sp, 1)
                            load(next_job, next_i, u)
                        store(job, i, u, n)

                if job.pairs > 1:
                    with sp.Fori(0, job.pairs - 1) as i:
                        pair(i, job, i + 1)
                pair(job.pairs - 1, jobs[c + 1] if c + 1 < len(jobs) else None, 0)
            for g in range(G):
                sp.wait_ge(stored[g], 1 + store_base[-1])

        @block.gpsimd
        def _(pool):
            st.start_at_one(pool)
            pool.sem_inc(summed, CREDIT)
            pool.sem_inc(left, CREDIT)
            pool.sem_inc(lo_ready, CREDIT)

            def split_weights(job, i, n0):
                for u in range(2):
                    n = n0 + u
                    if job.kind != "values":
                        pool.wait_ge(w_in[u], (i + (base[jobs.index(job)] // 2 + 1)) * 16 + 1)
                        pool.wait_ge(summed, n * 4 + 5)
                        pool.sem_inc(idle_pool, 1)
                        nc.gpsimd.tensor_copy(w_hi[:, u, 0:job.KB], w[:, u, 0:job.KB]).then_inc(w_hi_done, 1)
                    pool.wait_ge(w_hi_done, n + 2)
                    nc.gpsimd.tensor_tensor(w_lo[:, u, 0:job.KB], w[:, u, 0:job.KB], w_hi[:, u, 0:job.KB], ALU.subtract).then_inc(w_lo_done, 1)

            def low_parts(c, job, i, u, n):
                if beside:
                    for g in range(G):
                        pool.wait_ge(left, n * 4 + (1 + CREDIT + g + 1))
                        nc.gpsimd.tensor_tensor(o_lo[:, g], o_plain[:, g], o_hi[:, g], ALU.subtract).then_inc(lo_ready, 1)

            units(pool, low_parts, split_weights)

        @block.tensor
        def _(pe):
            def unit(c, job, i, u, n):
                xT_hi, xT_lo = job.xT
                KB = job.KB
                if job.kind != "values":
                    pe.wait_ge(w_lo_done, n + 2)
                elif u == 0:
                    pe.wait_ge(w_lo_done, n + 3)
                for g in range(G):
                    pe.wait_ge(left, n * 4 + (g + 2))
                    if job.kind == "values":
                        for h in range(2):
                            t0 = (u * 8 + g * 2 + h) * P
                            terms = [(a, b, k) for a, b in ((xT_hi, w_hi), (xT_lo, w_hi), (xT_hi, w_lo)) for k in range(KB)]
                            for j, (a, b, k) in enumerate(terms):
                                m = nc.tensor.matmul(acc[:, u, g, h * 256:(h + 1) * 256], a[:, k, t0:t0 + P], b[:, :, k],
                                                     start=(j == 0), stop=(j == len(terms) - 1))
                    else:
                        terms = [(a, b, k) for a, b in ((w_hi, xT_hi), (w_lo, xT_hi), (w_hi, xT_lo)) for k in range(KB)]
                        for j, (a, b, k) in enumerate(terms):
                            m = nc.tensor.matmul(acc[:, u, g], a[:, u, k], b[:, k, g * 512:(g + 1) * 512],
                                                 start=(j == 0), stop=(j == len(terms) - 1))
                    m.then_inc(summed, 1)

            units(pe, unit)

        @block.scalar
        def _(act):
            def split_weights(job, i, n):
                if job.kind == "values":
                    for u in range(2):
                        act.wait_ge(w_in[u], (i + (base[jobs.index(job)] // 2 + 1)) * 16 + 1)
                        act.wait_ge(summed, n * 4 + (1 + CREDIT))
                        nc.scalar.activation(w_hi[:, u, 0:job.KB], w[:, u, 0:job.KB], ACT.Copy).then_inc(w_hi_done, 1)

            def unit(c, job, i, u, n):
                each = 32 if job.split else 16
                for g in range(G):
                    act.wait_ge(stored[g], (i * 2 + u) * each + (1 + store_base[c]))
                    act.wait_ge(summed, n * 4 + (1 + CREDIT + g + 1))
                    if job.split:
                        nc.scalar.activation(o_hi[:, g].bitcast(F32R), acc[:, u, g], ACT.Copy, scale=job.scale).then_inc(left_hi, 1)
                        if beside:
                            nc.scalar.activation(o_plain[:, g], acc[:, u, g], ACT.Copy, scale=job.scale).then_inc(left, 1)
                    else:
                        nc.scalar.activation(o_lo[:, g], acc[:, u, g], ACT.Silu).then_inc(left_hi, 1)

            units(act, unit, split_weights)

        @block.vector
        def _(dve):
            if beside:
                beside(st, dve)
                return

            def unit(c, job, i, u, n):
                for g in range(G):
                    if g == 0 and not job.split:
                        dve.wait_ge(left, n * 4 + (1 + CREDIT))
                    dve.wait_ge(left_hi, n * 4 + (g + 2))
                    if job.split:
                        nc.vector.scalar_tensor_tensor(o_lo[:, g], acc[:, u, g], job.scale, o_hi[:, g], ALU.mult, ALU.subtract).then_inc(left, 1)
                    else:
                        dve.sem_inc(left, 1)

            units(dve, unit)


def stage_narrow(nc, sems, ins, hT, ident, widx, cqT, ckvT, kidxT):
    hT_hi, hT_lo = hT
    with Stage(nc, sems, "narrow") as st:
        w = st.sb("w", [P, 2, SMALL], F32)
        w_hi, w_lo = (st.sb(n, [P, KD, SMALL], F32R) for n in ("w_hi", "w_lo"))
        sq = st.sb("sq", [P, QR], F32)
        norm = st.sb("norm", [P, 2, QR + KVR + ID], F32)
        gain = st.sb("gain", [P, 4], F32)
        inv_n = st.sb("inv_n", [P, 3], F32)
        ss, ms, mse, sd, rs = (st.sb(n, [P, 3], F32) for n in ("ss", "ms", "mse", "sd", "rs"))
        o_hi, o_lo = (st.sb(n, [P, 2, 4, P], F32R) for n in ("o_hi", "o_lo"))
        acc = st.ps("acc", [P, 2, 512])
        pt = st.ps("pt", [P, 2, 4, P])
        w_in = [st.sem("w_in0"), st.sem("w_in1")]
        gains_in, consts, w_hi_done, w_lo_done, summed, squared, rooted, inverted, normed, turned, left_hi, left_lo, chain = (
            st.sem(n) for n in ("gains_in", "consts", "w_hi_done", "w_lo_done", "summed", "squared", "rooted", "inverted", "normed",
                                "turned", "left_hi", "left_lo", "chain"))
        stored = [st.sem("stored0"), st.sem("stored1")]
        block = st.block()
        segs = [(0, QR), (QR, QR + KVR), (QR + KVR, QR + KVR + ID)]

        @block.sync
        def _(sp):
            win = ins["a_w_in"][0].rearrange("(k p) n -> k p n", p=P)
            for k in range(KD):
                if k >= 2:
                    sp.wait_ge(w_lo_done, k - 1)
                sp.dma_start(w[:, k % 2], win[k, :, 0:SMALL]).then_inc(w_in[k % 2], 16)
                if k == 1:
                    sp.dma_start(gain[:, 0:2], ins["a_q_norm"][0].rearrange("(k p) -> p k", p=P), allow_slow_non_contiguous=True).then_inc(gains_in, 16)
                    sp.dma_start(gain[:, 2:3], ins["a_kv_norm"].rearrange("o p -> p o"), allow_slow_non_contiguous=True).then_inc(gains_in, 16)
                    sp.dma_start(gain[0:ID, 3:4], ins["a_kidx_norm"].rearrange("o p -> p o"), allow_slow_non_contiguous=True).then_inc(gains_in, 16)
            for tb in range(NB):
                sp.wait_ge(left_lo, 6 * tb + 6)
                cols = slice(tb * P, (tb + 1) * P)
                for part, buf in ((0, o_hi), (1, o_lo)):
                    for j in range(2):
                        sp.dma_start(cqT[part, j * P:(j + 1) * P, cols], buf[:, tb % 2, j].bitcast(F32)).then_inc(stored[tb % 2], 16)
                    sp.dma_start(ckvT[part, :, cols], buf[:, tb % 2, 2].bitcast(F32)).then_inc(stored[tb % 2], 16)
                    sp.dma_start(kidxT[part, :, cols], buf[0:ID, tb % 2, 3].bitcast(F32)).then_inc(stored[tb % 2], 16)
            for u in range(2):
                sp.wait_ge(stored[u], NB // 2 * 128)

        @block.gpsimd
        def _(pool):
            for j, (a, b) in enumerate(segs):
                nc.gpsimd.memset(inv_n[:, j:j + 1], 1.0 / (b - a)).then_inc(consts, 1)
            for k in range(KD):
                pool.wait_ge(w_in[k % 2], 16 * (k // 2 + 1))
                nc.gpsimd.tensor_copy(w_hi[:, k], w[:, k % 2]).then_inc(w_hi_done, 1)
                pool.wait_ge(w_hi_done, k + 1)
                nc.gpsimd.tensor_tensor(w_lo[:, k], w[:, k % 2], w_hi[:, k], ALU.subtract).then_inc(w_lo_done, 1)

        @block.tensor
        def _(pe):
            def project(tb):
                if tb >= 2:
                    pe.wait_ge(normed, 4 * (tb - 1))
                terms = [(a, b, k) for k in range(KD) for a, b in ((hT_hi, w_hi), (hT_lo, w_hi), (hT_hi, w_lo))]
                for n, (a, b, k) in enumerate(terms):
                    if tb == 0 and n % 3 == 0:
                        pe.wait_ge(w_lo_done, k + 1)
                    m = nc.tensor.matmul(acc[:, tb % 2, 0:SMALL], a[:, k, tb * P:(tb + 1) * P], b[:, k],
                                         start=(n == 0), stop=(n == len(terms) - 1))
                m.then_inc(summed, 1)

            def turn(tb):
                pe.wait_ge(normed, 4 * tb + 4)
                if tb >= 2:
                    pe.wait_ge(left_lo, 6 * (tb - 1))
                for j in range(3):
                    nc.tensor.transpose(pt[:, tb % 2, j], norm[:, tb % 2, j * P:(j + 1) * P], ident[:])
                nc.tensor.transpose(pt[0:ID, tb % 2, 3], norm[:, tb % 2, 3 * P:3 * P + ID], ident[:]).then_inc(turned, 1)

            for tb in range(NB):
                project(tb)
                if tb:
                    turn(tb - 1)
            turn(NB - 1)

        parts = [(j, P if j < 3 else ID) for j in range(4)]

        @block.scalar
        def _(act):
            act.wait_ge(gains_in, 48)
            act.wait_ge(consts, 3)

            def leave(tb):
                act.wait_ge(turned, tb + 1)
                if tb >= 2:
                    act.wait_ge(stored[tb % 2], 128 * (tb // 2))
                for j, rows in parts:
                    nc.scalar.activation(o_hi[0:rows, tb % 2, j], pt[0:rows, tb % 2, j], ACT.Copy,
                                         scale=gain[0:rows, j:j + 1]).then_inc(left_hi, 1)

            for tb in range(NB):
                act.wait_ge(summed, tb + 1)
                if tb:
                    act.wait_ge(inverted, tb)
                for j, (a, b) in enumerate(segs):
                    if tb or j:
                        act.wait_ge(squared, 3 * tb + j)
                    nc.scalar.activation(sq[:, 0:b - a], acc[:, tb % 2, a:b], ACT.Square, accum_out=ss[:, j:j + 1]).then_inc(squared, 1)
                act.wait_ge(chain, 2 * tb + 2)
                nc.scalar.activation(sd[:], mse[:], ACT.Sqrt).then_inc(rooted, 1)
                if tb:
                    leave(tb - 1)
            leave(NB - 1)

        @block.vector
        def _(dve):
            dve.wait_ge(gains_in, 48)
            dve.wait_ge(consts, 3)

            def leave(tb):
                dve.wait_ge(left_hi, 4 * tb + 4)
                for j, rows in parts:
                    m = nc.vector.scalar_tensor_tensor(o_lo[0:rows, tb % 2, j], pt[0:rows, tb % 2, j], gain[0:rows, j:j + 1],
                                                       o_hi[0:rows, tb % 2, j], ALU.mult, ALU.subtract)
                    m.then_inc(left_lo, 3 if j == 3 else 1)

            for tb in range(NB):
                dve.wait_ge(squared, 3 * tb + 3)
                nc.vector.tensor_tensor(ms[:], ss[:], inv_n[:], ALU.mult).then_inc(chain, 1)
                dve.wait_ge(chain, 2 * tb + 1)
                nc.vector.tensor_scalar(mse[:], ms[:], EPS, None, ALU.add).then_inc(chain, 1)
                dve.wait_ge(rooted, tb + 1)
                if tb:
                    dve.wait_ge(normed, 4 * tb)
                nc.vector.reciprocal(rs[:], sd[:]).then_inc(inverted, 1)
                dve.wait_ge(inverted, tb + 1)
                if tb >= 2:
                    dve.wait_ge(turned, tb - 1)
                for j, (a, b) in enumerate(segs):
                    nc.vector.tensor_scalar(norm[:, tb % 2, a:b], acc[:, tb % 2, a:b], rs[:, j:j + 1], None, ALU.mult).then_inc(normed, 1)
                nc.vector.tensor_scalar(widx[:, tb], acc[:, tb % 2, SMALL - IH:SMALL], IH ** -0.5 * ID ** -0.5, None,
                                        ALU.mult).then_inc(normed, 1)
                if tb:
                    leave(tb - 1)
            leave(NB - 1)


def near_start(b):
    return max(b - 1, 0) * P


def mask_offset(b):
    return P * sum(i + 1 for i in range(2, b))


def chunks(b):
    n = (b + 1) * P
    return [(c, min(c + 512, n)) for c in range(0, n, 512)]


def quads(b):
    return [(j, min(j + 4, b + 1)) for j in range(0, b + 1, 4)]


SR, TR, OR = 2, 4, 2
LR, LR2 = 4, 2
LAG = 2
PAIR = 2 * P
PAIRS = [1, 3, 5, 7, 6, 4, 2, 0]
ORDER = [2 * r + i for r in PAIRS for i in range(2)]
NCH = [len(chunks(b)) for b in ORDER]
BEFORE = [sum(NCH[:p]) for p in range(NB + 1)]
NPVQ = [(2 * r + 5) // 4 for r in PAIRS]
PV_BEFORE = [sum(NPVQ[:r]) for r in range(len(PAIRS) + 1)]
READERS = [[place for place, r in enumerate(PAIRS) if NPVQ[place] > c] for c in range(G)]


def pieces(b, i):
    a, z = chunks(b)[i]
    ns = near_start(b)
    return ([(a, min(z, ns), False)] if a < ns else []) + ([(max(a, ns), z, True)] if z > ns else [])


def stage_attention(nc, sems, name, heads, M, ident, bias_dram, q_dram, k_dram, v_dram, o_dram, sums, mask=None, neglam=None):
    V2 = M == 1
    width = HD if V2 else P
    NCHUNK = M * BEFORE[NB]
    NQUAD = BEFORE[NB]
    NPV = PV_BEFORE[-1]
    NPAIR = len(PAIRS)
    TAIL = LAG + 3
    BEHIND = 2 if V2 else 1
    SPLIT = [sum(1 for i in range(NCH[p]) if len(pieces(ORDER[p], i)) == 2) for p in range(NB)]
    NSPLIT = M * sum(SPLIT)
    assert NCHUNK % SR == 0 and NQUAD % TR == 0 and NB % LR == 0
    with_mask = lambda p: V2 and ORDER[p] >= 2
    NMASKED = [sum(with_mask(x) for x in range(p)) for p in range(NB + 1)]
    NM = 4

    with Stage(nc, sems, name) as st:
        q = st.sb("q", [P, 2, M, 2, PAIR], F32R)
        k = st.sb("k", [P, 2, M, T], F32R)
        v = st.sb("v", [P, 1 if V2 else 2, NB, P], F32R)
        near, near_next = (st.sb(n, [P, M, NEAR], F32) for n in ("near", "near_next"))
        near_mask = st.sb("near_mask", [P, NM, NEAR], F32) if V2 else None
        lg = st.sb("lg", [P, LR, T], F32)
        lg2 = st.sb("lg2", [P, LR2, T], F32) if M == 2 else None
        pT_hi, pT_lo = (st.sb(n, [P, 2, NB, PAIR], F32R) for n in ("pT_hi", "pT_lo"))
        o_sb = st.sb("o_sb", [P, OR, PAIR], F32)
        o_half = st.sb("o_half", [HD, OR, PAIR], F32) if V2 else None
        mx = st.sb("mx", [P, NB, M, 8], F32)
        negm = st.sb("negm", [P, NB, M], F32)
        rec, ratio = (st.sb(n, [P, NB], F32) if M == 2 else None for n in ("rec", "ratio"))
        s_ps, t_ps, o_ps = st.ps("s", [P, SR, 512]), st.ps("t", [P, TR, 4, P]), st.ps("o", [P, OR, 512])
        k_in, near_in, near_done, s_done, s_left, dve_chain, max_done, exp_done, mixed, mix_chain, turned, t_hi, t_lo, pv_quad, half_done, o_left, masked, mx_set = (
            st.sem(n) for n in ("k_in", "near_in", "near_done", "s_done", "s_left", "dve_chain", "max_done", "exp_done", "mixed", "mix_chain",
                                "turned", "t_hi", "t_lo", "pv_quad", "half_done", "o_left", "masked", "mx_set"))
        q_in, v_in, o_stored = ([st.sem(f"{n}{u}") for u in range(c)] for n, c in (("q_in", 2), ("v_in", 4), ("o_stored", 2)))
        idle_sp, idle_dve, idle_pool = st.sem("idle_sp"), st.sem("idle_dve"), st.sem("idle_pool")
        block = st.block()
        chunk_no = lambda p, i, m: M * (BEFORE[p] + i) + m

        def values_here(p):
            r, late = divmod(p - LAG - 2, 2)
            if not 0 <= r < NPAIR:
                return []
            last = r == NPAIR - 1
            return [(r, c) for c in range(NPVQ[r]) if (last and not late) or (not last and (c >= NPVQ[r] // 2) == bool(late))]

        outputs_here = lambda p: [r for r in range(NPAIR) if p - LAG == 2 * r + 4]

        def walk(engine, place):
            for p in range(TAIL):
                place(0, p, None)
            with engine.Fori(0, heads - 1) as h:
                for p in range(TAIL, NB):
                    place(h, p, None)
                for p in range(TAIL):
                    place(h + 1, p, h)
            for p in range(TAIL, NB):
                place(heads - 1, p, None)
            for p in range(TAIL):
                place(None, p, heads - 1)

        def both(h, p, before):
            return ([(before, NB + p)] if before is not None else []) + ([(h, p)] if h is not None else [])

        @block.sync
        def _(sp):
            def load_q(h, r):
                cols = slice(PAIRS[r] * PAIR, (PAIRS[r] + 1) * PAIR)
                for m in range(M):
                    rows = ds((h * M + m) * HD, HD)
                    sp.dma_start(q[:, r % 2, m, 0].bitcast(F32), q_dram[0:2, rows, cols]).then_inc(q_in[r % 2], 16)
                    for part in range(2):
                        sp.dma_start(q[(1 - part) * HD:(2 - part) * HD, r % 2, m, 1].bitcast(F32), q_dram[part, rows, cols]).then_inc(q_in[r % 2], 16)

            def load_k(h):
                for m in range(M):
                    dst = k[:, ds(h % 2, 1), m].rearrange("p o t -> p (o t)")
                    sp.dma_start(dst.bitcast(F32), k_dram[0:2, ds((h * M + m) * HD, HD), :]).then_inc(k_in, 16)

            def load_near(h):
                for m in range(M):
                    sp.dma_start(near_next[:, m], bass.AP(bias_dram.tensor, (h * M + m) * (P * 384) + P - 1, [[383, P], [1, NEAR]])).then_inc(near_in, 16)

            def load_v(h, c):
                for part in range(2):
                    dst = v[:, 0, 4 * c:4 * c + 4, part * HD:(part + 1) * HD] if V2 else v[:, part, 4 * c:4 * c + 4]
                    sp.dma_start(dst.bitcast(F32), v_dram[part, c * 512:(c + 1) * 512].rearrange("(j p) e -> p j e", p=P)[:, :, ds(h * width, width)]
                                 ).then_inc(v_in[c], 16)

            def store(h, r):
                sp.wait_ge(o_left, OR + h * NPAIR + r + 1)
                sp.sem_inc(idle_sp, 1)
                cols = slice(PAIRS[r] * PAIR, (PAIRS[r] + 1) * PAIR)
                sp.dma_start(o_dram[ds(h * width, width), cols], o_sb[0:width, r % 2]).then_inc(o_stored[r % 2], 16)

            def step(h, r, before, following):
                if h is not None:
                    sp.wait_ge(s_done, h * NCHUNK + M * BEFORE[2 * r + 2])
                    sp.sem_inc(idle_sp, 1)
                    if r + 2 < NPAIR:
                        load_q(h, r + 2)
                    elif following is not None:
                        load_q(following, r + 2 - NPAIR)
                if r == 0 and h is not None:
                    if following is not None:
                        load_k(following)
                    sp.wait_ge(near_done, h + 1)
                    sp.sem_inc(idle_sp, 1)
                    load_near(h if following is None else following)
                for head, next_head, n in ((before, h, r + NPAIR), (h, following, r)):
                    for c in range(G):
                        if head is not None and next_head is not None and n - 2 == READERS[c][-1]:
                            sp.wait_ge(pv_quad, NPV + head * NPV + PV_BEFORE[n - 1])
                            sp.sem_inc(idle_sp, 1)
                            load_v(next_head, c)
                    if head is not None and 0 <= n - 3 < NPAIR:
                        store(head, n - 3)

            load_q(0, 0)
            load_k(0)
            load_near(0)
            load_q(0, 1)
            for c in range(4):
                load_v(0, c)
            for r in range(3):
                step(0, r, None, 1)
            with sp.Fori(0, heads - 2) as h:
                for r in range(3, NPAIR):
                    step(h, r, None, h + 1)
                for r in range(3):
                    step(h + 1, r, h, h + 2)
            for r in range(3, NPAIR):
                step(heads - 2, r, None, heads - 1)
            for r in range(3):
                step(heads - 1, r, heads - 2, None)
            for r in range(3, NPAIR):
                step(heads - 1, r, None, None)
            for r in range(3):
                step(None, r, heads - 1, None)
            for u in range(2):
                sp.wait_ge(o_stored[u], 1 + heads * NPAIR // 2 * 16)
            sp.wait_ge(near_in, (heads + 1) * 16 * M)

        if V2:
            @block.gpsimd
            def _(pool):
                with pool.Fori(0, heads) as h:
                    pool.wait_ge(near_done, h + 1)
                    for p in range(NB):
                        if with_mask(p):
                            n, b = NMASKED[p], ORDER[p]
                            used = [x for x in range(p) if with_mask(x) and NMASKED[x] == n - NM]
                            if used:
                                pool.wait_ge(s_left, SR + h * NCHUNK + BEFORE[used[0] + 1])
                            pool.sem_inc(idle_pool, 1)
                            o = mask_offset(b) + near_start(b)
                            nc.gpsimd.tensor_tensor(near_mask[:, n % NM], near[:, 0], mask[:, o:o + NEAR], ALU.add).then_inc(masked, 1)

        @block.tensor
        def _(pe):
            pe.sem_inc(s_left, SR)
            pe.sem_inc(t_lo, TR)
            pe.sem_inc(o_left, OR)

            def logits(h, p, i):
                b, (a, z) = ORDER[p], chunks(ORDER[p])[i]
                if i == 0 and p % 2 == 0:
                    pe.wait_ge(q_in[p // 2 % 2], h * (4 * 48 * M) + (p // 4 + 1) * 48 * M)
                for m in range(M):
                    n = chunk_no(p, i, m)
                    out, cols = s_ps[:, n % SR, 0:z - a], slice((b % 2) * P, (b % 2 + 1) * P)
                    keys = k[:, ds(h % 2, 1), m, a:z].rearrange("p o t -> p (o t)")
                    pe.wait_ge(s_left, h * NCHUNK + n + 1)
                    nc.tensor.matmul(out, q[:, p // 2 % 2, m, 0, cols], keys, start=True, stop=False)
                    nc.tensor.matmul(out, q[:, p // 2 % 2, m, 1, cols], keys, start=False, stop=True).then_inc(s_done, 1)

            def turn(h, p, i):
                n, (a, z) = BEFORE[p] + i, quads(ORDER[p])[i]
                if i == 0 and M == 2:
                    pe.wait_ge(mixed, LR2 + h * NB + p + 1)
                elif i == 0:
                    pe.wait_ge(exp_done, h * NB + p + 1)
                pe.wait_ge(t_lo, h * NQUAD + n + 1)
                for j in range(a, z):
                    x = nc.tensor.transpose(t_ps[:, n % TR, j - a], lg[:, p % LR, j * P:(j + 1) * P], ident[:])
                x.then_inc(turned, 1)

            def values(h, r, c):
                last = 2 * PAIRS[r] + 1
                if c == 0:
                    pe.wait_ge(o_left, h * NPAIR + r + 1)
                if r == READERS[c][0]:
                    pe.wait_ge(v_in[c], h * 32 + 32)
                pe.wait_ge(t_lo, TR + h * NQUAD + BEFORE[2 * r + 1] + c + 1)
                terms = [(0, pT_hi), (0, pT_lo)] if V2 else [(0, pT_hi), (0, pT_lo), (1, pT_hi)]
                for j in range(4 * c, min(4 * c + 4, last + 1)):
                    a = P if j == last else 0
                    for i, (part, pT) in enumerate(terms):
                        x = nc.tensor.matmul(o_ps[:, r % 2, a:PAIR], v[:, part, j], pT[:, r % 2, j, a:PAIR],
                                             start=(j == 0 and i == 0), stop=(j == last and i == len(terms) - 1))
                x.then_inc(pv_quad, 1)

            def place(h, p, before):
                if h is not None and p == 0:
                    pe.wait_ge(k_in, h * 16 * M + 16 * M)
                    logits(h, 0, 0)
                back, t = (h, p - LAG) if p >= LAG else (before, NB + p - LAG)
                for i in range(4):
                    if h is not None and 1 <= i < NCH[p]:
                        logits(h, p, i)
                    if back is not None and 0 <= t < NB and i < NCH[t]:
                        turn(back, t, i)
                if h is not None and p + 1 < NB:
                    logits(h, p + 1, 0)
                for head, x in both(h, p, before):
                    for r, c in values_here(x):
                        values(head, r, c)

            walk(pe, place)

        @block.vector
        def _(dve):
            dve.sem_inc(turned, NQUAD)
            dve.sem_inc(mixed, LR2)
            dve.sem_inc(dve_chain, 1)
            for u in range(2):
                dve.sem_inc(o_stored[u], 1)

            def logits(h, p, i, m):
                b, n, c0 = ORDER[p], chunk_no(p, i, m), i * 512
                dst, slot, top = (lg, p % LR, mx[:, p, m]) if m == 0 else (lg2, p % LR2, mx[:, p, m])
                if i == 0 and m == 0:
                    dve.wait_ge(turned, h * NQUAD + (NQUAD + BEFORE[p - LR + 1] if p >= LR else BEFORE[NB - LR + p + 1]))
                elif i == 0:
                    dve.wait_ge(mixed, h * NB + p + 1)
                if i == 0 and p == 0:
                    dve.wait_ge(near_done, h + 1)
                dve.wait_ge(s_done, h * NCHUNK + n + 1)
                for a, z, is_near in pieces(b, i):
                    src, out = s_ps[:, n % SR, a - c0:z - c0], dst[:, slot, a:z]
                    col = 2 * i + is_near
                    ends = z == chunks(b)[i][1]
                    tab = None
                    if is_near:
                        off = P * (1 - b)
                        tab = near[:, m, a + off:z + off]
                        if with_mask(p):
                            dve.wait_ge(masked, h * NMASKED[NB] + NMASKED[p] + 1)
                            tab = near_mask[:, NMASKED[p] % NM, a + off:z + off]
                    elif V2:
                        tab = mask[:, mask_offset(b) + a:mask_offset(b) + z]
                    if tab is not None:
                        dve.sem_inc(idle_dve, 1)
                        x = nc.vector.tensor_tensor_reduce(out, src, tab, 1.0, 2 * NEG, ALU.add, ALU.max, top[:, col:col + 1])
                    else:
                        x = nc.vector.tensor_scalar(out, src, 1.0, 2 * NEG, ALU.mult, ALU.max, accum_out=top[:, col:col + 1])
                    x.then_inc(s_left if ends else dve_chain, 1)

            def maximum(h, p):
                dve.wait_ge(s_left, SR + h * NCHUNK + M * BEFORE[p + 1])
                dve.wait_ge(dve_chain, 1 + h * NSPLIT + M * sum(SPLIT[:p + 1]))
                nc.vector.tensor_reduce(negm[:, p], mx[:, p], AX.X, ALU.max, negate=True).then_inc(max_done, 1)

            def invert(h, p):
                dve.wait_ge(exp_done, h * 2 * NB + 2 * p + 2)
                nc.vector.reciprocal(rec[:, p:p + 1], sums[:, ORDER[p], ds(h * 2 + 1, 1)]).then_inc(mix_chain, 1)

            def mix(h, p):
                n, l1 = (ORDER[p] + 1) * P, sums[:, ORDER[p], ds(h * 2, 1)]
                dve.wait_ge(mix_chain, h * (2 * NB) + 2 * p + 1)
                nc.vector.scalar_tensor_tensor(ratio[:, p:p + 1], l1, rec[:, p:p + 1], neglam[:], ALU.mult, ALU.mult).then_inc(mix_chain, 1)
                dve.wait_ge(mix_chain, h * (2 * NB) + 2 * p + 2)
                nc.vector.scalar_tensor_tensor(lg[:, p % LR, 0:n], lg2[:, p % LR2, 0:n], ratio[:, p:p + 1], lg[:, p % LR, 0:n],
                                               ALU.mult, ALU.add).then_inc(mixed, 1)

            def split_lo(h, p, i):
                n, (a, z), c = BEFORE[p] + i, quads(ORDER[p])[i], (ORDER[p] % 2) * P
                dve.wait_ge(t_hi, h * NQUAD + n + 1)
                nc.vector.tensor_tensor(pT_lo[:, p // 2 % 2, a:z, c:c + P], t_ps[:, n % TR, 0:z - a], pT_hi[:, p // 2 % 2, a:z, c:c + P],
                                        ALU.subtract).then_inc(t_lo, 1)

            def output(h, r):
                if V2:
                    dve.wait_ge(half_done, h * NPAIR + r + 1)
                    dve.wait_ge(o_stored[r % 2], 1 + h * (NPAIR // 2 * 16) + (r // 2) * 16)
                    nc.vector.tensor_tensor(o_sb[0:HD, r % 2], o_ps[0:HD, r % 2, 0:PAIR], o_half[:, r % 2], ALU.add).then_inc(o_left, 1)

            nc.vector.memset(mx[:], 2 * NEG).then_inc(mx_set, 1)
            dve.wait_ge(mx_set, 1)
            def place(h, p, before):
                back, t = (h, p - LAG) if p >= LAG else (before, NB + p - LAG)
                for i in range(4 + BEHIND):
                    if h is not None and i < NCH[p]:
                        for m in range(M):
                            logits(h, p, i, m)
                    if back is not None and 0 <= t < NB and BEHIND <= i < NCH[t] + BEHIND:
                        split_lo(back, t, i - BEHIND)
                if M == 2:
                    for head, x in both(h, p, before):
                        if 1 <= x <= NB:
                            invert(head, x - 1)
                if h is not None:
                    maximum(h, p)
                for head, x in both(h, p, before):
                    for r in outputs_here(x):
                        output(head, r)
                    if M == 2 and 1 <= x <= NB:
                        mix(head, x - 1)

            walk(dve, place)

        @block.scalar
        def _(act):
            act.sem_inc(pv_quad, NPV)

            def copy_near(h):
                nc.scalar.activation(near[:], near_next[:], ACT.Copy).then_inc(near_done, 1)

            def exps(h, p, m):
                b, n = ORDER[p], (ORDER[p] + 1) * P
                buf = lg[:, p % LR, 0:n] if m == 0 else lg2[:, p % LR2, 0:n]
                if m == 0:
                    act.wait_ge(max_done, h * NB + p + 1)
                nc.scalar.activation(buf, buf, ACT.Exp, bias=negm[:, p, m:m + 1], accum_out=sums[:, b, ds(h * M + m, 1)]).then_inc(exp_done, 1)

            def split_hi(h, p, i):
                n, (a, z), c, r = BEFORE[p] + i, quads(ORDER[p])[i], (ORDER[p] % 2) * P, p // 2
                act.wait_ge(turned, NQUAD + h * NQUAD + n + 1)
                if i == 0 and p % 2 == 0:
                    act.wait_ge(pv_quad, h * NPV + (NPV + PV_BEFORE[r - 1] if r >= 2 else PV_BEFORE[NPAIR + r - 1]))
                nc.scalar.activation(pT_hi[:, r % 2, a:z, c:c + P], t_ps[:, n % TR, 0:z - a], ACT.Copy).then_inc(t_hi, 1)

            def output(h, r):
                act.wait_ge(pv_quad, NPV + h * NPV + PV_BEFORE[r + 1])
                if V2:
                    act.wait_ge(o_left, h * NPAIR + r + 1)
                    nc.scalar.activation(o_half[:, r % 2], o_ps[HD:P, r % 2, 0:PAIR], ACT.Copy).then_inc(half_done, 1)
                else:
                    act.wait_ge(o_stored[r % 2], 1 + h * (NPAIR // 2 * 16) + (r // 2) * 16)
                    nc.scalar.activation(o_sb[:, r % 2], o_ps[:, r % 2, 0:PAIR], ACT.Copy).then_inc(o_left, 1)

            act.wait_ge(near_in, 16 * M)
            copy_near(0)
            def place(h, p, before):
                back, t = (h, p - LAG) if p >= LAG else (before, NB + p - LAG)
                for head, x in both(h, p, before):
                    if 1 <= x <= NB:
                        for m in range(M):
                            exps(head, x - 1, m)
                    if x == NB:
                        act.wait_ge(near_in, head * 16 * M + 32 * M)
                        copy_near(head)
                for i in range(4):
                    if back is not None and 0 <= t < NB and i < NCH[t]:
                        split_hi(back, t, i)
                for head, x in both(h, p, before):
                    for r in outputs_here(x):
                        output(head, r)

            walk(act, place)


SELECTING = range(2, NB)
KEYS = mask_offset(NB)


def stage_score(nc, sems, widx, qidx, kidxT, k_up, k_down):
    with Stage(nc, sems, "score") as st:
        k_hh, k_ll = (st.sb(n, [P, T], F32R) for n in ("k_hh", "k_ll"))
        q = st.sb("q", [P, 2, IH, P], F32R)
        relu = st.sb("relu", [P, 2, T], F32)
        score = st.sb("score", [P, T], F32)
        causal = st.sb("causal", [P, P], F32)
        flip = st.sb("flip", [P, T], I32)
        key = st.sb("key", [P, 2, T], I32)
        s_ps = st.ps("s", [P, 2, 4 * 512])
        k_in, scored, relued, summed, keyed, packed, causal_step, chain = (
            st.sem(n) for n in ("k_in", "scored", "relued", "summed", "keyed", "packed", "causal_step", "chain"))
        q_in = [st.sem("q_in0"), st.sem("q_in1")]
        units = [(i, b, h) for i, b in enumerate(SELECTING) for h in range(IH)]
        block = st.block()

        @block.sync
        def _(sp):
            for part in range(2):
                rows = slice(part * ID, (part + 1) * ID)
                sp.dma_start(k_hh[rows].bitcast(F32), kidxT[0]).then_inc(k_in, 16)
                sp.dma_start(k_ll[rows].bitcast(F32), kidxT[1]).then_inc(k_in, 16)
            for i, b in enumerate(SELECTING):
                if i >= 2:
                    sp.wait_ge(scored, IH * (i - 1))
                for part in range(2):
                    sp.dma_start(q[part * ID:(part + 1) * ID, i % 2].bitcast(F32),
                                 qidx[part].rearrange("(h d) t -> d h t", d=ID)[:, :, b * P:(b + 1) * P]).then_inc(q_in[i % 2], 16)

        @block.gpsimd
        def _(pool):
            nc.gpsimd.memset(causal[:], 0.0).then_inc(causal_step, 1)
            pool.wait_ge(causal_step, 1)
            nc.gpsimd.affine_select(out=causal[:], in_=causal[:], compare_op=ALU.is_ge, fill=LOWEST, base=0,
                                    pattern=[[-1, P]], channel_multiplier=1).then_inc(causal_step, 1)

        @block.tensor
        def _(pe):
            pe.wait_ge(k_in, 64)
            for n, (i, b, h) in enumerate(units):
                if h == 0:
                    pe.wait_ge(q_in[i % 2], 32 * (i // 2 + 1))
                if n >= 2:
                    pe.wait_ge(relued, n - 1)
                for a, z in chunks(b):
                    out = s_ps[:, n % 2, a:z]
                    nc.tensor.matmul(out, q[:, i % 2, h], k_hh[:, a:z], start=True, stop=False)
                    x = nc.tensor.matmul(out, q[:, i % 2, h], k_ll[:, a:z], start=False, stop=True)
                x.then_inc(scored, 1)

        @block.scalar
        def _(act):
            def pack(i):
                b = SELECTING[i]
                n, o = (b + 1) * P, mask_offset(b)
                act.wait_ge(keyed, i + 1)
                halves = key[:, i % 2].bitcast(U16).rearrange("p (s two) -> p s two", two=2)
                nc.scalar.activation(k_up[:, o:o + n], halves[:, 0:n, 1], ACT.Copy).then_inc(packed, 1)
                nc.scalar.activation(k_down[:, o:o + n], halves[:, 0:n, 0], ACT.Copy).then_inc(packed, 1)

            for n, (i, b, h) in enumerate(units):
                act.wait_ge(scored, n + 1)
                if n >= 2:
                    act.wait_ge(summed, n - 1)
                nc.scalar.activation(relu[:, n % 2, 0:(b + 1) * P], s_ps[:, n % 2, 0:(b + 1) * P], ACT.Relu).then_inc(relued, 1)
                if h == 3 and i:
                    pack(i - 1)
            pack(len(SELECTING) - 1)

        @block.vector
        def _(dve):
            done = [0]

            def step(x):
                x.then_inc(chain, 1)
                done[0] += 1
                dve.wait_ge(chain, done[0])

            for n, (i, b, h) in enumerate(units):
                w, N = widx[:, b, h:h + 1], (b + 1) * P
                dve.wait_ge(relued, n + 1)
                if n:
                    dve.wait_ge(summed, n)
                if h == 0:
                    if i:
                        dve.wait_ge(keyed, i)
                    nc.vector.tensor_scalar(score[:, 0:N], relu[:, n % 2, 0:N], w, 0.0, ALU.mult, ALU.add).then_inc(summed, 1)
                else:
                    nc.vector.scalar_tensor_tensor(score[:, 0:N], relu[:, n % 2, 0:N], w, score[:, 0:N], ALU.mult, ALU.add).then_inc(summed, 1)
                if h == IH - 1:
                    dve.wait_ge(causal_step, 2)
                    dve.wait_ge(summed, n + 1)
                    step(nc.vector.tensor_tensor(score[:, N - P:N], score[:, N - P:N], causal[:], ALU.add))
                    step(nc.vector.tensor_scalar(flip[:, 0:N], score[:, 0:N].bitcast(I32), 31, -2 ** 31, ALU.arith_shift_right, ALU.bitwise_or))
                    if i >= 2:
                        dve.wait_ge(packed, 2 * (i - 1))
                    nc.vector.tensor_tensor(key[:, i % 2, 0:N], score[:, 0:N].bitcast(I32), flip[:, 0:N], ALU.bitwise_xor).then_inc(keyed, 1)


class Selection:

    def __init__(self, sb, k_up, k_down, mask):
        self.k_up, self.k_down, self.mask = k_up, k_down, mask
        NS = len(SELECTING)
        self.cand, self.cnt, self.need, self.ge, self.moved, self.top, self.low = (
            sb(n, [P, NS], F32) for n in ("cand", "cnt", "need", "ge", "moved", "top", "low"))
        self.bit, self.half = sb("bit", [P, 1], F32), sb("half", [P, 1], F32)
        self.cols = [(i, mask_offset(b), (b + 1) * P) for i, b in enumerate(SELECTING)]

    def upper(self, nc, dve, chain, counted):
        k_up, k_down, cand, cnt, need, ge, moved, bit, half, top = (
            self.k_up, self.k_down, self.cand, self.cnt, self.need, self.ge, self.moved, self.bit, self.half, self.top)
        NS, done = len(SELECTING), [0]

        def step(x):
            x.then_inc(chain, 1)
            done[0] += 1
            dve.wait_ge(chain, done[0])

        def count(op, against):
            for i, o, N in self.cols:
                nc.vector.tensor_scalar(self.mask[:, o:o + N], k_up[:, o:o + N], against[:, i:i + 1], 0.0, op, ALU.add,
                                        accum_out=cnt[:, i:i + 1]).then_inc(counted, 1)

        step(nc.vector.memset(need[:], float(TOPK)))
        step(nc.vector.memset(cand[:], 32768.0))
        step(nc.vector.memset(bit[:], 32768.0))
        step(nc.vector.memset(half[:], 16384.0))
        c0 = done[0]
        with dve.Fori(0, STEPS) as s:
            count(ALU.is_ge, cand)
            dve.wait_ge(counted, s * NS + NS)
            nc.vector.tensor_tensor(ge[:], cnt[:], need[:], ALU.is_ge).then_inc(chain, 1)
            dve.wait_ge(chain, s * 4 + (c0 + 1))
            nc.vector.scalar_tensor_tensor(moved[:], ge[:], bit[:], cand[:], ALU.mult, ALU.add).then_inc(chain, 1)
            dve.wait_ge(chain, s * 4 + (c0 + 2))
            nc.vector.tensor_scalar(cand[:], moved[:], half[:], None, ALU.subtract).then_inc(chain, 1)
            nc.vector.tensor_scalar(bit[:], bit[:], 0.5, None, ALU.mult).then_inc(chain, 1)
            dve.wait_ge(chain, s * 4 + (c0 + 4))
            nc.vector.tensor_scalar(half[:], half[:], 0.5, None, ALU.mult).then_inc(self.halved, 1)
            dve.wait_ge(self.halved, s + 1)
        done[0] += STEPS * 4
        step(nc.vector.tensor_scalar(top[:], cand[:], 0.5, None, ALU.subtract))
        count(ALU.is_gt, top)
        dve.wait_ge(counted, (STEPS + 1) * NS)
        step(nc.vector.tensor_scalar(need[:], cnt[:], -1.0, float(TOPK), ALU.mult, ALU.add))
        for i, o, N in self.cols:
            nc.vector.scalar_tensor_tensor(k_down[:, o:o + N], k_up[:, o:o + N], top[:, i:i + 1], k_down[:, o:o + N],
                                           ALU.is_equal, ALU.mult).then_inc(chain, 1)


STEPS = 16
BY_ACT = range(len(SELECTING) - 3, len(SELECTING))


def stage_search_lower(nc, sems, ins, search, modulation, ada, gp_dram):
    k_down, mask, cnt, need, ge, moved, low, cols = (
        search.k_down, search.mask, search.cnt, search.need, search.ge, search.moved, search.low, search.cols)
    NS, NA = len(SELECTING), len(BY_ACT)
    with Stage(nc, sems, "search_lower") as st:
        cand, minus, enough, factor, offset = (st.sb(n, [P, NS], F32) for n in ("cand", "minus", "enough", "factor", "offset"))
        bit, half = st.sb("bit", [P, 1], F32), st.sb("half", [P, 1], F32)
        w = st.sb("w", [P, 2, KD, 512], F32)
        postg, bgate, gp = (st.sb(n, [P, D], F32) for n in ("postg", "bgate", "gp"))
        scale = st.sb("scale", [P, KD], F32)
        pcol, pgate = st.ps("pcol", [P, 512]), st.ps("pgate", [P, 2, 2, 512])
        halved, set_up, counted, counted_act, chain, cand_ready, w_used, gate_in, gate_step, stored, columns_done = (
            st.sem(n) for n in ("halved", "set_up", "counted", "counted_act", "chain", "cand_ready", "w_used", "gate_in", "gate_step", "stored", "columns_done"))
        w_in = [st.sem("w_in0"), st.sem("w_in1")]
        block = st.block()

        @block.sync
        def _(sp):
            modulation.load(sp, w, w_in, w_used, ins["mod_w"], LATE)
            for l in range(2):
                if l:
                    sp.wait_ge(gate_step, 2)
                sp.dma_start(postg[:], ins["post_g"][l].partition_broadcast(P)).then_inc(gate_in, 16)
                sp.dma_start(bgate[:], ins["mod_b"][l, 2 * D:3 * D].partition_broadcast(P)).then_inc(gate_in, 16)
                sp.wait_ge(gate_step, 2 * l + 2)
                sp.dma_start(gp_dram[l], gp[:]).then_inc(stored, 16)
            sp.wait_ge(stored, 32)

        @block.tensor
        def _(pe):
            modulation.multiply(nc, pe, w, w_in, w_used, LATE, pcol, pgate)

        @block.scalar
        def _(act):
            with act.Fori(0, STEPS) as s:
                act.wait_ge(cand_ready, s + 1)
                for i in BY_ACT:
                    _, o, N = cols[i]
                    nc.scalar.activation(mask[:, o:o + N], k_down[:, o:o + N], ACT.Sign, bias=minus[:, i:i + 1],
                                         accum_out=cnt[:, i:i + 1]).then_inc(counted_act, 1)

        @block.vector
        def _(dve):
            nc.vector.memset(cand[:], 32768.0).then_inc(set_up, 1)
            nc.vector.memset(bit[:], 32768.0).then_inc(set_up, 1)
            nc.vector.memset(half[:], 16384.0).then_inc(set_up, 1)
            nc.vector.memset(factor[:], 1.0).then_inc(set_up, 1)
            nc.vector.memset(offset[:], 0.0).then_inc(set_up, 1)
            nc.vector.memset(minus[:], 0.5 - 32768.0).then_inc(cand_ready, 1)
            dve.wait_ge(set_up, 5)
            nc.vector.memset(factor[:, BY_ACT[0]:], 2.0).then_inc(set_up, 1)
            for i in BY_ACT:
                nc.vector.memset(offset[:, i:i + 1], -float(cols[i][2])).then_inc(set_up, 1)
            dve.wait_ge(set_up, 6 + NA)
            nc.vector.tensor_tensor(enough[:], need[:], factor[:], ALU.mult).then_inc(set_up, 1)
            dve.wait_ge(set_up, 7 + NA)
            nc.vector.tensor_tensor(enough[:], enough[:], offset[:], ALU.add).then_inc(set_up, 1)
            dve.wait_ge(set_up, 8 + NA)
            with dve.Fori(0, STEPS) as s:
                for i, o, N in cols:
                    if i not in BY_ACT:
                        nc.vector.tensor_scalar(mask[:, o:o + N], k_down[:, o:o + N], cand[:, i:i + 1], 0.0, ALU.is_ge, ALU.add,
                                                accum_out=cnt[:, i:i + 1]).then_inc(counted, 1)
                dve.wait_ge(counted, s * (NS - NA) + (NS - NA))
                dve.wait_ge(counted_act, s * NA + NA)
                nc.vector.tensor_tensor(ge[:], cnt[:], enough[:], ALU.is_ge).then_inc(chain, 1)
                dve.wait_ge(chain, s * 4 + 1)
                nc.vector.scalar_tensor_tensor(moved[:], ge[:], bit[:], cand[:], ALU.mult, ALU.add).then_inc(chain, 1)
                dve.wait_ge(chain, s * 4 + 2)
                nc.vector.tensor_scalar(cand[:], moved[:], half[:], None, ALU.subtract).then_inc(chain, 1)
                nc.vector.tensor_scalar(bit[:], bit[:], 0.5, None, ALU.mult).then_inc(chain, 1)
                dve.wait_ge(chain, s * 4 + 4)
                nc.vector.tensor_scalar(half[:], half[:], 0.5, None, ALU.mult).then_inc(halved, 1)
                nc.vector.tensor_scalar(minus[:], cand[:], -1.0, 0.5, ALU.mult, ALU.add).then_inc(cand_ready, 1)
                dve.wait_ge(halved, s + 1)
            nc.vector.tensor_scalar(low[:], cand[:], 0.5, None, ALU.subtract).then_inc(set_up, 1)
            dve.wait_ge(w_used, len(LATE))
            for l in range(2):
                dve.wait_ge(gate_in, 32 * l + 32)
                if l:
                    dve.wait_ge(stored, 16)
                nc.vector.tensor_tensor(gp[:], pgate[:, l].rearrange("p a b -> p (a b)"), bgate[:], ALU.add).then_inc(gate_step, 1)
                dve.wait_ge(gate_step, 2 * l + 1)
                nc.vector.tensor_tensor(gp[:], gp[:], postg[:], ALU.mult).then_inc(gate_step, 1)
            modulation.finish_columns(nc, dve, 1, pcol, ada, scale, columns_done)


def stage_mask(nc, sems, search):
    k_up, k_down, top, low, mask = search.k_up, search.k_down, search.top, search.low, search.mask
    NS = len(SELECTING)
    with Stage(nc, sems, "mask") as st:
        neg_top = st.sb("neg_top", [P, NS], F32)
        up_dist, dist, rank = (st.sb(n, [P, 2, T], F32) for n in ("up_dist", "dist", "rank"))
        above, equal, taken, kept = (st.sb(n, [P, 2, T], BF16) for n in ("above", "equal", "taken", "kept"))
        cnt, need = (st.sb(n, [P, NS], F32) for n in ("cnt", "need"))
        negated, scaled, measured, counted, equal_done, need_done, ranked, taken_done, kept_done, masked = (
            st.sem(n) for n in ("negated", "scaled", "measured", "counted", "equal_done", "need_done", "ranked", "taken_done", "kept_done", "masked"))
        block = st.block()

        @block.scalar
        def _(act):
            act.wait_ge(negated, 1)
            def mask_out(i):
                _, o, N = search.cols[i]
                act.wait_ge(kept_done, i + 1)
                nc.scalar.activation(mask[:, o:o + N], kept[:, i % 2, 0:N], ACT.Copy, scale=-NEG, bias=NEG).then_inc(masked, 1)

            for i, o, N in search.cols:
                if i >= 2:
                    act.wait_ge(measured, i - 1)
                nc.scalar.activation(up_dist[:, i % 2, 0:N], k_up[:, o:o + N], ACT.Identity, scale=131072.0, bias=neg_top[:, i:i + 1]).then_inc(scaled, 1)
                if i:
                    mask_out(i - 1)
            mask_out(NS - 1)

        @block.vector
        def _(dve):
            nc.vector.tensor_scalar(neg_top[:], top[:], -131072.0, None, ALU.mult).then_inc(negated, 1)

            def measure(i, o, N):
                h = i % 2
                dve.wait_ge(scaled, i + 1)
                if i >= 2:
                    dve.wait_ge(equal_done, i - 1)
                    dve.wait_ge(counted, i - 1)
                nc.vector.scalar_tensor_tensor(dist[:, h, 0:N], k_down[:, o:o + N], low[:, i:i + 1], up_dist[:, h, 0:N],
                                               ALU.subtract, ALU.add).then_inc(measured, 1)

            def compare(i, o, N):
                h = i % 2
                dve.wait_ge(measured, i + 1)
                if i >= 2:
                    dve.wait_ge(kept_done, i - 1)
                    dve.wait_ge(taken_done, i - 1)
                nc.vector.tensor_scalar(above[:, h, 0:N], dist[:, h, 0:N], 0.0, 0.0, ALU.is_gt, ALU.add, accum_out=cnt[:, i:i + 1]).then_inc(counted, 1)
                nc.vector.tensor_scalar(equal[:, h, 0:N], dist[:, h, 0:N], 0.0, None, ALU.is_equal).then_inc(equal_done, 1)

            def take(i, o, N):
                h = i % 2
                dve.wait_ge(counted, i + 1)
                nc.vector.tensor_scalar(need[:, i:i + 1], cnt[:, i:i + 1], -1.0, float(TOPK), ALU.mult, ALU.add).then_inc(need_done, 1)
                dve.wait_ge(equal_done, i + 1)
                nc.vector.tensor_tensor_scan(rank[:, h, 0:N], equal[:, h, 0:N], equal[:, h, 0:N], 0.0, ALU.add, ALU.max).then_inc(ranked, 1)
                dve.wait_ge(ranked, i + 1)
                dve.wait_ge(need_done, i + 1)
                nc.vector.scalar_tensor_tensor(taken[:, h, 0:N], rank[:, h, 0:N], need[:, i:i + 1], equal[:, h, 0:N], ALU.is_le, ALU.mult).then_inc(taken_done, 1)
                dve.wait_ge(taken_done, i + 1)
                if i >= 2:
                    dve.wait_ge(masked, i - 1)
                nc.vector.tensor_tensor(kept[:, h, 0:N], above[:, h, 0:N], taken[:, h, 0:N], ALU.add).then_inc(kept_done, 1)

            measure(*search.cols[0])
            for i, o, N in search.cols:
                compare(i, o, N)
                if i + 1 < NS:
                    measure(*search.cols[i + 1])
                take(i, o, N)


def stage_output(nc, sems, name, M, x_dram, dst, weights, o_dram, gate_dram, gp_row, sums, ident, subln=None):
    heads, GT, NG, NU = NMAPS // M, 2 * P, T // (2 * P), KD // 2
    with Stage(nc, sems, name) as st:
        w = st.sb("w", [P, 4, D], F32)
        w_hi, w_lo = (st.sb(n, [P, KD, D], F32R) for n in ("w_hi", "w_lo"))
        gp = st.sb("gp", [P, D], F32)
        inv = st.sb("inv", [P, 2, heads], F32)
        inv_wide = st.sb("inv_wide", [P, 2, D], F32)
        o, gate, scaled = (st.sb(n, [P, NU, 2, GT], F32) for n in ("o", "gate", "scaled"))
        gated = st.sb("gated", [P, 2, 2, GT], F32)
        og_hi, og_lo = (st.sb(n, [P, 2, KD, GT], F32R) for n in ("og_hi", "og_lo"))
        x = st.sb("x", [P, 2, 2, D], F32)
        z, out = (st.sb(n, [P, 2, D], F32) for n in ("z", "out"))
        ysq = st.sb("ysq", [P, D], BF16)
        eps = st.sb("eps", [P, 1], F32)
        ss, sd, rs = (st.sb(n, [P, 2], F32) for n in ("ss", "sd", "rs"))
        if M == 2:
            ones, gcol = st.sb("ones", [P, 1], F32), st.sb("gcol", [P, 1], F32)
            hsq = st.sb("hsq", [P, NU, 2, GT], F32)
            lsq, hms, hsd = (st.sb(n, [P, 2, heads], F32) for n in ("lsq", "hms", "hsd"))
        inv_ps, head_ps = st.ps("inv", [P, 2, 2, GT]), st.ps("head", [P, 2, heads])
        y_ps = st.ps("y", [P, 2, 2, 512])
        names = ("consts_in", "consts_set", "w_hi_done", "w_lo_done", "inverted", "widened", "turned", "scaled_done", "h_squared", "h_summed", "l_squared",
                 "h_meaned", "h_rooted", "gated_done", "hi_done", "lo_done", "y_done", "y_squared", "y_rooted", "y_inverted", "z_done", "added")
        (consts_in, consts_set, w_hi_done, w_lo_done, inverted, widened, turned, scaled_done, h_squared, h_summed, l_squared,
         h_meaned, h_rooted, gated_done, hi_done, lo_done, y_done, y_squared, y_rooted, y_inverted, z_done, added) = (st.sem(n) for n in names)
        w_in, o_in, x_in, stored = ([st.sem(f"{n}{u}") for u in range(c)] for n, c in (("w_in", 4), ("o_in", NU), ("x_in", 2), ("stored", 2)))
        idle_sp = st.sem("idle_sp")
        block = st.block()

        def groups(engine, step):
            with engine.Fori(0, NG // 2 - 1) as i:
                step(i * 2, 0, False)
                step(i * 2 + 1, 1, False)
            step(NG - 2, 0, False)
            step(NG - 1, 1, True)

        def after(engine, sem, count):
            if not (isinstance(count, int) and count <= 0):
                engine.wait_ge(sem, count + 1)

        @block.sync
        def _(sp):
            def load(g, par, first):
                for u in range(NU):
                    if not first:
                        after(sp, gated_done, (g - 1) * NU + u + 1)
                        sp.sem_inc(idle_sp, 1)
                    for dram, buf in ((o_dram, o), (gate_dram, gate)):
                        sp.dma_start(buf[:, u], dram[u * GT:(u + 1) * GT, ds(g * GT, GT)].rearrange("(k p) t -> p k t", p=P)).then_inc(o_in[u], 16)
                if not first:
                    after(sp, added, (g - 1) * 2)
                    sp.sem_inc(idle_sp, 1)
                sp.dma_start(x[:, par], x_dram[ds(g * GT, GT), :].rearrange("(j p) n -> p j n", p=P)).then_inc(x_in[par], 16)

            def step(g, par, last):
                if not isinstance(g, int):
                    load(g + 2, par, False)
                for j in range(2):
                    after(sp, added, g * 2 + j + 1)
                    sp.sem_inc(idle_sp, 1)
                    sp.dma_start(dst[ds(g * GT + j * P, P), :], out[:, j]).then_inc(stored[j], 16)

            for k in range(4):
                sp.dma_start(w[:, k], weights[k * P:(k + 1) * P, :]).then_inc(w_in[k], 16)
            load(0, 0, True)
            sp.dma_start(gp[:], gp_row).then_inc(consts_in, 16)
            if M == 2:
                sp.dma_start(gcol[:], subln.rearrange("o p -> p o"), allow_slow_non_contiguous=True).then_inc(consts_in, 16)
            for k in range(4, KD):
                after(sp, w_lo_done, k - 3)
                sp.dma_start(w[:, k % 4], weights[k * P:(k + 1) * P, :]).then_inc(w_in[k % 4], 16)
            load(1, 1, False)
            groups(sp, step)
            for j in range(2):
                after(sp, stored[j], NG * 16)

        @block.gpsimd
        def _(pool):
            st.start_at_one(pool)
            nc.gpsimd.memset(eps[:], EPS).then_inc(consts_set, 1)
            if M == 2:
                nc.gpsimd.memset(ones[:], 1.0 / P).then_inc(consts_set, 1)

            def step(g, par, last):
                for j in range(2):
                    if j == 0:
                        pool.wait_ge(x_in[par], 1 + (g + 2 - par) * 8)
                    after(pool, z_done, g * 2 + j + 1)
                    after(pool, stored[j], g * 16)
                    nc.gpsimd.tensor_tensor(out[:, j], z[:, j], x[:, par, j], ALU.add).then_inc(added, 1)

            groups(pool, step)

        @block.tensor
        def _(pe):
            def turn(g, u):
                if u == 0:
                    after(pe, widened, g + 1)
                after(pe, scaled_done, g * NU + u - 1)
                for kk in range(2):
                    for j in range(2):
                        m = nc.tensor.transpose(inv_ps[:, u % 2, kk, j * P:(j + 1) * P], inv_wide[:, j, (2 * u + kk) * P:(2 * u + kk + 1) * P], ident[:])
                m.then_inc(turned, 1)

            def head_sums(g):
                if M == 2:
                    after(pe, h_squared, g * NU + NU)
                    after(pe, h_meaned, g)
                    for k in range(heads):
                        for j in range(2):
                            m = nc.tensor.matmul(head_ps[:, j, k:k + 1], hsq[:, k // 2, k % 2, j * P:(j + 1) * P], ones[:], start=True, stop=True)
                    m.then_inc(h_summed, 1)

            def project(g, par, j, n):
                if n == 0:
                    after(pe, z_done, (g - 1) * 2 + j + 1)
                terms = [(a, b, k) for k in range(KD) for a, b in ((og_hi, w_hi), (og_lo, w_hi), (og_hi, w_lo))]
                for i, (a, b, k) in enumerate(terms):
                    if j == 0 and n == 0 and i % 3 == 0:
                        if k % 2 == 0:
                            after(pe, lo_done, g * NU + k // 2 + 1)
                        after(pe, w_lo_done, k + 1)
                    m = nc.tensor.matmul(y_ps[:, j, n], a[:, par, k, j * P:(j + 1) * P], b[:, k, n * 512:(n + 1) * 512],
                                         start=(i == 0), stop=(i == len(terms) - 1))
                if n == 1:
                    m.then_inc(y_done, 1)

            def step(g, par, last):
                project(g, par, 0, 0)
                if not last:
                    head_sums(g + 1)
                project(g, par, 0, 1)
                if not last:
                    turn(g + 1, 0)
                    turn(g + 1, 1)
                project(g, par, 1, 0)
                if not last:
                    turn(g + 1, 2)
                    turn(g + 1, 3)
                project(g, par, 1, 1)

            after(pe, consts_set, 2 * M - 1)
            head_sums(0)
            for u in range(NU):
                turn(0, u)
            groups(pe, step)

        @block.scalar
        def _(act):
            def square_heads(g):
                if M == 2:
                    for u in range(NU):
                        after(act, o_in[u], (g + 1) * 32)
                        after(act, h_summed, g)
                        nc.scalar.activation(hsq[:, u], o[:, u], ACT.Square).then_inc(h_squared, 1)
                    after(act, h_meaned, g + 1)
                    after(act, inverted, g)
                    nc.scalar.activation(hsd[:], hms[:], ACT.Sqrt).then_inc(h_rooted, 1)

            def split_hi(g, par, u):
                after(act, gated_done, g * NU + u + 1)
                if u == 0:
                    after(act, y_done, (g - 1) * 2)
                nc.scalar.activation(og_hi[:, par, 2 * u:2 * u + 2], gated[:, u % 2], ACT.Copy).then_inc(hi_done, 1)

            def norm(g, j):
                after(act, y_done, g * 2 + j + 1)
                after(act, y_squared, g * 2 + j)
                after(act, y_inverted, (g - 1) * 2 + j + 1)
                nc.scalar.activation(ysq[:], flat(y_ps[:, j]), ACT.Square, accum_out=ss[:, j:j + 1]).then_inc(y_squared, 1)
                after(act, y_squared, g * 2 + j + 1)
                nc.scalar.activation(sd[:, j:j + 1], ss[:, j:j + 1], ACT.Sqrt, bias=eps[:], scale=1.0 / D).then_inc(y_rooted, 1)

            def prepare(g, par, norm_between=None):
                square_heads(g)
                for u in range(NU):
                    split_hi(g, par, u)
                    if u == 1 and norm_between is not None:
                        norm(norm_between, 0)

            def step(g, par, last):
                if last:
                    norm(g, 0)
                else:
                    prepare(g + 1, 1 - par, g)
                norm(g, 1)

            for k in range(KD):
                after(act, w_in[k % 4], 16 * (k // 4 + 1))
                nc.scalar.activation(w_hi[:, k], w[:, k % 4], ACT.Copy).then_inc(w_hi_done, 1)
            after(act, consts_set, M)
            prepare(0, 0)
            groups(act, step)

        @block.vector
        def _(dve):
            def widen(g):
                l1 = sums.rearrange("p b (h m) -> p b h m", m=M)[:, ds(g * 2, 2), :, 0]
                after(dve, widened, g)
                if M == 2:
                    after(dve, h_meaned, g)
                    nc.vector.scalar_tensor_tensor(lsq[:], l1, EPS, l1, ALU.mult, ALU.mult).then_inc(l_squared, 1)
                    after(dve, l_squared, g + 1)
                    after(dve, h_summed, g + 1)
                    after(dve, h_rooted, g)
                    nc.vector.tensor_tensor(hms[:], head_ps[:], lsq[:], ALU.add).then_inc(h_meaned, 1)
                    after(dve, h_rooted, g + 1)
                    l1 = hsd[:]
                nc.vector.reciprocal(inv[:], l1).then_inc(inverted, 1)
                after(dve, inverted, g + 1)
                after(dve, turned, g * NU)
                nc.vector.tensor_copy(inv_wide.rearrange("p j (h e) -> p j h e", h=heads),
                                      inv[:].unsqueeze(3).to_broadcast([P, 2, heads, D // heads])).then_inc(widened, 1)

            def scale(g, u):
                after(dve, turned, g * NU + u + 1)
                after(dve, o_in[u], (g + 1) * 32)
                after(dve, gated_done, (g - 1) * NU + u + 1)
                if M == 2:
                    nc.vector.scalar_tensor_tensor(scaled[:, u], inv_ps[:, u % 2], gcol[:], o[:, u], ALU.mult, ALU.mult).then_inc(scaled_done, 1)
                else:
                    nc.vector.tensor_tensor(scaled[:, u], inv_ps[:, u % 2], o[:, u], ALU.mult).then_inc(scaled_done, 1)

            def gate_unit(g, u):
                after(dve, scaled_done, g * NU + u + 1)
                after(dve, lo_done, g * NU + u - 1)
                nc.vector.tensor_tensor(gated[:, u % 2], scaled[:, u], gate[:, u], ALU.mult).then_inc(gated_done, 1)

            def split_lo(g, par, u):
                after(dve, hi_done, g * NU + u + 1)
                nc.vector.tensor_tensor(og_lo[:, par, 2 * u:2 * u + 2], gated[:, u % 2], og_hi[:, par, 2 * u:2 * u + 2],
                                        ALU.subtract).then_inc(lo_done, 1)

            def norm(g, j):
                after(dve, y_rooted, g * 2 + j + 1)
                after(dve, z_done, (g - 1) * 2 + j + 1)
                nc.vector.reciprocal(rs[:, j:j + 1], sd[:, j:j + 1]).then_inc(y_inverted, 1)
                after(dve, y_inverted, g * 2 + j + 1)
                after(dve, added, (g - 1) * 2 + j + 1)
                nc.vector.scalar_tensor_tensor(z[:, j], flat(y_ps[:, j]), rs[:, j:j + 1], gp[:], ALU.mult, ALU.mult).then_inc(z_done, 1)

            def prepare(g, par, norm_between=None):
                for s in range(NU + 1):
                    if s < NU:
                        scale(g, s)
                        gate_unit(g, s)
                    if s >= 1:
                        split_lo(g, par, s - 1)
                    if s == 2 and norm_between is not None:
                        norm(norm_between, 0)

            def step(g, par, last):
                if last:
                    norm(g, 0)
                else:
                    widen(g + 1)
                    prepare(g + 1, 1 - par, g)
                norm(g, 1)

            after(dve, consts_in, 16 * M)
            if M == 2:
                nc.vector.tensor_scalar(gcol[:], gcol[:], 1.0 - LAMBDA_INIT, None, ALU.mult).then_inc(consts_set, 1)
                after(dve, consts_set, 3)
            for k in range(KD):
                after(dve, w_hi_done, k + 1)
                nc.vector.tensor_tensor(w_lo[:, k], w[:, k % 4], w_hi[:, k], ALU.subtract).then_inc(w_lo_done, 1)
            widen(0)
            prepare(0, 0)
            groups(dve, step)


def stage_identity(nc, sems, ident):
    with Stage(nc, sems, "identity") as st:
        made = st.sem("made")
        block = st.block()

        @block.gpsimd
        def _(pool):
            nc.gpsimd.memset(ident[:], 0.0).then_inc(made, 1)
            pool.wait_ge(made, 1)
            nc.gpsimd.affine_select(out=ident[:], in_=ident[:], compare_op=ALU.not_equal, fill=1.0, base=0,
                                    pattern=[[-1, P]], channel_multiplier=1).then_inc(made, 1)
            pool.wait_ge(made, 2)


def program(nc, ins, out):
    scratch = lambda name, shape: nc.dram_tensor(f"scratch_{name}", shape, F32).ap()
    gp_dram, bias_dram = scratch("gp", (2, P, D)), scratch("bias", (NMAPS, P, 384))
    qT, kT, v = scratch("qT", (2, D, T)), scratch("kT", (2, D, T)), scratch("v", (2, T, D))
    gateT, oT, x1 = scratch("gateT", (D, T)), scratch("oT", (D, T)), scratch("x1", (T, D))
    cqT, ckvT, kidxT, qidx = scratch("cqT", (2, QR, T)), scratch("ckvT", (2, KVR, T)), scratch("kidxT", (2, ID, T)), scratch("qidx", (2, IH * ID, T))
    sems = Semaphores(nc)
    with ExitStack() as keep:
        sb = lambda ctx, name, shape, dt: ctx.enter_context(nc.sbuf_tensor(name, shape, dt))
        ident, ada, neglam = sb(keep, "ident", [P, P], F32), sb(keep, "ada", [P, 2, 2, KD], F32), sb(keep, "neglam", [P, 1], F32)
        sums, widx = sb(keep, "sums", [P, NB, NMAPS], F32), sb(keep, "widx", [P, NB, IH], F32)
        stage_identity(nc, sems, ident)
        modulation = Modulation(lambda *a: sb(keep, *a))
        stage_modulation(nc, sems, ins, modulation, ada, neglam, bias_dram)

        with ExitStack() as c:
            hT = [sb(c, f"a_{n}", [P, KD, T], F32R) for n in ("hT_hi", "hT_lo")]
            stage_input(nc, sems, "a_in", ins["x"][0], ada, 0, ident, hT)
            win = ins["a_w_in"][0].rearrange("(k p) n -> p k n", p=P)
            stage_project(nc, sems, "a_gate", [Job("silu", hT, KD, lambda n: win[:, :, ds(n * P + SMALL, P)], KD, 1.0, gateT)])
            stage_narrow(nc, sems, ins, hT, ident, widx, cqT, ckvT, kidxT)
        with ExitStack() as m:
            mask = sb(m, "mask", [P, KEYS], BF16)
            with ExitStack() as c:
                k_up, k_down = (sb(c, n, [P, KEYS], U16) for n in ("k_up", "k_down"))
                search = Selection(lambda *a: sb(c, *a), k_up, k_down, mask)
                wq, wqi = (ins[n][0].rearrange("(k p) n -> p k n", p=P) for n in ("a_w_uq", "a_w_qidx"))
                wk, wv = (ins[n][0].rearrange("h r d -> r h d") for n in ("a_w_uk", "a_w_uv"))

                def load_latents(c, suffix, latents):
                    loaded = sems.new(f"latents_loaded_{suffix}")
                    with nc.Block() as block:
                        @block.sync
                        def _(sp):
                            for dram, buf in latents:
                                for part in range(2):
                                    sp.dma_start(buf[part].bitcast(F32)[:], dram[part].rearrange("(k p) t -> p k t", p=P)).then_inc(loaded, 16)
                            sp.wait_ge(loaded, 32 * len(latents))

                with ExitStack() as l:
                    cq = [sb(l, f"cq1_{n}", [P, 2, T], F32R) for n in ("hi", "lo")]
                    load_latents(l, "q", [(cqT, cq)])
                    stage_project(nc, sems, "a_qidx", [Job("split", cq, 2, lambda n: wqi[:, :, ds(n * P, P)], 4, 1.0, qidx[0], qidx[1])])
                sems.retire()
                stage_score(nc, sems, widx, qidx, kidxT, k_up, k_down)
                with ExitStack() as l:
                    cq = [sb(l, f"cq_{n}", [P, 2, T], F32R) for n in ("hi", "lo")]
                    ckv = [sb(l, f"ckv_{n}", [P, 1, T], F32R) for n in ("hi", "lo")]
                    load_latents(l, "all", [(cqT, cq), (ckvT, ckv)])
                    chain, counted, search.halved = (sems.new(f"search_{n}") for n in ("chain", "counted", "halved"))
                    stage_project(nc, sems, "a_qkv", [Job("split", cq, 2, lambda n: wq[:, :, ds(n * P, P)], 8, HD ** -0.5, qT[0], qT[1]),
                                                      Job("split", ckv, 1, lambda n: wk[:, ds(n * 2, 2), :], 8, 1.0, kT[0], kT[1]),
                                                      Job("values", ckv, 1, lambda n: wv[:, ds(n * 2, 2), :], 8, 1.0, v[0], v[1])],
                                  beside=lambda st, dve: search.upper(nc, dve, chain, counted))
                stage_search_lower(nc, sems, ins, search, modulation, ada, gp_dram)
                stage_mask(nc, sems, search)
            sems.retire()
            stage_attention(nc, sems, "a_att", 16, 1, ident, bias_dram, qT, kT, v, oT, sums, mask=mask)
        stage_output(nc, sems, "a_out", 1, ins["x"][0], x1, ins["a_w_out"][0], oT, gateT, gp_dram[0], sums, ident)

        sems.retire()

        with ExitStack() as c:
            hT = [sb(c, f"b_{n}", [P, KD, T], F32R) for n in ("hT_hi", "hT_lo")]
            stage_input(nc, sems, "b_in", x1, ada, 1, ident, hT)
            win = ins["b_w_in"][0].rearrange("(k p) n -> p k n", p=P)
            stage_project(nc, sems, "b_qkgv", [Job("split", hT, KD, lambda n: win[:, :, ds(n * P, P)], KD, HD ** -0.5, qT[0], qT[1]),
                                               Job("split", hT, KD, lambda n: win[:, :, ds(n * P + D, P)], KD, 1.0, kT[0], kT[1]),
                                               Job("silu", hT, KD, lambda n: win[:, :, ds(n * P + 3 * D, P)], KD, 1.0, gateT),
                                               Job("values", hT, KD, lambda n: win[:, :, ds(n * P + 2 * D, P)], KD, 1.0, v[0], v[1])])
        stage_attention(nc, sems, "b_att", 8, 2, ident, bias_dram, qT, kT, v, oT, sums, neglam=neglam)
        stage_output(nc, sems, "b_out", 2, x1, out, ins["b_w_out"][0], oT, gateT, gp_dram[1], sums, ident, subln=ins["b_subln"])


_INS = ["x", "c", "rel_bias", "mod_w", "mod_b", "pre_g", "post_g", "a_w_in", "a_q_norm", "a_kv_norm", "a_kidx_norm", "a_w_uq",
        "a_w_qidx", "a_w_uk", "a_w_uv", "a_w_out", "b_w_in", "b_lam_q1", "b_lam_k1", "b_lam_q2", "b_lam_k2", "b_subln", "b_w_out"]


def kernel(**inputs):
    import concourse.bacc as bacc
    from concourse.bass_utils import run_bass_kernel_spmd

    nc = bacc.Bacc("TRN2", target_bir_lowering=False, num_devices=1)
    arrays = {name: np.ascontiguousarray(inputs[name]) for name in _INS}
    arrays["onehot"] = bucket_onehot()
    ins = {name: nc.dram_tensor(f"in_{name}", a.shape, mybir.dt.from_np(a.dtype), kind="ExternalInput").ap() for name, a in arrays.items()}
    out = nc.dram_tensor("out_dram", (1, T, D), F32, kind="ExternalOutput").ap()
    program(nc, ins, out[0])
    r = run_bass_kernel_spmd(nc, [{f"in_{name}": a for name, a in arrays.items()}], core_ids=[0])
    return r.results[0]["out_dram"]
```
